# Optimizing a Trainium2 kernel written in Bass

```python
import math
import jax, jax.numpy as jnp
from jax import lax
import numpy as np

D_MODEL = 2048
BATCH = 1
SEQ = 256
DEPTH = 1

HEAD_DIM = 128
N_HEADS = D_MODEL // HEAD_DIM
N_FOX_HEADS = N_HEADS // 2
N_NSA_HEADS = N_HEADS - N_FOX_HEADS
NSA_GROUP = 4
NSA_KV_HEADS = N_NSA_HEADS // NSA_GROUP
D_MIX = (N_FOX_HEADS + N_NSA_HEADS) * HEAD_DIM
CMP_BLOCK = 32
CMP_STRIDE = 16
SLC_BLOCK = 64
SLC_TOPK = 16
WINDOW = 512
Q_BLOCK = 128
D_FF = -(-8 * D_MODEL // (3 * 256)) * 256
RMS_EPS = 1e-6
NEG_INF = -1e30
FORCE_SCORE = 1e9

FOX_W = N_FOX_HEADS * HEAD_DIM
NSA_W = N_NSA_HEADS * HEAD_DIM
KV_W = NSA_KV_HEADS * HEAD_DIM
IN_SPLITS = (FOX_W, FOX_W, FOX_W, N_FOX_HEADS, NSA_W, KV_W, KV_W, KV_W, KV_W, KV_W, KV_W, 3 * N_NSA_HEADS)
IN_WIDTH = sum(IN_SPLITS)


def _rms_norm(x, g):
    xf = x.astype(jnp.float32)
    y = xf * lax.rsqrt(jnp.mean(xf * xf, axis=-1, keepdims=True) + RMS_EPS)
    return (y * g.astype(jnp.float32)).astype(x.dtype)

def _masked_softmax(s, mask):
    s = jnp.where(mask, s, NEG_INF)
    m = jnp.max(s, axis=-1, keepdims=True)
    p = jnp.where(mask, jnp.exp(s - m), 0.0)
    return p / jnp.maximum(jnp.sum(p, axis=-1, keepdims=True), 1e-30)

def _alibi_slopes(n):
    return jnp.exp2(-8.0 * jnp.arange(1, n + 1, dtype=jnp.float32) / n)

def _overlap_matrix(n_cmp, n_slc):
    ci = np.arange(n_cmp)[:, None]
    sj = np.arange(n_slc)[None, :]
    ov = (ci * CMP_STRIDE < (sj + 1) * SLC_BLOCK) & (ci * CMP_STRIDE + CMP_BLOCK > sj * SLC_BLOCK)
    return ov.astype(np.float32)

def _compress(tok, pos_emb, w):
    B, T, G, Dh = tok.shape
    chunks = tok.reshape(B, T // CMP_STRIDE, CMP_STRIDE, G, Dh)
    blocks = jnp.concatenate([chunks[:, :-1], chunks[:, 1:]], axis=2)
    return jnp.einsum("bnlgd,lde->bnge", blocks + pos_emb[None, None, :, None, :], w)

def _hybrid_mixer(h, w_in, fox_forget_bias, fox_q_norm, fox_k_norm, nsa_q_norm, cmp_k_norm,
                  slc_k_norm, win_k_norm, cmp_pos_k, cmp_pos_v, cmp_w_k, cmp_w_v, w_out):
    B, T, _ = h.shape
    dt = h.dtype
    f32 = jnp.float32
    Hf, Hn, G, R, Dh = N_FOX_HEADS, N_NSA_HEADS, NSA_KV_HEADS, NSA_GROUP, HEAD_DIM
    scale = HEAD_DIM ** -0.5
    n_cmp = T // CMP_STRIDE - 1
    n_slc = T // SLC_BLOCK
    k_sel = min(SLC_TOPK, n_slc)
    n_qb = T // Q_BLOCK

    proj = h @ w_in
    cuts = [int(c) for c in np.cumsum(IN_SPLITS)[:-1]]
    qf, kf, vf, ff, qn, kc, vc, ks, vs, kw, vw, gt = jnp.split(proj, cuts, axis=-1)

    qf = _rms_norm(qf.reshape(B, T, Hf, Dh), fox_q_norm)
    kf = _rms_norm(kf.reshape(B, T, Hf, Dh), fox_k_norm)
    vf = vf.reshape(B, T, Hf, Dh)
    log_f = jax.nn.log_sigmoid(ff.astype(f32) + fox_forget_bias.astype(f32))
    cum_f = jnp.transpose(jnp.cumsum(log_f, axis=1), (0, 2, 1))

    qn = _rms_norm(qn.reshape(B, T, G, R, Dh), nsa_q_norm)
    k_cmp = _rms_norm(_compress(kc.reshape(B, T, G, Dh), cmp_pos_k, cmp_w_k), cmp_k_norm)
    v_cmp = _compress(vc.reshape(B, T, G, Dh), cmp_pos_v, cmp_w_v)
    cmp_end = jnp.arange(n_cmp) * CMP_STRIDE + (CMP_BLOCK - 1)
    k_slc = jnp.transpose(_rms_norm(ks.reshape(B, n_slc, SLC_BLOCK, G, Dh), slc_k_norm), (0, 3, 1, 2, 4))
    v_slc = jnp.transpose(vs.reshape(B, n_slc, SLC_BLOCK, G, Dh), (0, 3, 1, 2, 4))
    pad = ((0, 0), (WINDOW, 0), (0, 0), (0, 0))
    k_win = jnp.pad(_rms_norm(kw.reshape(B, T, G, Dh), win_k_norm), pad)
    v_win = jnp.pad(vw.reshape(B, T, G, Dh), pad)
    gates = jax.nn.sigmoid(gt.astype(f32)).astype(dt).reshape(B, T, G, R, 3)

    slopes = _alibi_slopes(Hn).reshape(G, R)
    overlap = jnp.asarray(_overlap_matrix(n_cmp, n_slc))
    key_pos = jnp.arange(T)
    blk_ids = jnp.arange(n_slc)
    bi = jnp.arange(B)[:, None, None, None]
    gi = jnp.arange(G)[None, :, None, None]
    win_off = jnp.arange(Q_BLOCK + WINDOW) - WINDOW
    slc_off = jnp.arange(SLC_BLOCK)

    def query_block(i):
        q0 = i * Q_BLOCK
        tpos = q0 + jnp.arange(Q_BLOCK)

        qf_b = lax.dynamic_slice_in_dim(qf, q0, Q_BLOCK, axis=1)
        cq = lax.dynamic_slice_in_dim(cum_f, q0, Q_BLOCK, axis=2)
        s = jnp.einsum("bqhd,bkhd->bhqk", qf_b, kf).astype(f32) * scale
        s = s + cq[..., None] - cum_f[:, :, None, :]
        p = _masked_softmax(s, key_pos[None, :] <= tpos[:, None])
        o_fox = jnp.einsum("bhqk,bkhd->bqhd", p.astype(dt), vf)

        qn_b = lax.dynamic_slice_in_dim(qn, q0, Q_BLOCK, axis=1)

        dist_c = (tpos[:, None] - cmp_end[None, :]).astype(f32)
        s_c = jnp.einsum("bqgrd,bngd->bgrqn", qn_b, k_cmp).astype(f32) * scale
        s_c = s_c - slopes[None, :, :, None, None] * dist_c
        p_c = _masked_softmax(s_c, dist_c >= 0)
        o_c = jnp.einsum("bgrqn,bngd->bqgrd", p_c.astype(dt), v_cmp)

        imp = jnp.einsum("bgrqn,nj->bgqj", p_c, overlap)
        cur = tpos // SLC_BLOCK
        forced = (blk_ids[None, :] == 0) | (blk_ids[None, :] == cur[:, None]) | (blk_ids[None, :] == cur[:, None] - 1)
        valid = blk_ids[None, :] * SLC_BLOCK <= tpos[:, None]
        imp = jnp.where(forced, FORCE_SCORE, jnp.where(valid, imp, -FORCE_SCORE))
        _, idx = lax.top_k(imp, k_sel)
        k_g = k_slc[bi, gi, idx]
        v_g = v_slc[bi, gi, idx]
        spos = idx[..., None] * SLC_BLOCK + slc_off
        dist_s = (tpos[None, None, :, None, None] - spos).astype(f32)[:, :, None]
        s_s = jnp.einsum("bqgrd,bgqkld->bgrqkl", qn_b, k_g).astype(f32) * scale
        s_s = s_s - slopes[None, :, :, None, None, None] * dist_s
        flat = (B, G, R, Q_BLOCK, k_sel * SLC_BLOCK)
        mask_s = jnp.broadcast_to(dist_s >= 0, s_s.shape).reshape(flat)
        p_s = _masked_softmax(s_s.reshape(flat), mask_s).reshape(s_s.shape)
        o_s = jnp.einsum("bgrqkl,bgqkld->bqgrd", p_s.astype(dt), v_g)

        k_wb = lax.dynamic_slice_in_dim(k_win, q0, Q_BLOCK + WINDOW, axis=1)
        v_wb = lax.dynamic_slice_in_dim(v_win, q0, Q_BLOCK + WINDOW, axis=1)
        wpos = q0 + win_off
        dist_w = tpos[:, None] - wpos[None, :]
        mask_w = (dist_w >= 0) & (dist_w < WINDOW) & (wpos[None, :] >= 0)
        s_w = jnp.einsum("bqgrd,bkgd->bgrqk", qn_b, k_wb).astype(f32) * scale
        s_w = s_w - slopes[None, :, :, None, None] * dist_w.astype(f32)
        p_w = _masked_softmax(s_w, mask_w)
        o_w = jnp.einsum("bgrqk,bkgd->bqgrd", p_w.astype(dt), v_wb)

        g_b = lax.dynamic_slice_in_dim(gates, q0, Q_BLOCK, axis=1)
        o_nsa = g_b[..., 0:1] * o_c + g_b[..., 1:2] * o_s + g_b[..., 2:3] * o_w
        return o_fox, o_nsa.reshape(B, Q_BLOCK, Hn, Dh)

    o_fox, o_nsa = lax.map(query_block, jnp.arange(n_qb))
    o_fox = jnp.moveaxis(o_fox, 0, 1).reshape(B, T, FOX_W)
    o_nsa = jnp.moveaxis(o_nsa, 0, 1).reshape(B, T, NSA_W)
    return jnp.concatenate([o_fox, o_nsa], axis=-1) @ w_out

def _swiglu(h, w_gate, w_up, w_down):
    return (jax.nn.silu(h @ w_gate) * (h @ w_up)) @ w_down

def first_inputs(seed: int = 0) -> dict:
    key = jax.random.key(seed)
    ks = jax.random.split(key, 20)
    f32 = jnp.float32
    nrm = lambda k, shape, s: jax.random.normal(k, shape, f32) * s
    gain = lambda k, shape: 1.0 + 0.02 * jax.random.normal(k, shape, f32)
    L = DEPTH
    return {
        "x": nrm(ks[0], (BATCH, SEQ, D_MODEL), 1.0),
        "attn_norm": gain(ks[1], (L, D_MODEL)),
        "w_in": nrm(ks[2], (L, D_MODEL, IN_WIDTH), D_MODEL ** -0.5),
        "fox_forget_bias": 3.0 + 0.5 * jax.random.normal(ks[3], (L, N_FOX_HEADS), f32),
        "fox_q_norm": gain(ks[4], (L, HEAD_DIM)),
        "fox_k_norm": gain(ks[5], (L, HEAD_DIM)),
        "nsa_q_norm": gain(ks[6], (L, HEAD_DIM)),
        "cmp_k_norm": gain(ks[7], (L, HEAD_DIM)),
        "slc_k_norm": gain(ks[8], (L, HEAD_DIM)),
        "win_k_norm": gain(ks[9], (L, HEAD_DIM)),
        "cmp_pos_k": nrm(ks[10], (L, CMP_BLOCK, HEAD_DIM), 0.02),
        "cmp_pos_v": nrm(ks[11], (L, CMP_BLOCK, HEAD_DIM), 0.02),
        "cmp_w_k": nrm(ks[12], (L, CMP_BLOCK, HEAD_DIM, HEAD_DIM), (CMP_BLOCK * HEAD_DIM) ** -0.5),
        "cmp_w_v": nrm(ks[13], (L, CMP_BLOCK, HEAD_DIM, HEAD_DIM), (CMP_BLOCK * HEAD_DIM) ** -0.5),
        "w_out": nrm(ks[14], (L, D_MIX, D_MODEL), D_MIX ** -0.5),
        "ffn_norm": gain(ks[15], (L, D_MODEL)),
        "w_gate": nrm(ks[16], (L, D_MODEL, D_FF), D_MODEL ** -0.5),
        "w_up": nrm(ks[17], (L, D_MODEL, D_FF), D_MODEL ** -0.5),
        "w_down": nrm(ks[18], (L, D_FF, D_MODEL), D_FF ** -0.5),
    }

def first_block(x, attn_norm, w_in, fox_forget_bias, fox_q_norm, fox_k_norm, nsa_q_norm, cmp_k_norm,
              slc_k_norm, win_k_norm, cmp_pos_k, cmp_pos_v, cmp_w_k, cmp_w_v, w_out, ffn_norm,
              w_gate, w_up, w_down):
    for l in range(DEPTH):
        h = _rms_norm(x, attn_norm[l])
        x = x + _hybrid_mixer(h, w_in[l], fox_forget_bias[l], fox_q_norm[l], fox_k_norm[l], nsa_q_norm[l],
                              cmp_k_norm[l], slc_k_norm[l], win_k_norm[l], cmp_pos_k[l], cmp_pos_v[l],
                              cmp_w_k[l], cmp_w_v[l], w_out[l])
        h = _rms_norm(x, ffn_norm[l])
        x = x + _swiglu(h, w_gate[l], w_up[l], w_down[l])
    return x


N_ATTN_HEADS = 8
ATTN_WIDTH = N_ATTN_HEADS * HEAD_DIM
N_CONV_GROUPS = 8
CONV_CH = N_CONV_GROUPS * HEAD_DIM
MIX_WIDTH = ATTN_WIDTH + CONV_CH
IN_COLS = 3 * ATTN_WIDTH + 2 * CONV_CH
CONV_K = 31
MOBA_BLOCK = 256
MOBA_TOPK = 3
Q_CHUNK = 128
D_FF_2 = -(-8 * D_MODEL // (3 * 256)) * 256
N_MOD = 6
LN_EPS = 1e-5
NEG_INF_2 = -1e30


def rms_norm(x, g):
    x32 = x.astype(jnp.float32)
    y = x32 * lax.rsqrt(jnp.mean(x32 * x32, axis=-1, keepdims=True) + RMS_EPS)
    return (y * g.astype(jnp.float32)).astype(x.dtype)

def layer_norm(x, g, b):
    x32 = x.astype(jnp.float32)
    mu = jnp.mean(x32, axis=-1, keepdims=True)
    var = jnp.mean(jnp.square(x32 - mu), axis=-1, keepdims=True)
    y = (x32 - mu) * lax.rsqrt(var + LN_EPS) * g.astype(jnp.float32) + b.astype(jnp.float32)
    return y.astype(x.dtype)

def causal_depthwise_conv(u, w, b):
    k = w.shape[0]
    y = lax.conv_general_dilated(
        u, w[:, None, :].astype(u.dtype), window_strides=(1,),
        padding=((k - 1, 0),), dimension_numbers=('NWC', 'WIO', 'NWC'),
        feature_group_count=u.shape[-1])
    return y + b.astype(u.dtype)

def moba_attention(q, k, v):
    B, H, S, Dh = q.shape
    nb = -(-S // MOBA_BLOCK)
    n_sel = min(MOBA_TOPK, nb)
    pad = nb * MOBA_BLOCK - S
    kb = jnp.pad(k, ((0, 0), (0, 0), (0, pad), (0, 0))).reshape(B, H, nb, MOBA_BLOCK, Dh)
    vb = jnp.pad(v, ((0, 0), (0, 0), (0, pad), (0, 0))).reshape(B, H, nb, MOBA_BLOCK, Dh)
    k_mean = jnp.mean(kb.astype(jnp.float32), axis=3)
    n_chunks = S // Q_CHUNK
    q_chunks = q.reshape(B, H, n_chunks, Q_CHUNK, Dh).transpose(2, 0, 1, 3, 4)
    scale = HEAD_DIM ** -0.5
    b_idx = jnp.arange(B)[:, None, None]
    h_idx = jnp.arange(H)[None, :, None]
    blk_ids = jnp.arange(nb)

    def one_chunk(args):
        qc, ci = args
        q_pos = ci * Q_CHUNK + jnp.arange(Q_CHUNK)
        blk = (ci * Q_CHUNK) // MOBA_BLOCK
        gate = jnp.einsum('bhqd,bhnd->bhqn', qc.astype(jnp.float32), k_mean)
        gate = jnp.where(blk_ids < blk, gate, NEG_INF_2)
        _, sel = lax.top_k(gate, n_sel)
        k_own = lax.dynamic_index_in_dim(kb, blk, axis=2, keepdims=False)
        v_own = lax.dynamic_index_in_dim(vb, blk, axis=2, keepdims=False)
        k_pos = blk * MOBA_BLOCK + jnp.arange(MOBA_BLOCK)
        s_own = jnp.einsum('bhqd,bhkd->bhqk', qc, k_own,
                           preferred_element_type=jnp.float32) * scale
        s_own = jnp.where(k_pos[None, :] <= q_pos[:, None], s_own, NEG_INF_2)
        scores = [s_own]
        for j in range(n_sel):
            k_sel = kb[b_idx, h_idx, sel[..., j]]
            s_j = jnp.einsum('bhqd,bhqkd->bhqk', qc, k_sel,
                             preferred_element_type=jnp.float32) * scale
            scores.append(jnp.where(j < blk, s_j, NEG_INF_2))
        p = jax.nn.softmax(jnp.concatenate(scores, axis=-1), axis=-1).astype(v.dtype)
        p = p.reshape(B, H, Q_CHUNK, n_sel + 1, MOBA_BLOCK)
        out = jnp.einsum('bhqk,bhkd->bhqd', p[..., 0, :], v_own,
                         preferred_element_type=jnp.float32)
        for j in range(n_sel):
            v_sel = vb[b_idx, h_idx, sel[..., j]]
            out = out + jnp.einsum('bhqk,bhqkd->bhqd', p[..., j + 1, :], v_sel,
                                   preferred_element_type=jnp.float32)
        return out.astype(q.dtype)

    out = lax.map(one_chunk, (q_chunks, jnp.arange(n_chunks)))
    return out.transpose(1, 2, 0, 3, 4).reshape(B, H, S, Dh)

def hybrid_mixer(h, w_in, conv_w, conv_b, conv_ln_g, conv_ln_b, w_out):
    B, S, _ = h.shape
    proj = h @ w_in
    q, k, v, a, g = jnp.split(
        proj, [ATTN_WIDTH, 2 * ATTN_WIDTH, 3 * ATTN_WIDTH, 3 * ATTN_WIDTH + CONV_CH], axis=-1)

    def heads(t):
        return t.reshape(B, S, N_ATTN_HEADS, HEAD_DIM).transpose(0, 2, 1, 3)

    attn = moba_attention(heads(q), heads(k), heads(v))
    attn = attn.transpose(0, 2, 1, 3).reshape(B, S, ATTN_WIDTH)
    u = a * jax.nn.sigmoid(g)
    u = causal_depthwise_conv(u, conv_w, conv_b)
    u = jax.nn.silu(layer_norm(u, conv_ln_g, conv_ln_b))
    mix = jnp.concatenate([attn, u], axis=-1)
    return mix @ w_out

def swiglu_ffn(h, w_gate, w_up, w_down):
    return (jax.nn.silu(h @ w_gate) * (h @ w_up)) @ w_down

def second_inputs(seed: int = 0) -> dict:
    key = jax.random.key(seed)
    ks = jax.random.split(key, 18)

    def nrm(k, shape, s):
        return jax.random.normal(k, shape, jnp.float32) * s

    L, D = DEPTH, D_MODEL
    return {
        'x': nrm(ks[0], (BATCH, SEQ, D), 1.0),
        'c': nrm(ks[1], (BATCH, D), 1.0),
        'ada_w': nrm(ks[2], (L, D, N_MOD * D), 0.5 * D ** -0.5),
        'ada_b': nrm(ks[3], (L, N_MOD * D), 0.02),
        'mix_pre_g': 1.0 + nrm(ks[4], (L, D), 0.02),
        'mix_post_g': 1.0 + nrm(ks[5], (L, D), 0.02),
        'w_in': nrm(ks[6], (L, D, IN_COLS), D ** -0.5),
        'conv_w': nrm(ks[7], (L, CONV_K, CONV_CH), CONV_K ** -0.5),
        'conv_b': nrm(ks[8], (L, CONV_CH), 0.02),
        'conv_ln_g': 1.0 + nrm(ks[9], (L, CONV_CH), 0.02),
        'conv_ln_b': nrm(ks[10], (L, CONV_CH), 0.02),
        'w_out': nrm(ks[11], (L, MIX_WIDTH, D), MIX_WIDTH ** -0.5),
        'ffn_pre_g': 1.0 + nrm(ks[12], (L, D), 0.02),
        'ffn_post_g': 1.0 + nrm(ks[13], (L, D), 0.02),
        'w_gate': nrm(ks[14], (L, D, D_FF_2), D ** -0.5),
        'w_up': nrm(ks[15], (L, D, D_FF_2), D ** -0.5),
        'w_down': nrm(ks[16], (L, D_FF_2, D), D_FF_2 ** -0.5),
    }

def second_block(x, c, ada_w, ada_b, mix_pre_g, mix_post_g, w_in, conv_w, conv_b,
              conv_ln_g, conv_ln_b, w_out, ffn_pre_g, ffn_post_g, w_gate, w_up, w_down):
    c_act = jax.nn.silu(c)
    for l in range(DEPTH):
        mod = c_act @ ada_w[l] + ada_b[l]
        sh1, sc1, g1, sh2, sc2, g2 = jnp.split(mod, N_MOD, axis=-1)
        h = rms_norm(x, mix_pre_g[l]) * (1.0 + sc1[:, None, :]) + sh1[:, None, :]
        y = hybrid_mixer(h, w_in[l], conv_w[l], conv_b[l], conv_ln_g[l], conv_ln_b[l], w_out[l])
        x = x + g1[:, None, :] * rms_norm(y, mix_post_g[l])
        h = rms_norm(x, ffn_pre_g[l]) * (1.0 + sc2[:, None, :]) + sh2[:, None, :]
        y = swiglu_ffn(h, w_gate[l], w_up[l], w_down[l])
        x = x + g2[:, None, :] * rms_norm(y, ffn_post_g[l])
    return x


def setup_inputs(seed=0):
    out = dict(first_inputs(seed))
    for name, value in second_inputs(seed + 1).items():
        if name != "x":
            out[name + "_2"] = value
    return out


def reference(
    x, attn_norm, w_in, fox_forget_bias, fox_q_norm, fox_k_norm, nsa_q_norm, cmp_k_norm,
    slc_k_norm, win_k_norm, cmp_pos_k, cmp_pos_v, cmp_w_k, cmp_w_v, w_out, ffn_norm, w_gate,
    w_up, w_down, c_2, ada_w_2, ada_b_2, mix_pre_g_2, mix_post_g_2, w_in_2, conv_w_2, conv_b_2,
    conv_ln_g_2, conv_ln_b_2, w_out_2, ffn_pre_g_2, ffn_post_g_2, w_gate_2, w_up_2, w_down_2,
):
    x = first_block(
        x, attn_norm, w_in, fox_forget_bias, fox_q_norm, fox_k_norm, nsa_q_norm, cmp_k_norm,
        slc_k_norm, win_k_norm, cmp_pos_k, cmp_pos_v, cmp_w_k, cmp_w_v, w_out, ffn_norm, w_gate,
        w_up, w_down,
    )
    return second_block(
        x, c_2, ada_w_2, ada_b_2, mix_pre_g_2, mix_post_g_2, w_in_2, conv_w_2, conv_b_2,
        conv_ln_g_2, conv_ln_b_2, w_out_2, ffn_pre_g_2, ffn_post_g_2, w_gate_2, w_up_2,
        w_down_2,
    )


_drawn_inputs = setup_inputs


def setup_inputs(seed=0):
    import zlib

    import numpy as np

    out = dict(_drawn_inputs(seed))
    spreads = {}
    factors = {'attn_norm': 4.545,
     'fox_q_norm': 8.0,
     'fox_k_norm': 8.0,
     'nsa_q_norm': 8.0,
     'cmp_k_norm': 8.0,
     'slc_k_norm': 8.0,
     'win_k_norm': 8.0,
     'cmp_pos_k': 28.553,
     'cmp_pos_v': 7.786,
     'ffn_norm': 3.858,
     'mix_pre_g_2': 8.0,
     'mix_post_g_2': 181.127,
     'conv_b_2': 57.04,
     'conv_ln_g_2': 171.843,
     'conv_ln_b_2': 179.377,
     'ffn_pre_g_2': 182.105,
     'ffn_post_g_2': 200.0}
    for name, (base, spread) in spreads.items():
        noise = np.random.default_rng([zlib.crc32(name.encode()), seed]).standard_normal(out[name].shape)
        drawn = base * np.exp(spread * noise) if base else spread * noise
        out[name] = __import__('jax').numpy.asarray(drawn.astype(out[name].dtype))
    for name, factor in factors.items():
        out[name] = (out[name] * factor).astype(out[name].dtype)
    return out
```

```python
def build_two_blocks(nc, io, out):
    import concourse.bass as bass
    from concourse import mybir
    from contextlib import ExitStack

    F32, F32R = mybir.dt.float32, mybir.dt.float32r
    ACT = mybir.ActivationFunctionType
    ALU = mybir.AluOpType
    AX = mybir.AxisListType
    P = 128

    T, D = io["x"].shape[1], io["x"].shape[2]
    TT = T // P
    KD = D // P
    FF = io["w_gate"].shape[2]
    HD = io["fox_q_norm"].shape[1]
    FOX_H = io["fox_forget_bias"].shape[1]
    NSA_H, NSA_G = 8, 2
    HPG = NSA_H // NSA_G
    CW = 512
    HPC = CW // HD
    KPU = 2
    NU = KD // KPU
    RAW_SLOTS, SPLIT_SLOTS = 4, 4
    SCALE = HD ** -0.5
    CMP_STRIDE, CMP_BLOCK = 16, io["cmp_pos_k"].shape[1]
    N_CMP = T // CMP_STRIDE - 1
    CONV_K, CONV_CH = io["conv_w_2"].shape[1], io["conv_w_2"].shape[2]
    CONV_G = CONV_CH // P
    BIG = 1e30
    TAB = T + P

    def wview(name):
        return io[name][0].rearrange("(k p) n -> p k n", p=P)

    W = {n: wview(n) for n in ("w_in", "w_out", "w_gate", "w_up", "w_down",
                               "w_in_2", "w_out_2", "w_gate_2", "w_up_2", "w_down_2", "ada_w_2")}

    def at(base, r, stride):
        return base if r is None else r * stride + base

    pos = {"C": 0, "U": 0, "R": 0, "A": 0}

    def chunk(w, n0, st, prev=None, k0=0, nu=NU, n_step=0, ada=None, **more):
        c = dict(w=w, n0=n0, n_step=n_step, st=st, prev=prev, k0=k0, nu=nu, C=pos["C"], U=pos["U"],
                 R=pos["R"], ada=None, **more)
        if ada is not None:
            c["ada"] = dict(ada, A=pos["A"])
            pos["A"] += 4
        pos["C"] += 1
        pos["U"] += nu
        pos["R"] += nu
        return c

    o_ff = 3 * FOX_H * HD
    o_qn = o_ff + FOX_H
    o_kv = o_qn + NSA_H * HD
    o_gt = o_kv + 6 * NSA_G * HD
    N_SMALL = FOX_H + 3 * NSA_H
    IN1 = [(0, ("normed", "fq", 0)), (CW, ("normed", "fq", 4)), (2 * CW, ("normed", "fk", 0)),
           (3 * CW, ("normed", "fk", 4)), (4 * CW, ("value", "fv", 0)), (5 * CW, ("value", "fv", 4)),
           (o_qn, ("normed", "nq", 0)), (o_qn + CW, ("normed", "nq", 4)), (o_kv, ("plain", "kcvc", 0)),
           (o_kv + CW, ("kv", "ks", 0)), (o_kv + 2 * CW, ("kv", "kw", 0))]
    S_IN1 = []
    prev = None
    for n0, cons in IN1:
        S_IN1.append(chunk("w_in", n0, "act", prev))
        prev = cons
    LAST1 = prev
    R_CMP = pos["R"]
    N_CMPU = 2 * 4
    pos["R"] += N_CMPU
    U_CMP = pos["U"]

    ada_blk = [0]

    def ada_pair(kind, col, dst, step=0, n=1):
        b = ada_blk[0]
        ada_blk[0] += n
        return [dict(kind=kind, col=col, dst=dst, blk=b, half=h, step=step) for h in range(2)]

    def out_pairs(w, dst, prev, ada, first):
        got = []
        for p in range(2):
            a = ada[p] or [None, None]
            for h in range(2):
                n = 2 * p + h
                got.append(chunk(w, n * CW, "mid", prev, ada=a[h], first=first if n == 0 else None))
                prev = ("add", dst, n, False)
        return got, prev

    S_OUT1, prev = out_pairs("w_out", "x", None,
                             [ada_pair("row", 4 * CW * 2, 0), ada_pair("row", 4 * CW * 2 + CW, CW)], "mix1")
    LAST_OUT1 = prev

    def ffn(tag, dst, ada_list, f):
        steps, prev, pair0 = [], None, f * (FF // CW)
        groups = [4, 4, 3]
        assert sum(groups) * CW == FF
        done = 0
        al = list(ada_list)
        for g, n in enumerate(groups):
            def pair(j, trips, prev):
                a = [None, None]
                if al:
                    blocks = [al.pop(0) for _ in range(min(trips, len(al)))]
                    assert len(blocks) == trips
                    st = blocks[1][1] - blocks[0][1] if trips > 1 else 0
                    assert all(blocks[q + 1][1] - blocks[q][1] == st and blocks[q + 1][0] == blocks[q][0]
                               for q in range(trips - 1))
                    a = ada_pair(blocks[0][0], blocks[0][1], blocks[0][2], st, trips)
                col = (done + j) * CW
                q = pair0 + done + j
                a1 = chunk("w_gate" + tag, col, "act", prev, n_step=CW, ada=a[0])
                a2 = chunk("w_up" + tag, col, "act", ("gate", q), n_step=CW, ada=a[1])
                if trips > 1:
                    for k, m in (("C", 2), ("U", 2 * NU), ("R", 2 * NU)):
                        pos[k] += m * (trips - 1)
                    if a[0]:
                        pos["A"] += 8 * (trips - 1)
                return [a1, a2], ("up", q, 4 * j)
            body, nxt = pair(0, 1, prev)
            steps += body
            j = 1
            while j < n:
                trips = 1
                while j + trips < n and (not al or (len(al) > trips and al[trips][0] == al[0][0]
                                         and al[trips][1] - al[trips - 1][1] == CW)):
                    trips += 1
                if trips > 1:
                    body, _ = pair(j, trips, nxt)
                    steps.append(dict(loop=trips, body=body))
                else:
                    body, _ = pair(j, 1, nxt)
                    steps += body
                j += trips
                nxt = ("up", pair0 + done + j - 1, 4 * (j - 1))
            prev = nxt
            kc = 4 * n
            for p in range(2):
                a = [None, None]
                if al:
                    k_, c_, d_ = al.pop(0)
                    a = ada_pair(k_, c_, d_)
                for h in range(2):
                    m = 2 * p + h
                    steps.append(chunk("w_down" + tag, m * CW, "mid", prev, k0=4 * done, nu=kc // KPU, ada=a[h],
                                       pairs=pair0 + done + n, first="ffn" if m == 0 else None))
                    prev = ("add", dst, m, dst == "y" and g == 0)
            done += n
        return steps, prev

    col_blocks = [("col", part * D + q * CW, (i * 4 + q) * 4) for i, part in enumerate((0, 1, 3, 4))
                  for q in range(4)]
    S_FFN1, LAST_FFN1 = ffn("", "x", col_blocks + [("row", 2 * D + 2 * CW, 2 * CW)], 0)

    IN2 = [(3 * 1024, ("keep_a", 0)), (4 * 1024, ("glu", 0)), (3 * 1024 + CW, ("keep_a", 1)),
           (4 * 1024 + CW, ("glu", 1)),
           (0, ("plain", "mq", 0)), (CW, ("plain", "mq", 4)), (2 * CW, ("plain", "mk", 0)),
           (3 * CW, ("plain", "mk", 4)), (4 * CW, ("value", "mv", 0)), (5 * CW, ("value", "mv", 4))]
    S_IN2 = []
    prev = None
    CONV_DVE_G = CONV_G // 2
    conv_ops = [(k, g) for k in range(CONV_K) for g in range(CONV_DVE_G)]
    CONV_FROM = 5
    for i, (n0, cons) in enumerate(IN2):
        cv = []
        if i >= CONV_FROM:
            per = -(-len(conv_ops) // (len(IN2) - CONV_FROM))
            cv = conv_ops[(i - CONV_FROM) * per:(i - CONV_FROM + 1) * per]
        S_IN2.append(chunk("w_in_2", n0, "act", prev, conv=cv))
        prev = cons
    LAST2 = prev
    S_OUT2, LAST_OUT2 = out_pairs("w_out_2", "y", None, [ada_pair("row", 2 * D + 3 * CW, 3 * CW), None], "mix2")
    for c in S_OUT2:
        if c["prev"]:
            c["prev"] = c["prev"][:3] + (True,)
    LAST_OUT2 = LAST_OUT2[:3] + (True,)
    S_FFN2, LAST_FFN2 = ffn("_2", "y", [("row2", 5 * D + q * CW, q * CW) for q in range(4)], 1)
    C_IN1, C_IN2 = len(S_IN1), S_IN2[0]["C"]
    LAST_C = {"in1": C_IN1, "out1": S_OUT1[-1]["C"] + 1, "ffn1": S_FFN1[-1]["C"] + 1,
              "in2": S_IN2[-1]["C"] + 1, "out2": S_OUT2[-1]["C"] + 1, "ffn2": S_FFN2[-1]["C"] + 1}
    LAST_U = {"in1": U_CMP, "out2": S_OUT2[-1]["U"] + NU, "in2": S_IN2[-1]["U"] + NU}
    TURNS = [c for _, c in IN1 if c[0] != "value"] + [c for _, c in IN2 if c[0] not in ("value", "keep_a")]
    NORMED = [c for _, c in IN1 if c[0] in ("normed", "kv")]

    consumer_of = {}

    def note(steps, last):
        for s in steps:
            for trip in range(s.get("loop", 1)):
                for c in s.get("body", [s]):
                    p = c["prev"]
                    C = c["C"] + 2 * trip
                    if p:
                        consumer_of[C - 1] = (p[0], p[1] + trip) if p[0] in ("gate", "up") else p
        consumer_of[C] = last

    note(S_IN1, LAST1)
    note(S_OUT1, LAST_OUT1)
    note(S_FFN1, LAST_FFN1)
    note(S_IN2, LAST2)
    note(S_OUT2, LAST_OUT2)
    note(S_FFN2, LAST_FFN2)
    READ, n_free = {}, [0, 0]
    for C in range(len(consumer_of)):
        p = consumer_of[C]
        if p[0] in ("gate", "up", "glu"):
            READ[C] = (p[0], 2 * p[1] + 2)
        else:
            n_free[C % 2] += 1
            READ[C] = (("free", C % 2), n_free[C % 2])

    JOBS = []
    for h in range(FOX_H):
        JOBS.append(dict(q="fq", k="fk", v="fv", h=h, kv=h, o=h, chunk=h, first=True, last=True, gate=None,
                         table="mask", decay=True, cmp=False))
    for h in range(NSA_H):
        for b, (k, vv) in enumerate((("ks", "vs"), ("kw", "vw"))):
            JOBS.append(dict(q="nq", k=k, v=vv, h=h, kv=h // HPG, o=FOX_H + h, chunk=FOX_H + h, first=b == 0,
                             last=b == 1, gate=3 * h + 1 + b, table="alibi", decay=False, cmp=b == 1))
    N_JOB1, N_OUT_1 = len(JOBS), FOX_H + NSA_H
    for h in range(8):
        JOBS.append(dict(q="mq", k="mk", v="mv", h=h, kv=h, o=N_OUT_1 + h, chunk=h, first=True, last=True,
                         gate=None, table="mask2", decay=False, cmp=False))

    top = ExitStack()
    with top:
        def sb(name, shape, dt=F32, scope=None, side=None):
            kw = {"side": side} if side else {}
            return (scope or top).enter_context(nc.sbuf_tensor(name, shape, dt, **kw))

        def sem(name):
            return top.enter_context(nc.semaphore(name))

        x_res = sb("x_res", [P, TT, D])
        mid_hi = sb("mid_hi", [P, KD, T], F32R)
        mid_lo = sb("mid_lo", [P, KD, T], F32R)
        raw = sb("raw", [P, RAW_SLOTS, KPU, CW])
        w_hi = sb("w_hi", [P, SPLIT_SLOTS, KPU, CW], F32R)
        w_lo = sb("w_lo", [P, SPLIT_SLOTS, KPU, CW], F32R)
        ysb = sb("ysb", [P, TT, CW])
        zsb = sb("zsb", [P, TT, CW])
        ident = sb("ident", [P, P])
        ones = sb("ones", [P, P])
        consts = sb("consts", [P, 4])
        cols = sb("cols", [P, P])
        pos_cols = sb("pos_cols", [P, 2 * CMP_BLOCK])
        conv_w_cols = sb("conv_w_cols", [P, CONV_G, CONV_K + 1])
        q_gain = sb("q_gain", [P, 2])
        norm_scale = sb("norm_scale", [P, 4, KD])
        norm_shift = sb("norm_shift", [P, 4, KD])
        mod_cols = sb("mod_cols", [P, 4 * KD])
        c_act = sb("c_act", [P, KD])
        sq_sum = sb("sq_sum", [P, 6, TT, 4])
        mean_sq = sb("mean_sq", [P, 6, TT])
        std = sb("std", [P, 6, TT])
        rstd = sb("rstd", [P, 6, TT])
        head_ss = sb("head_ss", [P, TT * HPC])
        head_std = sb("head_std", [P, TT * HPC])
        head_rstd = sb("head_rstd", [P, TT * HPC])
        ada_bias = sb("ada_bias", [1, CW])

        right = ExitStack()
        act_hi = sb("act_hi", [P, KD, T], F32R, right, "right")
        act_lo = sb("act_lo", [P, KD, T], F32R, right, "right")
        right.close()
        right = ExitStack()
        rows0 = sb("rows0", [P, P], F32, right, "right")
        rows1 = sb("rows1", [2 * CMP_BLOCK, P], F32, right, "right")
        conv_rows = sb("conv_rows", [CONV_K, CONV_CH], F32, right, "right")
        w_small = sb("w_small", [P, KD, N_SMALL], F32, right, "right")
        right.close()
        right = ExitStack()
        blk_k = sb("blk_k", [P, CMP_BLOCK, 64], F32, right, "right")
        blk_v = sb("blk_v", [P, CMP_BLOCK, 64], F32, right, "right")
        lf_cols = sb("lf_cols", [P, TT, FOX_H, 64], F32, right, "right")
        right.close()
        right = ExitStack()
        dec_l = sb("dec_l", [64, FOX_H, T], F32, right, "right")
        dec_r = sb("dec_r", [64, FOX_H, T], F32, right, "right")
        cost1 = sb("cost1", [P, 2, TAB], F32, right, "right")
        prob1 = sb("prob1", [P, 2, TAB], F32, right, "right")
        probT1 = sb("probT1", [P, 2, TAB], F32, right, "right")
        cmp_cost = sb("cmp_cost", [P, TT * NSA_H, 32], F32, right, "right")
        cmp_prob = sb("cmp_prob", [P, TT * NSA_H, 32], F32, right, "right")
        cmp_probT = sb("cmp_probT", [P, 2, T], F32, right, "right")
        right.close()
        right = ExitStack()
        cost2 = sb("cost2", [P, 2, TAB], F32, right, "right")
        prob2 = sb("prob2", [P, 2, TAB], F32, right, "right")
        probT2 = sb("probT2", [P, 2, TAB], F32, right, "right")
        conv_sq = sb("conv_sq", [P, CONV_G, T], F32, right, "right")
        conv_mu = sb("conv_mu", [P, T], F32, right, "right")
        conv_rs = sb("conv_rs", [P, T], F32, right, "right")
        right.close()
        right = ExitStack()
        for n_ in ("act_hold_a", "act_hold_b"):
            sb(n_, [P, KD, T], F32, right, "right")

        A = ExitStack()
        heads = {n: sb(n, [P, k, T], F32, A) for n, k in
                 (("fq", FOX_H), ("fk", FOX_H), ("nq", NSA_H), ("kc", NSA_G), ("vc", NSA_G), ("ks", NSA_G),
                  ("kw", NSA_G))}
        vals = {n: sb(n, [P, TT, k, HD], F32, A) for n, k in (("fv", FOX_H), ("vs", NSA_G), ("vw", NSA_G))}
        ws_hi = sb("ws_hi", [P, KD, N_SMALL], F32R, A)
        ws_lo = sb("ws_lo", [P, KD, N_SMALL], F32R, A)
        small = sb("small", [P, TT, N_SMALL], F32, A)
        forget_bias = sb("forget_bias", [P, FOX_H], F32, A)
        upper = sb("upper", [P, T], F32, A)
        mask = sb("mask", [P, T], F32, A)
        dist = sb("dist", [P, T], F32, A)
        alibi = sb("alibi", [P, NSA_H, T], F32, A)
        cmp_tab = sb("cmp_tab", [P, TT, NSA_H, 32], F32, A)
        cmp_ok = sb("cmp_ok", [P, TT, 32], F32, A)
        lf = sb("lf", [P, 6, TT, FOX_H], F32, A)
        gates = sb("gates", [P, TT, 3 * NSA_H], F32, A)
        gate_e = sb("gate_e", [P, TT, 3 * NSA_H], F32, A)
        kcn = sb("kcn", [64, HD], F32, A)
        kc_ss = sb("kc_ss", [64, 3], F32, A)
        kcmpT = sb("kcmpT", [P, 64], F32, A)
        vcmp = sb("vcmp", [P, NSA_G, HD], F32, A)
        cmp_min = sb("cmp_min", [P, TT * NSA_H], F32, A)
        cmp_sum = sb("cmp_sum", [P, TT * NSA_H], F32, A)
        row_min1 = sb("row_min1", [P, 2, TT], F32, A)
        row_sum1 = sb("row_sum1", [P, 2, TT], F32, A)
        row_inv1 = sb("row_inv1", [P, 2, TT], F32, A)
        A.close()

        B = ExitStack()
        gate_row1 = sb("gate_row1", [P, D], F32, B)
        ada_raw = sb("ada_raw", [P, 2, KPU, CW], F32, B)
        ada_acc = sb("ada_acc", [P, CW], F32, B)
        mask2 = sb("mask2", [P, T], F32, B)
        Cs = ExitStack()
        for n in ("mq", "mk"):
            heads[n] = sb(n, [P, 8, T], F32, Cs)
        vals["mv"] = sb("mv", [P, TT, 8, HD], F32, Cs)
        a_keep = sb("a_keep", [P, TT, CW], F32, Cs)
        uT = sb("uT", [P, CONV_G, CONV_K - 1 + T], F32, Cs)
        convT = sb("convT", [P, CONV_G, T], F32, Cs)
        conv_tmp = sb("conv_tmp", [P, 1, T], F32, Cs)
        row_min2 = sb("row_min2", [P, 2, TT], F32, Cs)
        row_sum2 = sb("row_sum2", [P, 2, TT], F32, Cs)
        row_inv2 = sb("row_inv2", [P, 2, TT], F32, Cs)
        Cs.close()
        Ds = ExitStack()
        y_acc = sb("y_acc", [P, TT, D], F32, Ds)
        gate_row2 = sb("gate_row2", [P, D], F32, Ds)
        Ds.close()
        B.close()
        right.close()

        bank = [top.enter_context(nc.psum_tensor(f"bank{i}", [P, CW], F32)) for i in range(8)]

        def acc(C):
            return [bank[2 * (C % 2)], bank[2 * (C % 2) + 1]]

        TURN = [bank[4], bank[5]]
        MISC = [bank[6], bank[7]]

        raw_loaded = [sem(f"raw_loaded{i}") for i in range(RAW_SLOTS)]
        hi_done, lo_done, parts_used = sem("hi_done"), sem("lo_done"), sem("parts_used")
        acc_free = [sem("acc_free0"), sem("acc_free1")]
        params_loaded, x_loaded, small_loaded = sem("params_loaded"), sem("x_loaded"), sem("small_loaded")
        tables_made = sem("tables_made")
        cols_turned, cols_ready = sem("cols_turned"), sem("cols_ready")
        c_ready = sem("c_ready")
        ss_act, ms_ready, std_ready, rstd_ready = (sem("ss_act"), sem("ms_ready"), sem("std_ready"),
                                                   sem("rstd_ready"))
        xn_ready, xn_turned, full_ready = sem("xn_ready"), sem("xn_turned"), sem("full_ready")
        act_hi_done, act_lo_done = sem("act_hi_done"), sem("act_lo_done")
        ws_split_hi, ws_split, small_mm, small_out = (sem("ws_split_hi"), sem("ws_split"), sem("small_mm"),
                                                      sem("small_out"))
        head_sq, head_std_ready = sem("head_sq"), sem("head_std_ready")
        turned, turn_out_a, turn_out_d = sem("turned"), sem("turn_out_a"), sem("turn_out_d")
        glu_sig, glu_ready = sem("glu_sig"), sem("glu_ready")
        sig_ready, h_ready, h_turned = sem("sig_ready"), sem("h_ready"), sem("h_turned")
        mid_hi_done, mid_lo_done = sem("mid_hi_done"), sem("mid_lo_done")
        ada_loaded = [sem("ada_loaded0"), sem("ada_loaded1")]
        ada_bias_loaded, ada_used, ada_summed, ada_out = (sem("ada_bias_loaded"), sem("ada_used"),
                                                          sem("ada_summed"), sem("ada_out"))
        gate_loaded = sem("gate_loaded")
        blk_zero, blk_ready, cmp_used = sem("blk_zero"), sem("blk_ready"), sem("cmp_used")
        kc_sq, kc_std, kc_n, kc_turned, kc_ready, vc_ready = (sem("kc_sq"), sem("kc_std"), sem("kc_n"),
                                                              sem("kc_turned"), sem("kc_ready"), sem("vc_ready"))
        lf_zero, lf_a, lf_d, lf_cum, dec_zero, dec_a, dec_d = (
            sem("lf_zero"), sem("lf_a"), sem("lf_d"), sem("lf_cum"), sem("dec_zero"), sem("dec_a"), sem("dec_d"))
        gate_exp, gates_ready = sem("gate_exp"), sem("gates_ready")
        cmp_scored, cmp_shift, cmp_exp, cmp_p, cmp_pT, cmp_pT_out = (
            sem("cmp_scored"), sem("cmp_shift"), sem("cmp_exp"), sem("cmp_p"), sem("cmp_pT"), sem("cmp_pT_out"))
        scored, reduced, exped, scaled, p_turned, p_out, pv_done = (
            sem("scored"), sem("reduced"), sem("exped"), sem("scaled"), sem("p_turned"), sem("p_out"),
            sem("pv_done"))
        o_hi, o_lo = sem("o_hi"), sem("o_lo")
        uT_zero, conv_pool, conv_dve = sem("uT_zero"), sem("conv_pool"), sem("conv_dve")
        ln_sum, ln_d, ln_sq, ln_var, ln_std, ln_y, ln_silu, ln_hi, ln_lo = (
            sem("ln_sum"), sem("ln_d"), sem("ln_sq"), sem("ln_var"), sem("ln_std"), sem("ln_y"), sem("ln_silu"),
            sem("ln_hi"), sem("ln_lo"))
        x_updated, out_stored = sem("x_updated"), sem("out_stored")
        chain_d, chain_a, chain_p = sem("chain_d"), sem("chain_a"), sem("chain_p")

        READ_SEM = {"gate": sig_ready, "up": h_ready, "glu": glu_sig, ("free", 0): acc_free[0],
                    ("free", 1): acc_free[1]}

        def wait_read(eng, C, r=None):
            key, value = READ[C]
            eng.wait_ge(READ_SEM[key], at(value, r, 2))

        ROWS0 = [(io["attn_norm"][0].rearrange("(k p) -> k p", p=P), 0, KD),
                 (io["ffn_norm"][0].rearrange("(k p) -> k p", p=P), 16, KD),
                 (io["mix_pre_g_2"][0].rearrange("(k p) -> k p", p=P), 32, KD),
                 (io["ffn_pre_g_2"][0].rearrange("(k p) -> k p", p=P), 48, KD),
                 (io["c_2"][0].rearrange("(k p) -> k p", p=P), 64, KD),
                 (io["fox_q_norm"], 80, 1), (io["fox_k_norm"], 81, 1), (io["nsa_q_norm"], 82, 1),
                 (io["cmp_k_norm"], 83, 1), (io["slc_k_norm"], 84, 1), (io["win_k_norm"], 85, 1),
                 (io["conv_b_2"][0].rearrange("(k p) -> k p", p=P), 86, CONV_G),
                 (io["conv_ln_g_2"][0].rearrange("(k p) -> k p", p=P), 94, CONV_G),
                 (io["conv_ln_b_2"][0].rearrange("(k p) -> k p", p=P), 102, CONV_G)]
        N_PARAM = len(ROWS0) + 4

        block = top.enter_context(nc.Block())

        def keep(eng, prev, t, put, done):
            kind = prev[0]
            src = TURN[t]
            cols_t = slice(t * P, (t + 1) * P)

            def v(k0, k1):
                return src[:, k0 * P:k1 * P].rearrange("p (k t) -> p k t", t=P)

            if kind == "glu":
                o = uT[:, 4 * prev[1]:4 * prev[1] + 4, CONV_K - 1 + t * P:CONV_K - 1 + (t + 1) * P]
                put(o, v(0, 4), 1.0).then_inc(done, 1)
            elif kind == "plain" and prev[1] == "kcvc":
                put(heads["kc"][:, :, cols_t], v(0, 2), 1.0)
                put(heads["vc"][:, :, cols_t], v(2, 4), 1.0).then_inc(done, 1)
            elif kind == "plain":
                g = -SCALE if prev[1] == "mq" else 1.0
                put(heads[prev[1]][:, prev[2]:prev[2] + HPC, cols_t], v(0, 4), g).then_inc(done, 1)
            else:
                k = HPC if kind == "normed" else NSA_G
                gain = {"fq": q_gain[:, 0:1], "fk": cols[:, 81:82], "nq": q_gain[:, 1:2],
                        "ks": cols[:, 84:85], "kw": cols[:, 85:86]}[prev[1]]
                put(heads[prev[1]][:, prev[2]:prev[2] + k, cols_t], v(0, k), gain).then_inc(done, 1)

        def run(steps, eng, do):
            for s in steps:
                if "loop" in s:
                    with eng.Fori(0, s["loop"]) as r:
                        for c in s["body"]:
                            do(c, r)
                else:
                    do(s, None)

        @block.sync
        def _(sp):
            for t in range(TT):
                sp.dma_start(x_res[:, t, :], io["x"][0, t * P:(t + 1) * P, :]).then_inc(x_loaded, 16)
            sp.dma_start(w_small[:, :, 0:FOX_H], W["w_in"][:, :, o_ff:o_ff + FOX_H]).then_inc(small_loaded, 16)
            sp.dma_start(w_small[:, :, FOX_H:N_SMALL], W["w_in"][:, :, o_gt:o_gt + 3 * NSA_H]).then_inc(
                small_loaded, 16)

            def slot_free(R, r, stride):
                R -= RAW_SLOTS
                if R < 0:
                    return
                if R_CMP <= R < R_CMP + N_CMPU:
                    sp.wait_ge(cmp_used, R - R_CMP + 1)
                else:
                    sp.wait_ge(lo_done, at((R if R < R_CMP else R - N_CMPU) + 1, r, stride))

            def ada_load(c, r, i):
                a = c["ada"]
                unit = a["A"] + i
                if unit >= 2:
                    sp.wait_ge(ada_used, at(2 * (unit - 1), r, 16))
                k = a["half"] * 8 + 2 * i
                n0 = at(a["col"], r, a["step"])
                sp.dma_start(ada_raw[:, unit % 2], W["ada_w_2"][:, k:k + KPU, bass.ds(n0, CW)]).then_inc(
                    ada_loaded[unit % 2], 16)
                if a["half"] == 0 and i == 0:
                    if a["blk"] >= 1:
                        sp.wait_ge(ada_summed, at(a["blk"], r, 1))
                    sp.dma_start(ada_bias[:, :], io["ada_b_2"][0:1, bass.ds(n0, CW)]).then_inc(ada_bias_loaded, 16)

            def load(c, r):
                for u in range(c["nu"]):
                    R = c["R"] + u
                    slot_free(R, r, 2 * c["nu"])
                    k = c["k0"] + KPU * u
                    n0 = at(c["n0"], r, c["n_step"])
                    sp.dma_start(raw[:, R % RAW_SLOTS], W[c["w"]][:, k:k + KPU, bass.ds(n0, CW)]).then_inc(
                        raw_loaded[R % RAW_SLOTS], 16)
                    if c["ada"] and u in (1, 2, 5, 6)[:4]:
                        ada_load(c, r, (1, 2, 5, 6).index(u))
                if c["ada"] and c["nu"] < 7:
                    ada_load(c, r, 3)

            run(S_IN1, sp, load)
            for j in range(N_CMPU):
                R = R_CMP + j
                slot_free(R, None, 0)
                src = io["cmp_w_k" if j < 4 else "cmp_w_v"][0].rearrange("l d e -> d l e")
                l0 = 8 * (j % 4)
                sp.dma_start(raw[:, R % RAW_SLOTS].rearrange("p a n -> p (a n)").rearrange("p (l e) -> p l e", e=HD),
                             src[:, l0:l0 + 8, :]).then_inc(raw_loaded[R % RAW_SLOTS], 16)
            c0 = S_OUT1[0]
            for u in range(RAW_SLOTS):
                slot_free(c0["R"] + u, None, 0)
                sp.dma_start(raw[:, (c0["R"] + u) % RAW_SLOTS],
                             W["w_out"][:, KPU * u:KPU * u + KPU, 0:CW]).then_inc(
                    raw_loaded[(c0["R"] + u) % RAW_SLOTS], 16)
            sp.wait_ge(o_lo, N_OUT_1)
            sp.dma_start(gate_row1[:, :], io["mix_post_g_2"][0].partition_broadcast(P)).then_inc(gate_loaded, 16)

            def load_out1(c, r):
                if c is c0:
                    for u in range(c["nu"]):
                        R = c["R"] + u
                        if u >= RAW_SLOTS:
                            slot_free(R, r, 0)
                            sp.dma_start(raw[:, R % RAW_SLOTS],
                                         W["w_out"][:, KPU * u:KPU * u + KPU, 0:CW]).then_inc(
                                raw_loaded[R % RAW_SLOTS], 16)
                        if u in (1, 2, 5, 6):
                            ada_load(c, r, (1, 2, 5, 6).index(u))
                else:
                    load(c, r)

            run(S_OUT1, sp, load_out1)
            run(S_FFN1, sp, load)
            run(S_IN2, sp, load)
            run(S_OUT2, sp, load)
            sp.wait_ge(o_lo, N_OUT_1 + 8)
            sp.wait_ge(ln_lo, 1)
            sp.dma_start(gate_row2[:, :], io["ffn_post_g_2"][0].partition_broadcast(P)).then_inc(gate_loaded, 16)
            run(S_FFN2, sp, load)
            for t in range(TT):
                for h in range(2):
                    sp.wait_ge(x_updated, 4 + 2 * t + h + 1)
                    sp.dma_start(out[0, t * P:(t + 1) * P, h * D // 2:(h + 1) * D // 2],
                                 x_res[:, t, h * D // 2:(h + 1) * D // 2]).then_inc(out_stored, 16)
            sp.wait_ge(out_stored, 16 * 2 * TT)

        @block.gpsimd
        def _(pool):
            n = [0]

            def link(ins):
                n[0] += 1
                ins.then_inc(chain_p, 1)
                pool.wait_ge(chain_p, n[0])

            for i, val in enumerate((1e-6, 1e-5, 1.0, 0.0)):
                link(pool.memset(consts[:, i:i + 1], val))
            link(pool.memset(ident[:, :], 0.0))
            link(pool.affine_select(out=ident[:, :], in_=ident[:, :], pattern=[[-1, P]],
                                    compare_op=ALU.not_equal, fill=1.0, base=0, channel_multiplier=1))
            link(pool.memset(ones[:, :], 1.0))
            pool.memset(norm_shift[:, 0:2, :], 0.0).then_inc(tables_made, 1)
            link(pool.memset(upper[:, :], 1.0))
            link(pool.affine_select(out=upper[:, :], in_=upper[:, :], pattern=[[1, T]], compare_op=ALU.is_ge,
                                    fill=0.0, base=0, channel_multiplier=-1))
            link(pool.memset(mask[:, :], 0.0))
            link(pool.affine_select(out=mask[:, :], in_=mask[:, :], pattern=[[-1, T]], compare_op=ALU.is_ge,
                                    fill=BIG, base=P, channel_multiplier=1))
            link(pool.iota(dist[:, :], pattern=[[-1, T]], base=P, channel_multiplier=1,
                           allow_small_or_imprecise_dtypes=True))
            for h in range(NSA_H):
                slope = 2.0 ** (-8.0 * (h + 1) / NSA_H)
                link(pool.tensor_scalar(alibi[:, h, :], dist[:, :], slope, None, ALU.mult))
                link(pool.tensor_tensor(alibi[:, h, :], alibi[:, h, :], mask[:, :], ALU.add))
            pat = [[P, TT], [0, NSA_H], [-CMP_STRIDE, 32]]
            base = -(CMP_BLOCK - 1)
            link(pool.iota(cmp_tab[:, :, :, :], pattern=pat, base=base, channel_multiplier=1,
                           allow_small_or_imprecise_dtypes=True))
            for h in range(NSA_H):
                slope = 2.0 ** (-8.0 * (h + 1) / NSA_H)
                link(pool.tensor_scalar(cmp_tab[:, :, h, :], cmp_tab[:, :, h, :], slope, None, ALU.mult))
            link(pool.affine_select(out=cmp_tab[:, :, :, :], in_=cmp_tab[:, :, :, :], pattern=pat,
                                    compare_op=ALU.is_ge, fill=BIG, base=base, channel_multiplier=1))
            link(pool.memset(cmp_ok[:, :, :], 1.0))
            link(pool.affine_select(out=cmp_ok[:, :, :], in_=cmp_ok[:, :, :], pattern=[pat[0], pat[2]],
                                    compare_op=ALU.is_ge, fill=0.0, base=base, channel_multiplier=1))
            pool.memset(vcmp[:, :, :], 0.0).then_inc(tables_made, 1)
            pool.wait_ge(parts_used, U_CMP)
            pool.memset(lf_cols[:, :, :, :], 0.0).then_inc(blk_zero, 1)
            pool.memset(blk_k[:, :, :], 0.0).then_inc(blk_zero, 1)
            pool.memset(blk_v[:, :, :], 0.0).then_inc(blk_zero, 1)
            pool.wait_ge(cmp_used, N_CMPU)
            link(pool.memset(dec_l[:, :, :], 0.0))
            link(pool.memset(dec_r[:, :, :], 0.0))
            link(pool.memset(dec_l[32:33, :, :], 1.0))
            pool.memset(dec_r[0:1, :, :], 1.0).then_inc(dec_zero, 1)
            pool.wait_ge(o_lo, N_OUT_1)
            link(pool.memset(mask2[:, :], 0.0))
            link(pool.affine_select(out=mask2[:, :], in_=mask2[:, :], pattern=[[-1, T]], compare_op=ALU.is_ge,
                                    fill=BIG, base=P, channel_multiplier=1))
            pool.memset(uT[:, :, 0:CONV_K - 1], 0.0).then_inc(uT_zero, 1)
            pool.wait_ge(uT_zero, 1)
            pool.wait_ge(turn_out_a, len([c for c in TURNS if c[1] not in ("mq", "mk")]))
            pool.wait_ge(turn_out_d, len([c for c in TURNS if c[1] not in ("mq", "mk")]))
            for k in range(CONV_K):
                for g in range(CONV_DVE_G, CONV_G):
                    src = uT[:, g, k:k + T]
                    wk = conv_w_cols[:, g, k:k + 1]
                    if k == 0:
                        ins = pool.tensor_scalar(convT[:, g, :], src, wk, cols[:, 86 + g:87 + g], ALU.mult, ALU.add)
                        link(ins)
                    else:
                        link(pool.tensor_scalar(conv_tmp[:, 0, :], src, wk, None, ALU.mult))
                        ins = pool.tensor_tensor(convT[:, g, :], convT[:, g, :], conv_tmp[:, 0, :], ALU.add)
                        if (k, g) == (CONV_K - 1, CONV_G - 1):
                            ins.then_inc(conv_pool, 1)
                        else:
                            link(ins)

        @block.tensor
        def _(pe):
            pe.wait_ge(tables_made, 1)
            pe.wait_ge(params_loaded, 16 * N_PARAM)
            pe.transpose(MISC[0][:, 0:110], rows0[0:110, :], ident[0:110, 0:110])
            pe.transpose(MISC[0][:, 128:192], rows1[:, :], ident[0:64, 0:64])
            for g in range(CONV_G):
                ins = pe.transpose(MISC[1][:, 32 * g:32 * g + CONV_K], conv_rows[:, g * P:(g + 1) * P],
                                   ident[0:CONV_K, 0:CONV_K])
            ins.then_inc(cols_turned, 1)

            def norm(n):
                for j in range(NU):
                    i = n * NU + j
                    pe.wait_ge(xn_ready, i + 1)
                    if i >= 2:
                        pe.wait_ge(full_ready, i - 1)
                    for c in range(KPU):
                        for t in range(TT):
                            ins = pe.transpose(TURN[i % 2][:, (c * TT + t) * P:(c * TT + t + 1) * P],
                                               ysb[:, i % 2, (t * KPU + c) * P:(t * KPU + c + 1) * P], ident[:, :])
                    ins.then_inc(xn_turned, 1)

            def consume(prev, C, r):
                if prev is None or prev[0] in ("value", "keep_a", "add", "gate"):
                    return
                if prev[0] == "up":
                    q = prev[1]
                    pe.wait_ge(h_ready, at(2 * q + 2, r, 2))
                    if q >= 1:
                        pe.wait_ge(mid_lo_done, at(2 * q, r, 2))
                    for t in range(TT):
                        for c in range(HPC):
                            ins = pe.transpose(TURN[t][:, c * P:(c + 1) * P], zsb[:, t, c * P:(c + 1) * P], ident[:, :])
                        ins.then_inc(h_turned, 1)
                    return
                i = TURNS.index(prev)
                if prev[0] == "glu":
                    pe.wait_ge(glu_ready, 2 * prev[1] + 2)
                else:
                    wait_read(pe, C - 1)
                if i >= 1:
                    pe.wait_ge(turn_out_a, i)
                    pe.wait_ge(turn_out_d, i)
                k = NSA_G if prev[0] == "kv" else HPC
                for t in range(TT):
                    for c in range(k):
                        ins = pe.transpose(TURN[t][:, c * P:(c + 1) * P], ysb[:, t, c * P:(c + 1) * P], ident[:, :])
                ins.then_inc(turned, 1)

            def gemm(c, r):
                hi, lo = (act_hi, act_lo) if c["st"] == "act" else (mid_hi, mid_lo)
                C, nu = c["C"], c["nu"]
                A_ = acc(C)
                for u in range(nu):
                    if u == 0:
                        if C >= 2:
                            wait_read(pe, C - 2, r)
                        if c.get("first") == "mix1":
                            pe.wait_ge(o_lo, N_OUT_1)
                        if c.get("first") == "mix2":
                            pe.wait_ge(o_lo, N_OUT_1 + 8)
                            pe.wait_ge(ln_lo, 1)
                    if c.get("first") == "ffn":
                        pe.wait_ge(mid_lo_done, 2 * (c["pairs"] - (0 if u >= nu - 2 else 1)))
                    U = c["U"] + u
                    pe.wait_ge(lo_done, at(U + 1, r, 2 * nu))
                    s = U % SPLIT_SLOTS
                    for kk in range(KPU):
                        k = KPU * u + kk
                        for t in range(TT):
                            h_, l_ = hi[:, k, t * P:(t + 1) * P], lo[:, k, t * P:(t + 1) * P]
                            pe.matmul(A_[t][:, :], h_, w_hi[:, s, kk, :], start=(k == 0), stop=False)
                            pe.matmul(A_[t][:, :], h_, w_lo[:, s, kk, :], start=False, stop=False)
                            ins = pe.matmul(A_[t][:, :], l_, w_hi[:, s, kk, :], start=False,
                                            stop=(k == KPU * nu - 1))
                    ins.then_inc(parts_used, 1)
                    if u == min(4, nu - 3):
                        consume(c["prev"], C, r)
                    a = c["ada"]
                    if a and a["half"] == 1 and u == 5:
                        pe.wait_ge(ada_used, at(2 * (a["A"] + 4), r, 16))
                        pe.wait_ge(ada_bias_loaded, at(16 * (a["blk"] + 1), r, 16))
                        if a["blk"] >= 1:
                            pe.wait_ge(ada_out, at(a["blk"], r, 1))
                        if a["kind"] == "col":
                            for j in range(4):
                                pe.matmul(MISC[0][:, j:j + 1], ada_acc[:, j * P:(j + 1) * P], ones[:, 0:1],
                                          start=True, stop=False)
                                ins = pe.matmul(MISC[0][:, j:j + 1], ada_bias[0:1, j * P:(j + 1) * P],
                                                ones[0:1, 0:1], start=False, stop=True)
                        else:
                            pe.matmul(MISC[0][:, :], ones[:, :], ada_acc[:, :], start=True, stop=False)
                            ins = pe.matmul(MISC[0][:, :], ones[0:1, :], ada_bias[0:1, :], start=False, stop=True)
                        ins.then_inc(ada_summed, 1)

            def attend(j0, j1, cost, prob, probT):
                def scores(j):
                    b, s = JOBS[j], bank[j % 2]
                    if j - j0 >= 2:
                        pe.wait_ge(reduced, 2 * (j - 1))
                    q, k = heads[b["q"]], heads[b["k"]]
                    for t, c0, n in ((0, 0, P), (1, P, T)):
                        ins = pe.matmul(s[:, c0:c0 + n], q[:, b["h"], t * P:(t + 1) * P], k[:, b["kv"], 0:n],
                                        start=True, stop=not b["decay"])
                        if b["decay"]:
                            ins = pe.matmul(s[:, c0:c0 + n], dec_l[:, b["h"], t * P:(t + 1) * P],
                                            dec_r[:, b["h"], 0:n], start=False, stop=True)
                    ins.then_inc(scored, 1)

                def turn(j):
                    pe.wait_ge(scaled, 2 * j + 2)
                    if j - j0 >= 2:
                        pe.wait_ge(p_out, j - 1)
                    for c in range(3):
                        ins = pe.transpose(bank[2 + j % 2][:, c * P:(c + 1) * P], prob[:, j % 2, c * P:(c + 1) * P],
                                           ident[:, :])
                    ins.then_inc(p_turned, 1)

                def values(j):
                    b = JOBS[j]
                    o = bank[4 + b["o"] % 2]
                    pe.wait_ge(p_out, j + 1)
                    if b["first"] and j > j0 and b["o"] - JOBS[j0]["o"] >= 2:
                        pe.wait_ge(o_lo, b["o"] - 1)
                    v = vals[b["v"]]
                    pT = probT[:, j % 2, :]
                    pe.matmul(o[:, 0:T], v[:, 0, b["kv"], :], pT[:, 0:T], start=b["first"], stop=False)
                    ins = pe.matmul(o[:, P:T], v[:, 1, b["kv"], :], pT[:, T:TAB], start=False, stop=b["last"] and not b["cmp"])
                    if b["cmp"]:
                        r0 = 32 * (b["h"] % 4)
                        ins = pe.matmul(o[:, 0:T], vcmp[r0:r0 + 32, b["kv"], :],
                                        cmp_probT[r0:r0 + 32, b["h"] // 4, :], start=False, stop=True)
                    ins.then_inc(pv_done, 1)

                for i in range(j0, j1 + 2):
                    if i < j1:
                        scores(i)
                    if j0 < i <= j1:
                        turn(i - 1)
                    if i >= j0 + 2:
                        values(i - 2)

            norm(0)
            pe.wait_ge(act_lo_done, NU)
            pe.wait_ge(ws_split, 1)
            pe.wait_ge(cols_ready, 2)
            for t in range(TT):
                for k in range(KD):
                    o = MISC[0][:, t * N_SMALL:(t + 1) * N_SMALL]
                    h_, l_ = act_hi[:, k, t * P:(t + 1) * P], act_lo[:, k, t * P:(t + 1) * P]
                    pe.matmul(o, h_, ws_hi[:, k, :], start=(k == 0), stop=False)
                    pe.matmul(o, h_, ws_lo[:, k, :], start=False, stop=False)
                    ins = pe.matmul(o, l_, ws_hi[:, k, :], start=False, stop=(k == KD - 1))
            ins.then_inc(small_mm, 1)
            run(S_IN1, pe, gemm)
            consume(LAST1, C_IN1, None)
            wait_read(pe, C_IN1 - 2)
            wait_read(pe, C_IN1 - 1)
            pe.wait_ge(lf_d, 2)
            pe.wait_ge(tables_made, 2)
            for h in range(FOX_H):
                o, c0 = bank[h // 2], (h % 2) * T
                pe.matmul(o[0:64, c0:c0 + T], lf_cols[:, 0, h, :], upper[:, :], start=True, stop=False)
                ins = pe.matmul(o[0:64, c0 + P:c0 + T], lf_cols[:, 1, h, :], upper[:, 0:P], start=False, stop=True)
            ins.then_inc(lf_cum, 1)
            pe.wait_ge(small_out, 1)
            for kind, blk in ((0, blk_k), (1, blk_v)):
                pe.wait_ge(blk_ready, kind + 1)
                for j in range(4):
                    R = R_CMP + 4 * kind + j
                    pe.wait_ge(raw_loaded[R % RAW_SLOTS], 16 * (R // RAW_SLOTS + 1))
                    w = raw[:, R % RAW_SLOTS].rearrange("p a n -> p (a n)")
                    for l in range(8):
                        ins = pe.matmul(MISC[kind][0:64, 0:HD], blk[:, 8 * j + l, :], w[:, l * HD:(l + 1) * HD],
                                        start=(j + l == 0), stop=(j == 3 and l == 7))
                    ins.then_inc(cmp_used, 1)
            pe.wait_ge(kc_n, 1)
            pe.wait_ge(turn_out_a, len(IN1) - 2)
            pe.wait_ge(turn_out_d, len(IN1) - 2)
            pe.transpose(TURN[0][:, 0:64], kcn[:, :], ident[0:64, 0:64]).then_inc(kc_turned, 1)
            pe.wait_ge(kc_ready, 1)
            pe.wait_ge(vc_ready, 1)
            for h in range(NSA_H):
                for t in range(TT):
                    g = h // HPG
                    c0 = (t * NSA_H + h) * 32
                    ins = pe.matmul(MISC[1][:, c0:c0 + 32], heads["nq"][:, h, t * P:(t + 1) * P],
                                    kcmpT[:, 32 * g:32 * g + 32], start=True, stop=True)
            ins.then_inc(cmp_scored, 1)
            pe.wait_ge(cmp_p, 1)
            for hh in range(2):
                for t in range(TT):
                    src = cmp_prob[:, t * NSA_H + hh * 4:t * NSA_H + hh * 4 + 4, :].rearrange("p h n -> p (h n)")
                    ins = pe.transpose(MISC[0][:, (hh * TT + t) * P:(hh * TT + t + 1) * P], src, ident[:, :])
            ins.then_inc(cmp_pT, 1)
            pe.wait_ge(cmp_pT_out, 1)
            pe.wait_ge(dec_a, 1)
            pe.wait_ge(dec_d, 1)
            attend(0, N_JOB1, cost1, prob1, probT1)

            def flush_acc(C):
                wait_read(pe, C - 2)
                wait_read(pe, C - 1)

            run(S_OUT1, pe, gemm)
            norm(1)
            pe.wait_ge(act_lo_done, 2 * NU)
            run(S_FFN1, pe, gemm)
            norm(2)
            pe.wait_ge(act_lo_done, 3 * NU)
            run(S_IN2, pe, gemm)
            consume(LAST2, LAST_C["in2"], None)
            flush_acc(LAST_C["in2"])
            pe.wait_ge(turn_out_a, len(TURNS))
            pe.wait_ge(turn_out_d, len(TURNS))
            attend(N_JOB1, len(JOBS), cost2, prob2, probT2)
            pe.wait_ge(conv_pool, 1)
            pe.wait_ge(conv_dve, len(conv_ops))
            for g in range(CONV_G):
                ins = pe.matmul(MISC[0][:, 0:T], ones[:, :], convT[:, g, :], start=(g == 0), stop=(g == CONV_G - 1))
            ins.then_inc(ln_sum, 1)
            pe.wait_ge(ln_sq, 1)
            for g in range(CONV_G):
                ins = pe.matmul(MISC[1][:, 0:T], ones[:, :], conv_sq[:, g, :], start=(g == 0), stop=(g == CONV_G - 1))
            ins.then_inc(ln_var, 1)
            run(S_OUT2, pe, gemm)
            norm(3)
            pe.wait_ge(act_lo_done, 4 * NU)
            run(S_FFN2, pe, gemm)

        @block.scalar
        def _(act):
            chain = [0]

            def link(ins):
                chain[0] += 1
                ins.then_inc(chain_a, 1)
                act.wait_ge(chain_a, chain[0])

            for src, r0, k in ROWS0:
                act.dma_start(rows0[r0:r0 + k, :], src).then_inc(params_loaded, 16)
            act.dma_start(rows1[0:CMP_BLOCK, :], io["cmp_pos_k"][0]).then_inc(params_loaded, 16)
            act.dma_start(rows1[CMP_BLOCK:, :], io["cmp_pos_v"][0]).then_inc(params_loaded, 16)
            act.dma_start(conv_rows[:, :], io["conv_w_2"][0]).then_inc(params_loaded, 16)
            act.dma_start(forget_bias[:, :], io["fox_forget_bias"][0].partition_broadcast(P)).then_inc(
                params_loaded, 16)

            def stats(i, src, n_sq):
                for q in range(4):
                    act.activation(MISC[0][:, :], src[:, 0, q * CW:(q + 1) * CW], ACT.Square,
                                   accum_out=sq_sum[:, i, 0, q:q + 1]).then_inc(ss_act, 1)
                    act.wait_ge(ss_act, 4 * i + q + 1)
                act.wait_ge(ms_ready, i + 1)
                act.activation(std[:, i, :], mean_sq[:, i, :], ACT.Sqrt, bias=consts[:, 0:1],
                               scale=1.0 / D).then_inc(std_ready, 1)

            def norm(n):
                for j in range(NU):
                    i = n * NU + j
                    act.wait_ge(full_ready, i + 1)
                    act.activation(act_hi[:, KPU * j:KPU * j + KPU, :].rearrange("p k t -> p (k t)"),
                                   zsb[:, i % 2, :], ACT.Copy).then_inc(act_hi_done, 1)

            def pre(prev, C, r):
                if prev is None:
                    return
                A_, free = acc(C - 1), acc_free[(C - 1) % 2]
                kind = prev[0]
                if kind == "gate":
                    q = prev[1]
                    if q >= 1:
                        act.wait_ge(h_ready, at(2 * q, r, 2))
                    for t in range(TT):
                        ins = act.activation(ysb[:, t, :], A_[t][:, :], ACT.Silu).then_inc(sig_ready, 1)
                elif kind == "value":
                    for t in range(TT):
                        ins = act.activation(vals[prev[1]][:, t, prev[2]:prev[2] + HPC, :].rearrange("p h d -> p (h d)"),
                                             A_[t][:, :], ACT.Copy)
                        if t == TT - 1:
                            ins.then_inc(free, 1)
                elif kind == "keep_a":
                    if prev[1] >= 1:
                        act.wait_ge(glu_ready, 2 * prev[1])
                    for t in range(TT):
                        ins = act.activation(a_keep[:, t, :], A_[t][:, :], ACT.Copy)
                        if t == TT - 1:
                            ins.then_inc(free, 1)
                elif kind == "glu":
                    for t in range(TT):
                        act.activation(zsb[:, t, :], A_[t][:, :], ACT.Sigmoid).then_inc(glu_sig, 1)
                elif kind == "plain":
                    i = TURNS.index(prev)
                    if i >= 1:
                        act.wait_ge(turned, i)
                    for t in range(TT):
                        ins = act.activation(ysb[:, t, :], A_[t][:, :], ACT.Copy)
                        if t == TT - 1:
                            ins.then_inc(free, 1)
                elif kind in ("normed", "kv"):
                    k = HPC if kind == "normed" else NSA_G
                    m = NORMED.index(prev)
                    for t in range(TT):
                        if kind == "kv":
                            act.activation(vals["vs" if prev[1] == "ks" else "vw"][:, t, :, :].rearrange(
                                "p h d -> p (h d)"), A_[t][:, NSA_G * HD:], ACT.Copy)
                        for h in range(k):
                            link(act.activation(zsb[:, t, h * HD:(h + 1) * HD], A_[t][:, h * HD:(h + 1) * HD],
                                                ACT.Square, accum_out=head_ss[:, t * HPC + h:t * HPC + h + 1]))
                    if m >= 1:
                        act.wait_ge(head_sq, m)
                    act.activation(head_std[:, :], head_ss[:, :], ACT.Sqrt, bias=consts[:, 0:1],
                                   scale=1.0 / HD).then_inc(head_std_ready, 1)

            def post(prev, C, r):
                if prev is None or prev[0] in ("value", "keep_a", "add", "gate"):
                    return
                if prev[0] == "up":
                    q = prev[1]
                    k0 = at(prev[2], r, 4)
                    for t in range(TT):
                        act.wait_ge(h_turned, at(2 * q + t + 1, r, 2))
                        act.activation(mid_hi[:, bass.ds(k0, 4), t * P:(t + 1) * P],
                                       TURN[t][:, :].rearrange("p (k t) -> p k t", t=P), ACT.Copy).then_inc(
                            mid_hi_done, 1)
                    return
                i = TURNS.index(prev)
                act.wait_ge(turned, i + 1)
                keep(act, prev, 0, lambda o, s, g: act.activation(o, s, ACT.Copy, scale=g), turn_out_a)

            def split(c, r):
                for u in range(c["nu"]):
                    R, U = c["R"] + u, c["U"] + u
                    act.wait_ge(raw_loaded[R % RAW_SLOTS], at(16 * (R // RAW_SLOTS + 1), r, 16 * 2 * c["nu"] // 4))
                    if U >= SPLIT_SLOTS:
                        act.wait_ge(parts_used, at(U - SPLIT_SLOTS + 1, r, 2 * c["nu"]))
                    act.activation(w_hi[:, U % SPLIT_SLOTS].rearrange("p k n -> p (k n)"),
                                   raw[:, R % RAW_SLOTS].rearrange("p k n -> p (k n)"), ACT.Copy).then_inc(hi_done, 1)
                    if u == 3:
                        pre(c["prev"], c["C"], r)
                post(c["prev"], c["C"], r)

            def finish(prev, C):
                act.wait_ge(parts_used, C)
                return prev

            def attend(j0, j1, cost, prob, probT, row_min, row_sum):
                for i in range(j0, j1 + 2):
                    if i < j1:
                        for t, c0, n in ((0, 0, P), (1, P, T)):
                            act.wait_ge(reduced, 2 * i + t + 1)
                            if i - j0 >= 2:
                                act.wait_ge(p_turned, i - 1)
                            act.activation(prob[:, i % 2, c0:c0 + n], cost[:, i % 2, c0:c0 + n], ACT.Exp,
                                           bias=row_min[:, i % 2, t:t + 1], scale=-1.0,
                                           accum_out=row_sum[:, i % 2, t:t + 1]).then_inc(exped, 1)
                    if j0 < i <= j1:
                        j = i - 1
                        act.wait_ge(p_turned, j + 1)
                        if j - j0 >= 2:
                            act.wait_ge(pv_done, j - 1)
                        act.activation(probT[:, j % 2, :], bank[2 + j % 2][:, 0:TAB], ACT.Copy).then_inc(p_out, 1)
                    if i >= j0 + 2 and JOBS[i - 2]["last"]:
                        b = JOBS[i - 2]
                        act.wait_ge(pv_done, i - 1)
                        act.activation(mid_hi[:, b["chunk"], :], bank[4 + b["o"] % 2][:, 0:T], ACT.Copy).then_inc(
                            o_hi, 1)

            act.wait_ge(tables_made, 1)
            act.wait_ge(x_loaded, 16 * TT)
            act.wait_ge(cols_ready, 2)
            stats(0, x_res, 0)
            act.activation(c_act[:, :], cols[:, 64:64 + KD], ACT.Silu).then_inc(c_ready, 1)
            act.wait_ge(small_loaded, 32)
            act.activation(ws_hi[:, :, :], w_small[:, :, :], ACT.Copy).then_inc(ws_split_hi, 1)
            norm(0)
            run(S_IN1, act, split)
            act.wait_ge(parts_used, LAST_U["in1"])
            pre(LAST1, C_IN1, None)
            post(LAST1, C_IN1, None)
            act.wait_ge(lf_d, 1)
            link(act.activation(lf[:, 2], lf[:, 1], ACT.Exp, scale=-1.0))
            act.activation(lf[:, 3], lf[:, 2], ACT.Ln, bias=consts[:, 2:3]).then_inc(lf_a, 1)
            act.activation(gate_e[:, :, :], small[:, :, FOX_H:], ACT.Exp, scale=-1.0).then_inc(gate_exp, 1)
            act.wait_ge(dec_zero, 1)
            act.wait_ge(lf_cum, 1)
            for q in range(FOX_H // 2):
                ins = act.activation(dec_l[0:1, 2 * q:2 * q + 2, :].rearrange("p h t -> p (h t)"), bank[q][0:1, :],
                                     ACT.Copy)
            ins.then_inc(dec_a, 1)
            act.wait_ge(cmp_used, 4)
            link(act.activation(kcn[:, :], MISC[0][0:64, 0:HD], ACT.Square, accum_out=kc_ss[:, 0:1]))
            act.activation(kc_ss[:, 1:2], kc_ss[:, 0:1], ACT.Sqrt, bias=consts[0:64, 0:1],
                           scale=1.0 / HD).then_inc(kc_std, 1)
            act.wait_ge(cmp_shift, 1)
            act.activation(cmp_prob[:, :, :], cmp_cost[:, :, :], ACT.Exp, scale=-1.0).then_inc(cmp_exp, 1)
            act.wait_ge(cmp_pT, 1)
            act.activation(cmp_probT[:, :, :].rearrange("p h t -> p (h t)"), MISC[0][:, :], ACT.Copy).then_inc(
                cmp_pT_out, 1)
            attend(0, N_JOB1, cost1, prob1, probT1, row_min1, row_sum1)
            run(S_OUT1, act, split)
            wait_read(act, LAST_C["out1"] - 1)
            stats(1, x_res, 1)
            norm(1)
            run(S_FFN1, act, split)
            wait_read(act, LAST_C["ffn1"] - 1)
            stats(2, x_res, 2)
            norm(2)
            run(S_IN2, act, split)
            act.wait_ge(parts_used, LAST_U["in2"])
            pre(LAST2, LAST_C["in2"], None)
            post(LAST2, LAST_C["in2"], None)
            attend(N_JOB1, len(JOBS), cost2, prob2, probT2, row_min2, row_sum2)
            act.wait_ge(ln_d, 1)
            act.activation(conv_sq[:, :, :], convT[:, :, :], ACT.Square).then_inc(ln_sq, 1)
            act.wait_ge(ln_var, 1)
            act.activation(conv_rs[:, :], MISC[1][:, 0:T], ACT.Sqrt, bias=consts[:, 1:2],
                           scale=1.0 / CONV_CH).then_inc(ln_std, 1)
            act.wait_ge(ln_y, 1)
            for g in range(CONV_G):
                link(act.activation(convT[:, g, :], convT[:, g, :], ACT.Silu, bias=cols[:, 102 + g:103 + g],
                                    scale=cols[:, 94 + g:95 + g]))
            act.activation(mid_hi[:, CONV_G:, :], convT[:, :, :], ACT.Copy).then_inc(ln_hi, 1)
            run(S_OUT2, act, split)
            wait_read(act, LAST_C["out2"] - 1)
            stats(3, y_acc, 3)
            act.wait_ge(x_updated, 4)
            stats(4, x_res, 4)
            norm(3)
            run(S_FFN2, act, split)
            wait_read(act, LAST_C["ffn2"] - 1)
            stats(5, y_acc, 5)

        @block.vector
        def _(dve):
            chain = [0]

            def link(ins):
                chain[0] += 1
                ins.then_inc(chain_d, 1)
                dve.wait_ge(chain_d, chain[0])

            def stats(i, src):
                for q in range(4):
                    link(dve.tensor_tensor_reduce(TURN[0][:, :], src[:, 1, q * CW:(q + 1) * CW],
                                                  src[:, 1, q * CW:(q + 1) * CW], 1.0, 0.0, ALU.mult, ALU.add,
                                                  sq_sum[:, i, 1, q:q + 1]))
                dve.wait_ge(ss_act, 4 * (i + 1))
                dve.tensor_reduce(mean_sq[:, i, :], sq_sum[:, i, :, :], AX.X, ALU.add).then_inc(ms_ready, 1)
                dve.wait_ge(std_ready, i + 1)
                dve.reciprocal(rstd[:, i, :], std[:, i, :]).then_inc(rstd_ready, 1)
                dve.wait_ge(rstd_ready, i + 1)

            def norm(n, i_stat):
                for j in range(NU):
                    i = n * NU + j

                    def rows(i, j):
                        if i >= 2:
                            dve.wait_ge(xn_turned, i - 1)
                        for t in range(TT):
                            ins = dve.tensor_scalar(ysb[:, i % 2, t * KPU * P:(t + 1) * KPU * P],
                                                    x_res[:, t, j * KPU * P:(j + 1) * KPU * P],
                                                    rstd[:, i_stat, t:t + 1], None, ALU.mult)
                        ins.then_inc(xn_ready, 1)

                    if j == 0:
                        rows(i, 0)
                    if j + 1 < NU:
                        rows(i + 1, j + 1)
                    dve.wait_ge(xn_turned, i + 1)
                    if i >= 2:
                        dve.wait_ge(act_hi_done, i - 1)
                        dve.wait_ge(act_lo_done, i - 1)
                    for c in range(KPU):
                        k = KPU * j + c
                        o, s = zsb[:, i % 2, c * T:(c + 1) * T], TURN[i % 2][:, c * T:(c + 1) * T]
                        if n < 2:
                            ins = dve.tensor_scalar(o, s, norm_scale[:, n, k:k + 1], None, ALU.mult)
                        else:
                            ins = dve.tensor_scalar(o, s, norm_scale[:, n, k:k + 1], norm_shift[:, n, k:k + 1],
                                                    ALU.mult, ALU.add)
                    ins.then_inc(full_ready, 1)
                    if j >= 1:
                        low(i - 1, j - 1)
                low(n * NU + NU - 1, NU - 1)

            def low(i, j):
                dve.wait_ge(full_ready, i + 1)
                dve.wait_ge(act_hi_done, i + 1)
                dve.tensor_tensor(act_lo[:, KPU * j:KPU * j + KPU, :].rearrange("p k t -> p (k t)"), zsb[:, i % 2, :],
                                  act_hi[:, KPU * j:KPU * j + KPU, :].bitcast(F32).rearrange("p k t -> p (k t)"),
                                  ALU.subtract).then_inc(act_lo_done, 1)

            def pre(prev, C, r):
                if prev is None:
                    return
                A_, free = acc(C - 1), acc_free[(C - 1) % 2]
                kind = prev[0]
                if kind == "up":
                    q = prev[1]
                    dve.wait_ge(sig_ready, at(2 * q + 2, r, 2))
                    if q >= 1:
                        dve.wait_ge(h_turned, at(2 * q, r, 2))
                    for t in range(TT):
                        dve.tensor_tensor(zsb[:, t, :], A_[t][:, :], ysb[:, t, :], ALU.mult).then_inc(h_ready, 1)
                    return
                if kind == "add":
                    _, dst, n, fresh = prev
                    d = x_res if dst == "x" else y_acc
                    for t in range(TT):
                        o = d[:, t, n * CW:(n + 1) * CW]
                        if fresh:
                            ins = dve.tensor_copy(o, A_[t][:, :])
                        else:
                            ins = dve.tensor_tensor(o, A_[t][:, :], o, ALU.add)
                        if t == TT - 1:
                            ins.then_inc(free, 1)
                    return
                if kind in ("normed", "kv"):
                    k = HPC if kind == "normed" else NSA_G
                    m, i = NORMED.index(prev), TURNS.index(prev)
                    dve.wait_ge(head_std_ready, m + 1)
                    dve.reciprocal(head_rstd[:, :], head_std[:, :]).then_inc(head_sq, 1)
                    dve.wait_ge(head_sq, m + 1)
                    if i >= 1:
                        dve.wait_ge(turned, i)
                    for t in range(TT):
                        ins = dve.tensor_tensor(
                            ysb[:, t, 0:k * HD].rearrange("p (h d) -> p h d", d=HD),
                            A_[t][:, 0:k * HD].rearrange("p (h d) -> p h d", d=HD),
                            head_rstd[:, t * HPC:t * HPC + k].unsqueeze(2).to_broadcast([P, k, HD]), ALU.mult)
                        if t == TT - 1:
                            ins.then_inc(free, 1)
                elif kind == "glu":
                    i = TURNS.index(prev)
                    dve.wait_ge(turned, i)
                    for t in range(TT):
                        dve.wait_ge(glu_sig, 2 * prev[1] + t + 1)
                        dve.tensor_tensor(ysb[:, t, :], zsb[:, t, :], a_keep[:, t, :], ALU.mult).then_inc(glu_ready, 1)

            def post(prev, C, r):
                if prev is None or prev[0] in ("value", "keep_a", "add", "gate"):
                    return
                if prev[0] == "up":
                    q = prev[1]
                    k0 = at(prev[2], r, 4)
                    for t in range(TT):
                        dve.wait_ge(mid_hi_done, at(2 * q + t + 1, r, 2))
                        dve.tensor_tensor(mid_lo[:, bass.ds(k0, 4), t * P:(t + 1) * P],
                                          TURN[t][:, :].rearrange("p (k t) -> p k t", t=P),
                                          mid_hi[:, bass.ds(k0, 4), t * P:(t + 1) * P].bitcast(F32),
                                          ALU.subtract).then_inc(mid_lo_done, 1)
                    return
                dve.wait_ge(turned, TURNS.index(prev) + 1)
                keep(dve, prev, 1, lambda o, s, g: dve.tensor_scalar(o, s, g, None, ALU.mult), turn_out_d)

            conv_n = [0]

            def conv_step(k, g):
                if conv_n[0] >= CONV_DVE_G:
                    dve.wait_ge(conv_dve, conv_n[0] - CONV_DVE_G + 1)
                if conv_n[0] == 0:
                    dve.wait_ge(turn_out_a, len([c for c in TURNS if c[1] not in ("mq", "mk")]))
                src, wk = uT[:, g, k:k + T], conv_w_cols[:, g, k:k + 1]
                if k == 0:
                    ins = dve.tensor_scalar(convT[:, g, :], src, wk, cols[:, 86 + g:87 + g], ALU.mult, ALU.add)
                else:
                    ins = dve.scalar_tensor_tensor(convT[:, g, :], src, wk, convT[:, g, :], ALU.mult, ALU.add)
                ins.then_inc(conv_dve, 1)
                conv_n[0] += 1

            def ada_step(c, r, i):
                a = c["ada"]
                unit = a["A"] + i
                dve.wait_ge(ada_loaded[unit % 2], at(16 * (unit // 2 + 1), r, 64))
                for kk in range(KPU):
                    k = a["half"] * 8 + 2 * i + kk
                    w = ada_raw[:, unit % 2, kk, :]
                    cc = c_act[:, k:k + 1]
                    if k == 0:
                        if a["blk"] >= 1:
                            dve.wait_ge(ada_summed, at(a["blk"], r, 1))
                        ins = dve.tensor_scalar(ada_acc[:, :], w, cc, None, ALU.mult)
                    else:
                        dve.wait_ge(ada_used, at(2 * unit + kk, r, 16))
                        ins = dve.scalar_tensor_tensor(ada_acc[:, :], w, cc, ada_acc[:, :], ALU.mult, ALU.add)
                    ins.then_inc(ada_used, 1)

            def ada_keep(c, r):
                a = c["ada"]
                dve.wait_ge(ada_summed, at(a["blk"] + 1, r, 1))
                if a["kind"] == "col":
                    j0 = a["dst"]
                    dve.tensor_copy(mod_cols[:, bass.ds(at(j0, r, 4), 4)], MISC[0][:, 0:4]).then_inc(ada_out, 1)
                else:
                    row = gate_row1 if a["kind"] == "row" else gate_row2
                    o = row[:, bass.ds(at(a["dst"], r, CW), CW)]
                    dve.tensor_tensor(o, MISC[0][:, :], o, ALU.mult).then_inc(ada_out, 1)

            def split(c, r):
                nu = c["nu"]
                conv = list(c.get("conv", []))
                for u in range(nu):
                    R, U = c["R"] + u, c["U"] + u
                    dve.wait_ge(hi_done, at(U + 1, r, 2 * nu))
                    if U >= SPLIT_SLOTS:
                        dve.wait_ge(parts_used, at(U - SPLIT_SLOTS + 1, r, 2 * nu))
                    dve.tensor_tensor(w_lo[:, U % SPLIT_SLOTS].rearrange("p k n -> p (k n)"),
                                      raw[:, R % RAW_SLOTS].rearrange("p k n -> p (k n)"),
                                      w_hi[:, U % SPLIT_SLOTS].bitcast(F32).rearrange("p k n -> p (k n)"),
                                      ALU.subtract).then_inc(lo_done, 1)
                    for _ in range(-(-len(conv) // (nu - u))):
                        conv_step(*conv.pop(0))
                    if c["ada"] and u in (1, 2, 5, 6):
                        ada_step(c, r, (1, 2, 5, 6).index(u))
                    if u == 3:
                        pre(c["prev"], c["C"], r)
                if c["ada"] and nu < 7:
                    ada_step(c, r, 3)
                post(c["prev"], c["C"], r)
                if c["ada"] and c["ada"]["half"] == 1:
                    ada_keep(c, r)

            def attend(j0, j1, cost, prob, row_min, row_sum, row_inv):
                for i in range(j0, j1 + 2):
                    if i < j1:
                        b = JOBS[i]
                        tab = {"mask": lambda: mask[:, :], "mask2": lambda: mask2[:, :],
                               "alibi": lambda: alibi[:, b["h"], :]}[b["table"]]()
                        dve.wait_ge(scored, i + 1)
                        if i - j0 >= 2:
                            dve.wait_ge(exped, 2 * (i - 1))
                        for t, c0, n in ((0, 0, P), (1, P, T)):
                            dve.tensor_tensor_reduce(cost[:, i % 2, c0:c0 + n], bank[i % 2][:, c0:c0 + n],
                                                     tab[:, T - n:T], 1.0, 3.0e38, ALU.add, ALU.min,
                                                     row_min[:, i % 2, t:t + 1]).then_inc(reduced, 1)
                    if j0 < i <= j1:
                        j = i - 1
                        b = JOBS[j]
                        dve.wait_ge(exped, 2 * j + 2)
                        link(dve.reciprocal(row_inv[:, j % 2, :], row_sum[:, j % 2, :]))
                        if b["gate"] is not None:
                            link(dve.tensor_tensor(row_inv[:, j % 2, :], row_inv[:, j % 2, :],
                                                   gates[:, :, b["gate"]], ALU.mult))
                        for t, c0, n in ((0, 0, P), (1, P, T)):
                            dve.tensor_scalar(prob[:, j % 2, c0:c0 + n], prob[:, j % 2, c0:c0 + n],
                                              row_inv[:, j % 2, t:t + 1], None, ALU.mult).then_inc(scaled, 1)
                    if i >= j0 + 2 and JOBS[i - 2]["last"]:
                        b = JOBS[i - 2]
                        dve.wait_ge(o_hi, b["o"] + 1)
                        dve.tensor_tensor(mid_lo[:, b["chunk"], :], bank[4 + b["o"] % 2][:, 0:T],
                                          mid_hi[:, b["chunk"], :].bitcast(F32), ALU.subtract).then_inc(o_lo, 1)

            def gated_add(i_stat, row, base):
                for t in range(TT):
                    for h in range(2):
                        s = slice(h * D // 2, (h + 1) * D // 2)
                        link(dve.scalar_tensor_tensor(y_acc[:, t, s], y_acc[:, t, s], rstd[:, i_stat, t:t + 1],
                                                      row[:, s], ALU.mult, ALU.mult))
                        ins = dve.tensor_tensor(x_res[:, t, s], x_res[:, t, s], y_acc[:, t, s], ALU.add)
                        ins.then_inc(x_updated, 1)
                        dve.wait_ge(x_updated, base + 2 * t + h + 1)

            dve.wait_ge(cols_turned, 1)
            dve.tensor_copy(cols[:, 0:110], MISC[0][:, 0:110]).then_inc(cols_ready, 1)
            dve.tensor_copy(pos_cols[:, :], MISC[0][:, 128:192])
            dve.tensor_copy(conv_w_cols[:, :, 0:CONV_K],
                            MISC[1][:, 0:32 * CONV_G].rearrange("p (g k) -> p g k", k=32)[:, :, 0:CONV_K]).then_inc(
                cols_ready, 1)
            dve.wait_ge(cols_ready, 2)
            dve.tensor_scalar(q_gain[:, 0:1], cols[:, 80:81], -SCALE, None, ALU.mult)
            dve.tensor_scalar(q_gain[:, 1:2], cols[:, 82:83], -SCALE, None, ALU.mult)
            link(dve.tensor_copy(norm_scale[:, 0:2, :].rearrange("p n k -> p (n k)"), cols[:, 0:2 * KD]))
            dve.wait_ge(tables_made, 1)
            dve.wait_ge(x_loaded, 16 * TT)
            stats(0, x_res)
            dve.wait_ge(ws_split_hi, 1)
            dve.tensor_tensor(ws_lo[:, :, :], w_small[:, :, :], ws_hi[:, :, :].bitcast(F32), ALU.subtract).then_inc(
                ws_split, 1)
            norm(0, 0)
            run(S_IN1, dve, split)
            pre(LAST1, C_IN1, None)
            post(LAST1, C_IN1, None)
            dve.wait_ge(small_mm, 1)
            dve.tensor_copy(small[:, :, :].rearrange("p t n -> p (t n)"), MISC[0][:, 0:TT * N_SMALL]).then_inc(
                small_out, 1)
            dve.wait_ge(small_out, 1)
            link(dve.tensor_tensor(lf[:, 0], small[:, :, 0:FOX_H],
                                   forget_bias[:, :].unsqueeze(1).to_broadcast([P, TT, FOX_H]), ALU.add))
            dve.scalar_tensor_tensor(lf[:, 1], lf[:, 0], -1.0, lf[:, 0], ALU.mult, ALU.max).then_inc(lf_d, 1)
            link(dve.tensor_scalar(lf[:, 4], lf[:, 0], 0.0, None, ALU.min))
            dve.wait_ge(lf_a, 1)
            link(dve.tensor_tensor(lf[:, 5], lf[:, 4], lf[:, 3], ALU.subtract))
            dve.wait_ge(tables_made, 2)
            dve.wait_ge(blk_zero, 1)
            dve.tensor_scalar(lf_cols[:, :, :, 0], lf[:, 5], -1.0, None, ALU.mult)
            dve.tensor_copy(lf_cols[:, :, :, 32], lf[:, 5]).then_inc(lf_d, 1)
            for kind, (blk, src) in enumerate(((blk_k, "kc"), (blk_v, "vc"))):
                dve.wait_ge(blk_zero, kind + 2)
                for g in range(NSA_G):
                    for j in range(2):
                        tok = heads[src][:, g, CMP_STRIDE * j:CMP_STRIDE * (j + N_CMP)].rearrange(
                            "p (n l) -> p l n", l=CMP_STRIDE)
                        pc = pos_cols[:, kind * CMP_BLOCK + 16 * j:kind * CMP_BLOCK + 16 * j + 16]
                        ins = dve.tensor_tensor(blk[:, 16 * j:16 * j + 16, 32 * g:32 * g + N_CMP], tok,
                                                pc.unsqueeze(2).to_broadcast([P, 16, N_CMP]), ALU.add)
                ins.then_inc(blk_ready, 1)
            dve.wait_ge(gate_exp, 1)
            link(dve.tensor_scalar(gate_e[:, :, :], gate_e[:, :, :], 1.0, None, ALU.add))
            dve.reciprocal(gates[:, :, :], gate_e[:, :, :]).then_inc(gates_ready, 1)
            dve.wait_ge(dec_zero, 1)
            dve.wait_ge(lf_cum, 1)
            for q in range(FOX_H // 2):
                ins = dve.tensor_copy(dec_r[32:33, 2 * q:2 * q + 2, :].rearrange("p h t -> p (h t)"),
                                      bank[q][32:33, :])
            ins.then_inc(dec_d, 1)
            dve.wait_ge(kc_std, 1)
            link(dve.reciprocal(kc_ss[:, 2:3], kc_ss[:, 1:2]))
            dve.tensor_scalar(kcn[:, :], MISC[0][0:64, 0:HD], kc_ss[:, 2:3], None, ALU.mult).then_inc(kc_n, 1)
            dve.wait_ge(cmp_used, 8)
            for q in range(4):
                for g in range(NSA_G):
                    ins = dve.tensor_copy(vcmp[32 * q:32 * q + 16, g, :], MISC[1][32 * g:32 * g + 16, 0:HD])
            ins.then_inc(vc_ready, 1)
            dve.wait_ge(kc_turned, 1)
            dve.tensor_scalar(kcmpT[:, :], TURN[0][:, 0:64], cols[:, 83:84], None, ALU.mult).then_inc(kc_ready, 1)
            dve.wait_ge(cmp_scored, 1)
            link(dve.tensor_tensor(cmp_cost[:, :, :].rearrange("p h n -> p (h n)"), MISC[1][:, :],
                                   cmp_tab[:, :, :, :].rearrange("p t h n -> p (t h n)"), ALU.add))
            link(dve.tensor_reduce(cmp_min[:, :], cmp_cost[:, :, :], AX.X, ALU.min))
            dve.tensor_tensor(cmp_cost[:, :, :], cmp_cost[:, :, :],
                              cmp_min[:, :].unsqueeze(2).to_broadcast([P, TT * NSA_H, 32]),
                              ALU.subtract).then_inc(cmp_shift, 1)
            dve.wait_ge(cmp_exp, 1)
            probs4 = cmp_prob[:, :, :].rearrange("p (t h) n -> p t h n", t=TT)
            link(dve.tensor_tensor(probs4, probs4, cmp_ok[:, :, :].unsqueeze(2).to_broadcast([P, TT, NSA_H, 32]),
                                   ALU.mult))
            link(dve.tensor_reduce(cmp_sum[:, :], cmp_prob[:, :, :], AX.X, ALU.add))
            link(dve.tensor_scalar(cmp_sum[:, :], cmp_sum[:, :], 1e-30, None, ALU.max))
            link(dve.reciprocal(cmp_min[:, :], cmp_sum[:, :]))
            dve.wait_ge(gates_ready, 1)
            link(dve.tensor_tensor(cmp_min[:, :].rearrange("p (t h) -> p t h", t=TT),
                                   cmp_min[:, :].rearrange("p (t h) -> p t h", t=TT),
                                   gates[:, :, :].rearrange("p t (h b) -> p t h b", b=3)[:, :, :, 0], ALU.mult))
            dve.tensor_tensor(cmp_prob[:, :, :], cmp_prob[:, :, :],
                              cmp_min[:, :].unsqueeze(2).to_broadcast([P, TT * NSA_H, 32]),
                              ALU.mult).then_inc(cmp_p, 1)
            attend(0, N_JOB1, cost1, prob1, row_min1, row_sum1, row_inv1)
            dve.wait_ge(gate_loaded, 16)
            dve.wait_ge(c_ready, 1)
            run(S_OUT1, dve, split)

            def last_add(prev, C, U):
                dve.wait_ge(parts_used, U)
                pre(prev, C, None)
                wait_read(dve, C - 1)

            last_add(LAST_OUT1, LAST_C["out1"], S_OUT1[-1]["U"] + NU)
            stats(1, x_res)
            norm(1, 1)
            run(S_FFN1, dve, split)
            last_add(LAST_FFN1, LAST_C["ffn1"], S_FFN1[-1]["U"] + S_FFN1[-1]["nu"])
            stats(2, x_res)
            dve.wait_ge(ada_out, 16)
            for i in range(2):
                sh, sc = 2 * i * KD, (2 * i + 1) * KD
                dve.tensor_copy(norm_shift[:, 2 + i, :], mod_cols[:, sh:sh + KD])
                link(dve.scalar_tensor_tensor(norm_scale[:, 2 + i, :], mod_cols[:, sc:sc + KD], 1.0,
                                              cols[:, (2 + i) * KD:(3 + i) * KD], ALU.add, ALU.mult))
            norm(2, 2)
            dve.wait_ge(uT_zero, 1)
            run(S_IN2, dve, split)
            dve.wait_ge(parts_used, LAST_U["in2"])
            pre(LAST2, LAST_C["in2"], None)
            post(LAST2, LAST_C["in2"], None)
            attend(N_JOB1, len(JOBS), cost2, prob2, row_min2, row_sum2, row_inv2)
            dve.wait_ge(ln_sum, 1)
            link(dve.tensor_scalar(conv_mu[:, :], MISC[0][:, 0:T], 1.0 / CONV_CH, None, ALU.mult))
            dve.tensor_tensor(convT[:, :, :], convT[:, :, :],
                              conv_mu[:, :].unsqueeze(1).to_broadcast([P, CONV_G, T]), ALU.subtract).then_inc(ln_d, 1)
            dve.wait_ge(ln_std, 1)
            link(dve.reciprocal(conv_rs[:, :], conv_rs[:, :]))
            dve.tensor_tensor(convT[:, :, :], convT[:, :, :],
                              conv_rs[:, :].unsqueeze(1).to_broadcast([P, CONV_G, T]), ALU.mult).then_inc(ln_y, 1)
            dve.wait_ge(ln_hi, 1)
            dve.tensor_tensor(mid_lo[:, CONV_G:, :], convT[:, :, :], mid_hi[:, CONV_G:, :].bitcast(F32),
                              ALU.subtract).then_inc(ln_lo, 1)
            dve.wait_ge(ln_lo, 1)
            run(S_OUT2, dve, split)
            last_add(LAST_OUT2, LAST_C["out2"], LAST_U["out2"])
            stats(3, y_acc)
            gated_add(3, gate_row1, 0)
            stats(4, x_res)
            norm(3, 4)
            dve.wait_ge(gate_loaded, 32)
            run(S_FFN2, dve, split)
            last_add(LAST_FFN2, LAST_C["ffn2"], S_FFN2[-1]["U"] + S_FFN2[-1]["nu"])
            stats(5, y_acc)
            gated_add(5, gate_row2, 4)


INPUTS = ["x", "attn_norm", "w_in", "fox_forget_bias", "fox_q_norm", "fox_k_norm", "nsa_q_norm", "cmp_k_norm",
          "slc_k_norm", "win_k_norm", "cmp_pos_k", "cmp_pos_v", "cmp_w_k", "cmp_w_v", "w_out", "ffn_norm",
          "w_gate", "w_up", "w_down", "c_2", "ada_w_2", "ada_b_2", "mix_pre_g_2", "mix_post_g_2", "w_in_2",
          "conv_w_2", "conv_b_2", "conv_ln_g_2", "conv_ln_b_2", "w_out_2", "ffn_pre_g_2", "ffn_post_g_2",
          "w_gate_2", "w_up_2", "w_down_2"]


def kernel(**inputs):
    import numpy as np
    import concourse.bacc as bacc
    from concourse import mybir
    from concourse.bass_utils import run_bass_kernel_spmd

    nc = bacc.Bacc("TRN2", target_bir_lowering=False, num_devices=1)
    arrays, io = {}, {}
    for name in INPUTS:
        a = np.ascontiguousarray(inputs[name])
        arrays[f"in_{name}"] = a
        io[name] = nc.dram_tensor(f"in_{name}", a.shape, mybir.dt.from_np(a.dtype), kind="ExternalInput").ap()
    shape = inputs["x"].shape
    out = nc.dram_tensor("out_x", shape, mybir.dt.float32, kind="ExternalOutput").ap()
    build_two_blocks(nc, io, out)
    r = run_bass_kernel_spmd(nc, [arrays], core_ids=[0])
    return r.results[0]["out_x"]
```

```python
def build_two_blocks(nc, io, out):
    import concourse.bass as bass
    from concourse import mybir
    from contextlib import ExitStack

    F32, F32R = mybir.dt.float32, mybir.dt.float32r
    ACT = mybir.ActivationFunctionType
    ALU = mybir.AluOpType
    AX = mybir.AxisListType
    P = 128

    T, D = io["x"].shape[1], io["x"].shape[2]
    TT = T // P
    KD = D // P
    FF = io["w_gate"].shape[2]
    HD = io["fox_q_norm"].shape[1]
    FOX_H = io["fox_forget_bias"].shape[1]
    NSA_H, NSA_G = 8, 2
    HPG = NSA_H // NSA_G
    CW = 512
    HPC = CW // HD
    KPU = 2
    NU = KD // KPU
    RAW_SLOTS, SPLIT_SLOTS = 4, 4
    SCALE = HD ** -0.5
    CMP_STRIDE, CMP_BLOCK = 16, io["cmp_pos_k"].shape[1]
    N_CMP = T // CMP_STRIDE - 1
    CONV_K, CONV_CH = io["conv_w_2"].shape[1], io["conv_w_2"].shape[2]
    CONV_G = CONV_CH // P
    BIG = 1e30
    TAB = T + P

    def wview(name):
        return io[name][0].rearrange("(k p) n -> p k n", p=P)

    W = {n: wview(n) for n in ("w_in", "w_out", "w_gate", "w_up", "w_down",
                               "w_in_2", "w_out_2", "w_gate_2", "w_up_2", "w_down_2", "ada_w_2")}

    def at(base, r, stride):
        return base if r is None else r * stride + base

    pos = {"C": 0, "U": 0, "R": 0, "A": 0}

    pending = []

    def chunk(w, n0, st, prev=None, k0=0, nu=NU, n_step=0, ada=None, **more):
        c = dict(w=w, n0=n0, n_step=n_step, st=st, prev=prev, k0=k0, nu=nu, C=pos["C"], U=pos["U"],
                 R=pos["R"], ada=None, keep=pending.pop() if pending else None, **more)
        if ada is not None and ada["half"] == 1:
            pending.append(dict(kind=ada["kind"], dst=ada["dst"], blk=ada["blk"]))
        if ada is not None:
            c["ada"] = dict(ada, A=pos["A"])
            pos["A"] += 4
        pos["C"] += 1
        pos["U"] += nu
        pos["R"] += nu
        return c

    o_ff = 3 * FOX_H * HD
    o_qn = o_ff + FOX_H
    o_kv = o_qn + NSA_H * HD
    o_gt = o_kv + 6 * NSA_G * HD
    N_SMALL = FOX_H + 3 * NSA_H
    IN1 = [(0, ("normed", "fq", 0)), (CW, ("normed", "fq", 4)), (2 * CW, ("normed", "fk", 0)),
           (3 * CW, ("normed", "fk", 4)), (4 * CW, ("value", "fv", 0)), (5 * CW, ("value", "fv", 4)),
           (o_qn, ("normed", "nq", 0)), (o_qn + CW, ("normed", "nq", 4)), (o_kv, ("plain", "kcvc", 0)),
           (o_kv + CW, ("kv", "ks", 0)), (o_kv + 2 * CW, ("kv", "kw", 0))]
    S_IN1 = []
    prev = None
    for n0, cons in IN1:
        S_IN1.append(chunk("w_in", n0, "act", prev))
        prev = cons
    LAST1 = prev
    SMALL_OUT = 5
    assert IN1[SMALL_OUT - 1][1][0] == IN1[SMALL_OUT][1][0] == "value"
    R_CMP = pos["R"]
    N_CMPU = 2 * 4
    pos["R"] += N_CMPU
    U_CMP = pos["U"]

    ada_blk = [0]

    def ada_pair(kind, col, dst, step=0, n=1):
        b = ada_blk[0]
        ada_blk[0] += n
        return [dict(kind=kind, col=col, dst=dst, blk=b, half=h, step=step) for h in range(2)]

    def out_pairs(w, dst, prev, ada, first):
        got = []
        for p in range(2):
            a = ada[p] or [None, None]
            for h in range(2):
                n = 2 * p + h
                got.append(chunk(w, n * CW, "mid", prev, ada=a[h], first=first if n == 0 else None))
                prev = ("add", dst, n, *(("sum", 1) if dst == "x" else ("gated_copy", 3)))
        return got, prev

    S_OUT1, prev = out_pairs("w_out", "x", None,
                             [ada_pair("row", 4 * CW * 2, 0), ada_pair("row", 4 * CW * 2 + CW, CW)], "mix1")
    LAST_OUT1 = prev
    KEEP_OUT1 = pending.pop()

    def ffn(tag, dst, ada_list, f):
        steps, prev, pair0 = [], None, f * (FF // CW)
        groups = [4, 4, 3]
        assert sum(groups) * CW == FF
        done = 0
        al = list(ada_list)
        for g, n in enumerate(groups):
            def pair(j, trips, prev):
                a = [None, None]
                if al:
                    blocks = [al.pop(0) for _ in range(min(trips, len(al)))]
                    assert len(blocks) == trips
                    st = blocks[1][1] - blocks[0][1] if trips > 1 else 0
                    assert all(blocks[q + 1][1] - blocks[q][1] == st and blocks[q + 1][0] == blocks[q][0]
                               for q in range(trips - 1))
                    a = ada_pair(blocks[0][0], blocks[0][1], blocks[0][2], st, trips)
                col = (done + j) * CW
                q = pair0 + done + j
                a1 = chunk("w_gate" + tag, col, "act", prev, n_step=CW, ada=a[0])
                a2 = chunk("w_up" + tag, col, "act", ("gate", q), n_step=CW, ada=a[1])
                if trips > 1:
                    for k, m in (("C", 2), ("U", 2 * NU), ("R", 2 * NU)):
                        pos[k] += m * (trips - 1)
                    if a[0]:
                        pos["A"] += 8 * (trips - 1)
                        pending[0]["blk"] += trips - 1
                        pending[0]["dst"] += (trips - 1) * (4 if a[0]["kind"] == "col" else CW)
                    else:
                        assert a1["keep"] is None
                return [a1, a2], ("up", q, 4 * j)
            body, nxt = pair(0, 1, prev)
            steps += body
            j = 1
            while j < n:
                trips = 1
                while j + trips < n and (not al or (len(al) > trips and al[trips][0] == al[0][0]
                                         and al[trips][1] - al[trips - 1][1] == CW)):
                    trips += 1
                if trips > 1:
                    body, _ = pair(j, trips, nxt)
                    steps.append(dict(loop=trips, body=body))
                else:
                    body, _ = pair(j, 1, nxt)
                    steps += body
                j += trips
                nxt = ("up", pair0 + done + j - 1, 4 * (j - 1))
            prev = nxt
            kc = 4 * n
            for p in range(2):
                a = [None, None]
                if al:
                    k_, c_, d_ = al.pop(0)
                    a = ada_pair(k_, c_, d_)
                for h in range(2):
                    m = 2 * p + h
                    steps.append(chunk("w_down" + tag, m * CW, "mid", prev, k0=4 * done, nu=kc // KPU, ada=a[h],
                                       pairs=pair0 + done + n, first="ffn" if m == 0 else None))
                    how = ("copy" if dst == "y" and g == 0 else "part", None)
                    if g == len(groups) - 1:
                        how = ("sum", 2) if dst == "x" else ("gated_sum", 5)
                    prev = ("add", dst, m, *how)
            done += n
        return steps, prev

    col_blocks = [("col", part * D + q * CW, (i * 4 + q) * 4) for i, part in enumerate((0, 1, 3, 4))
                  for q in range(4)]
    S_FFN1, LAST_FFN1 = ffn("", "x", col_blocks + [("row", 2 * D + 2 * CW, 2 * CW)], 0)

    KEEP_FFN1 = pending.pop()
    IN2 = [(3 * 1024, ("keep_a", 0)), (4 * 1024, ("glu", 0)), (3 * 1024 + CW, ("keep_a", 1)),
           (4 * 1024 + CW, ("glu", 1)),
           (0, ("plain", "mq", 0)), (CW, ("plain", "mq", 4)), (2 * CW, ("plain", "mk", 0)),
           (3 * CW, ("plain", "mk", 4)), (4 * CW, ("value", "mv", 0)), (5 * CW, ("value", "mv", 4))]
    S_IN2 = []
    prev = None
    CONV_POOL = [1, 2, 3]
    CONV_DVE = [g for g in range(CONV_G) if g not in CONV_POOL]
    CONV_A, CONV_B = 3, 5
    early = [(k, g) for k in range(CONV_K) for g in CONV_DVE if g < 4]
    late = [(k, g) for k in range(CONV_K) for g in CONV_DVE if g >= 4]
    for i, (n0, cons) in enumerate(IN2):
        cv = []
        if CONV_A <= i < CONV_B:
            per = -(-len(early) // (CONV_B - CONV_A))
            cv = early[(i - CONV_A) * per:(i - CONV_A + 1) * per]
        if i >= CONV_B:
            per = -(-len(late) // (len(IN2) - CONV_B))
            cv = late[(i - CONV_B) * per:(i - CONV_B + 1) * per]
        S_IN2.append(chunk("w_in_2", n0, "act", prev, conv=cv))
        prev = cons
    LAST2 = prev
    S_OUT2, LAST_OUT2 = out_pairs("w_out_2", "y", None, [ada_pair("row", 2 * D + 3 * CW, 3 * CW), None], "mix2")
    S_FFN2, LAST_FFN2 = ffn("_2", "y", [("row2", 5 * D + q * CW, q * CW) for q in range(4)], 1)
    C_IN1, C_IN2 = len(S_IN1), S_IN2[0]["C"]
    LAST_C = {"in1": C_IN1, "out1": S_OUT1[-1]["C"] + 1, "ffn1": S_FFN1[-1]["C"] + 1,
              "in2": S_IN2[-1]["C"] + 1, "out2": S_OUT2[-1]["C"] + 1, "ffn2": S_FFN2[-1]["C"] + 1}
    LAST_U = {"in1": U_CMP, "out2": S_OUT2[-1]["U"] + NU, "in2": S_IN2[-1]["U"] + NU}
    TURNS = [c for _, c in IN1 if c[0] != "value"] + [c for _, c in IN2 if c[0] not in ("value", "keep_a")]
    NORMED = [c for _, c in IN1 if c[0] in ("normed", "kv")]

    consumer_of = {}

    def note(steps, last):
        for s in steps:
            for trip in range(s.get("loop", 1)):
                for c in s.get("body", [s]):
                    p = c["prev"]
                    C = c["C"] + 2 * trip
                    if p:
                        consumer_of[C - 1] = (p[0], p[1] + trip) if p[0] in ("gate", "up") else p
        consumer_of[C] = last

    note(S_IN1, LAST1)
    note(S_OUT1, LAST_OUT1)
    note(S_FFN1, LAST_FFN1)
    note(S_IN2, LAST2)
    note(S_OUT2, LAST_OUT2)
    note(S_FFN2, LAST_FFN2)
    READ, n_free = {}, [0, 0]
    for C in range(len(consumer_of)):
        p = consumer_of[C]
        if p[0] in ("gate", "up", "glu"):
            READ[C] = (p[0], 2 * p[1] + 2)
        else:
            n_free[C % 2] += 1
            READ[C] = (("free", C % 2), n_free[C % 2])

    JOBS = []
    for h in range(FOX_H):
        JOBS.append(dict(q="fq", k="fk", v="fv", h=h, kv=h, o=h, chunk=h, first=True, last=True, gate=None,
                         table="mask", decay=True, cmp=False))
    for h in range(NSA_H):
        for b, (k, vv) in enumerate((("ks", "vs"), ("kw", "vw"))):
            JOBS.append(dict(q="nq", k=k, v=vv, h=h, kv=h // HPG, o=FOX_H + h, chunk=FOX_H + h, first=b == 0,
                             last=b == 1, gate=3 * h + 1 + b, table="alibi", decay=False, cmp=b == 1))
    N_JOB1, N_OUT_1 = len(JOBS), FOX_H + NSA_H
    for h in range(8):
        JOBS.append(dict(q="mq", k="mk", v="mv", h=h, kv=h, o=N_OUT_1 + h, chunk=h, first=True, last=True,
                         gate=None, table="mask2", decay=False, cmp=False))

    top = ExitStack()
    with top:
        def sb(name, shape, dt=F32, scope=None, side=None):
            kw = {"side": side} if side else {}
            return (scope or top).enter_context(nc.sbuf_tensor(name, shape, dt, **kw))

        def sem(name):
            return top.enter_context(nc.semaphore(name))

        x_res = sb("x_res", [P, TT, D])
        mid_hi = sb("mid_hi", [P, KD, T], F32R)
        mid_lo = sb("mid_lo", [P, KD, T], F32R)
        raw = sb("raw", [P, RAW_SLOTS, KPU, CW])
        w_hi = sb("w_hi", [P, SPLIT_SLOTS, KPU, CW], F32R)
        w_lo = sb("w_lo", [P, SPLIT_SLOTS, KPU, CW], F32R)
        ysb = sb("ysb", [P, TT, CW])
        zsb = sb("zsb", [P, TT, CW])
        ident = sb("ident", [P, P])
        ones = sb("ones", [P, P])
        consts = sb("consts", [P, 4])
        cols = sb("cols", [P, P])
        pos_cols = sb("pos_cols", [P, 2 * CMP_BLOCK])
        conv_w_cols = sb("conv_w_cols", [P, CONV_G, CONV_K + 1])
        q_gain = sb("q_gain", [P, 2])
        norm_scale = sb("norm_scale", [P, 4, KD])
        norm_shift = sb("norm_shift", [P, 4, KD])
        mod_cols = sb("mod_cols", [P, 4 * KD])
        c_act = sb("c_act", [P, KD])
        sq_sum = sb("sq_sum", [P, 6, TT, D // CW])
        mean_sq = sb("mean_sq", [P, 6, TT])
        std = sb("std", [P, 6, TT])
        rstd = sb("rstd", [P, 6, TT])
        head_ss = sb("head_ss", [P, TT * HPC])
        head_std = sb("head_std", [P, TT * HPC])
        head_rstd = sb("head_rstd", [P, TT * HPC])
        ada_bias = sb("ada_bias", [1, CW])

        right = ExitStack()
        act_hi = sb("act_hi", [P, KD, T], F32R, right, "right")
        act_lo = sb("act_lo", [P, KD, T], F32R, right, "right")
        right.close()
        right = ExitStack()
        rows0 = sb("rows0", [P, P], F32, right, "right")
        rows1 = sb("rows1", [2 * CMP_BLOCK, P], F32, right, "right")
        conv_rows = sb("conv_rows", [CONV_K, CONV_CH], F32, right, "right")
        w_small = sb("w_small", [P, KD, N_SMALL], F32, right, "right")
        right.close()
        right = ExitStack()
        blk_k = sb("blk_k", [P, CMP_BLOCK, 64], F32, right, "right")
        blk_v = sb("blk_v", [P, CMP_BLOCK, 64], F32, right, "right")
        lf_cols = sb("lf_cols", [P, TT, FOX_H, 64], F32, right, "right")
        right.close()
        right = ExitStack()
        dec_l = sb("dec_l", [64, FOX_H, T], F32, right, "right")
        dec_r = sb("dec_r", [64, FOX_H, T], F32, right, "right")
        cost1 = sb("cost1", [P, 2, TAB], F32, right, "right")
        prob1 = sb("prob1", [P, 2, TAB], F32, right, "right")
        probT1 = sb("probT1", [P, 2, TAB], F32, right, "right")
        cmp_cost = sb("cmp_cost", [P, TT * NSA_H, 32], F32, right, "right")
        cmp_prob = sb("cmp_prob", [P, TT * NSA_H, 32], F32, right, "right")
        cmp_probT = sb("cmp_probT", [P, 2, T], F32, right, "right")
        right.close()
        right = ExitStack()
        cost2 = sb("cost2", [P, 2, TAB], F32, right, "right")
        prob2 = sb("prob2", [P, 2, TAB], F32, right, "right")
        probT2 = sb("probT2", [P, 2, TAB], F32, right, "right")
        conv_sq = sb("conv_sq", [P, CONV_G, T], F32, right, "right")
        conv_mu = sb("conv_mu", [P, T], F32, right, "right")
        conv_rs = sb("conv_rs", [P, T], F32, right, "right")
        right.close()
        right = ExitStack()
        for n_ in ("act_hold_a", "act_hold_b"):
            sb(n_, [P, KD, T], F32, right, "right")

        A = ExitStack()
        heads = {n: sb(n, [P, k, T], F32, A) for n, k in
                 (("fq", FOX_H), ("fk", FOX_H), ("nq", NSA_H), ("kc", NSA_G), ("vc", NSA_G), ("ks", NSA_G),
                  ("kw", NSA_G))}
        vals = {n: sb(n, [P, TT, k, HD], F32, A) for n, k in (("fv", FOX_H), ("vs", NSA_G), ("vw", NSA_G))}
        ws = sb("ws", [P, KD, 2, N_SMALL], F32R, A)
        small = sb("small", [P, TT, N_SMALL], F32, A)
        forget_bias = sb("forget_bias", [P, FOX_H], F32, A)
        upper = sb("upper", [P, T], F32, A)
        mask = sb("mask", [P, T], F32, A)
        dist = sb("dist", [P, T], F32, A)
        alibi = sb("alibi", [P, NSA_H, T], F32, A)
        cmp_tab = sb("cmp_tab", [P, TT, NSA_H, 32], F32, A)
        cmp_ok = sb("cmp_ok", [P, TT, 32], F32, A)
        lf = sb("lf", [P, 6, TT, FOX_H], F32, A)
        gates = sb("gates", [P, TT, 3 * NSA_H], F32, A)
        gate_e = sb("gate_e", [P, TT, 3 * NSA_H], F32, A)
        kcn = sb("kcn", [64, HD], F32, A)
        kc_ss = sb("kc_ss", [64, 3], F32, A)
        kcmpT = sb("kcmpT", [P, 64], F32, A)
        vcmp = sb("vcmp", [P, NSA_G, HD], F32, A)
        cmp_min = sb("cmp_min", [P, TT * NSA_H], F32, A)
        cmp_sum = sb("cmp_sum", [P, TT * NSA_H], F32, A)
        row_min1 = sb("row_min1", [P, 2, TT], F32, A)
        row_sum1 = sb("row_sum1", [P, 2, TT], F32, A)
        row_inv1 = sb("row_inv1", [P, 2, TT], F32, A)
        A.close()

        B = ExitStack()
        gate_row1 = sb("gate_row1", [P, D], F32, B)
        ada_raw = sb("ada_raw", [P, 2, KPU, CW], F32, B)
        ada_acc = sb("ada_acc", [P, CW], F32, B)
        mask2 = sb("mask2", [P, T], F32, B)
        Cs = ExitStack()
        for n in ("mq", "mk"):
            heads[n] = sb(n, [P, 8, T], F32, Cs)
        vals["mv"] = sb("mv", [P, TT, 8, HD], F32, Cs)
        a_keep = sb("a_keep", [P, TT, CW], F32, Cs)
        uT = sb("uT", [P, CONV_G, CONV_K - 1 + T], F32, Cs)
        convT = sb("convT", [P, CONV_G, T], F32, Cs)
        conv_tmp = sb("conv_tmp", [P, 1, T], F32, Cs)
        row_min2 = sb("row_min2", [P, 2, TT], F32, Cs)
        row_sum2 = sb("row_sum2", [P, 2, TT], F32, Cs)
        row_inv2 = sb("row_inv2", [P, 2, TT], F32, Cs)
        Cs.close()
        Ds = ExitStack()
        y_acc = sb("y_acc", [P, TT, D], F32, Ds)
        gate_row2 = sb("gate_row2", [P, D], F32, Ds)
        Ds.close()
        B.close()
        right.close()

        bank = [top.enter_context(nc.psum_tensor(f"bank{i}", [P, CW], F32)) for i in range(8)]

        def acc(C):
            return [bank[2 * (C % 2)], bank[2 * (C % 2) + 1]]

        TURN = [bank[4], bank[5]]
        MISC = [bank[6], bank[7]]

        raw_loaded = [sem(f"raw_loaded{i}") for i in range(RAW_SLOTS)]
        hi_done, lo_done, parts_used = sem("hi_done"), sem("lo_done"), sem("parts_used")
        acc_free = [sem("acc_free0"), sem("acc_free1")]
        params_loaded, small_loaded = sem("params_loaded"), sem("small_loaded")
        x_loaded = [sem(f"x_loaded{t}") for t in range(TT)]
        tables_made = sem("tables_made")
        cols_turned, cols_ready = sem("cols_turned"), sem("cols_ready")
        c_ready = sem("c_ready")
        ss_act, ms_ready, std_ready, rstd_ready = (sem("ss_act"), sem("ms_ready"), sem("std_ready"),
                                                   sem("rstd_ready"))
        xn_ready_a, xn_ready_d, xn_turned, full_ready = (sem("xn_ready_a"), sem("xn_ready_d"), sem("xn_turned"),
                                                         sem("full_ready"))
        y_gated, small_folded = sem("y_gated"), sem("small_folded")
        act_hi_done, act_lo_done = sem("act_hi_done"), sem("act_lo_done")
        ws_split_hi, ws_split, small_mm, small_out = (sem("ws_split_hi"), sem("ws_split"), sem("small_mm"),
                                                      sem("small_out"))
        head_sq, head_std_ready = sem("head_sq"), sem("head_std_ready")
        turned, turn_out_a, turn_out_d = sem("turned"), sem("turn_out_a"), sem("turn_out_d")
        glu_sig, glu_ready = sem("glu_sig"), sem("glu_ready")
        sig_ready, h_ready, h_turned = sem("sig_ready"), sem("h_ready"), sem("h_turned")
        mid_hi_done, mid_lo_done = sem("mid_hi_done"), sem("mid_lo_done")
        ada_loaded = [sem("ada_loaded0"), sem("ada_loaded1")]
        ada_bias_loaded, ada_used, ada_summed, ada_out = (sem("ada_bias_loaded"), sem("ada_used"),
                                                          sem("ada_summed"), sem("ada_out"))
        gate_loaded = sem("gate_loaded")
        blk_zero, blk_ready, cmp_used = sem("blk_zero"), sem("blk_ready"), sem("cmp_used")
        kc_sq, kc_std, kc_n, kc_turned, kc_ready, vc_ready = (sem("kc_sq"), sem("kc_std"), sem("kc_n"),
                                                              sem("kc_turned"), sem("kc_ready"), sem("vc_ready"))
        lf_zero, lf_a, lf_d, lf_cum, dec_zero, dec_a, dec_d = (
            sem("lf_zero"), sem("lf_a"), sem("lf_d"), sem("lf_cum"), sem("dec_zero"), sem("dec_a"), sem("dec_d"))
        gate_exp, gates_ready = sem("gate_exp"), sem("gates_ready")
        cmp_scored, cmp_shift, cmp_exp, cmp_p, cmp_pT, cmp_pT_out = (
            sem("cmp_scored"), sem("cmp_shift"), sem("cmp_exp"), sem("cmp_p"), sem("cmp_pT"), sem("cmp_pT_out"))
        scored, reduced, exped, scaled, p_turned, p_out, pv_done = (
            sem("scored"), sem("reduced"), sem("exped"), sem("scaled"), sem("p_turned"), sem("p_out"),
            sem("pv_done"))
        o_hi, o_lo = sem("o_hi"), sem("o_lo")
        uT_zero, conv_pool, conv_dve = sem("uT_zero"), sem("conv_pool"), sem("conv_dve")
        ln_sum, ln_d, ln_sq, ln_var, ln_std, ln_y, ln_silu, ln_hi, ln_lo = (
            sem("ln_sum"), sem("ln_d"), sem("ln_sq"), sem("ln_var"), sem("ln_std"), sem("ln_y"), sem("ln_silu"),
            sem("ln_hi"), sem("ln_lo"))
        x_updated, out_stored = sem("x_updated"), sem("out_stored")
        chain_d, chain_a, chain_p = sem("chain_d"), sem("chain_a"), sem("chain_p")

        READ_SEM = {"gate": sig_ready, "up": h_ready, "glu": glu_sig, ("free", 0): acc_free[0],
                    ("free", 1): acc_free[1]}

        def wait_read(eng, C, r=None):
            key, value = READ[C]
            eng.wait_ge(READ_SEM[key], at(value, r, 2))

        ROWS0 = [(io["attn_norm"][0].rearrange("(k p) -> k p", p=P), 0, KD),
                 (io["ffn_norm"][0].rearrange("(k p) -> k p", p=P), 16, KD),
                 (io["mix_pre_g_2"][0].rearrange("(k p) -> k p", p=P), 32, KD),
                 (io["ffn_pre_g_2"][0].rearrange("(k p) -> k p", p=P), 48, KD),
                 (io["c_2"][0].rearrange("(k p) -> k p", p=P), 64, KD),
                 (io["fox_q_norm"], 80, 1), (io["fox_k_norm"], 81, 1), (io["nsa_q_norm"], 82, 1),
                 (io["cmp_k_norm"], 83, 1), (io["slc_k_norm"], 84, 1), (io["win_k_norm"], 85, 1),
                 (io["conv_b_2"][0].rearrange("(k p) -> k p", p=P), 86, CONV_G),
                 (io["conv_ln_g_2"][0].rearrange("(k p) -> k p", p=P), 94, CONV_G),
                 (io["conv_ln_b_2"][0].rearrange("(k p) -> k p", p=P), 102, CONV_G)]
        N_PARAM = len(ROWS0) + 4

        block = top.enter_context(nc.Block())

        def keep(eng, prev, t, put, done):
            kind = prev[0]
            src = TURN[t]
            cols_t = slice(t * P, (t + 1) * P)

            def v(k0, k1):
                return src[:, k0 * P:k1 * P].rearrange("p (k t) -> p k t", t=P)

            if kind == "glu":
                o = uT[:, 4 * prev[1]:4 * prev[1] + 4, CONV_K - 1 + t * P:CONV_K - 1 + (t + 1) * P]
                put(o, v(0, 4), 1.0).then_inc(done, 1)
            elif kind == "plain" and prev[1] == "kcvc":
                put(heads["kc"][:, :, cols_t], v(0, 2), 1.0)
                put(heads["vc"][:, :, cols_t], v(2, 4), 1.0).then_inc(done, 1)
            elif kind == "plain":
                g = -SCALE if prev[1] == "mq" else 1.0
                put(heads[prev[1]][:, prev[2]:prev[2] + HPC, cols_t], v(0, 4), g).then_inc(done, 1)
            else:
                k = HPC if kind == "normed" else NSA_G
                gain = {"fq": q_gain[:, 0:1], "fk": cols[:, 81:82], "nq": q_gain[:, 1:2],
                        "ks": cols[:, 84:85], "kw": cols[:, 85:86]}[prev[1]]
                put(heads[prev[1]][:, prev[2]:prev[2] + k, cols_t], v(0, k), gain).then_inc(done, 1)

        def squares(i):
            return i * TT * (D // CW)

        def run(steps, eng, do):
            for s in steps:
                if "loop" in s:
                    with eng.Fori(0, s["loop"]) as r:
                        for c in s["body"]:
                            do(c, r)
                else:
                    do(s, None)

        @block.sync
        def _(sp):
            for t in range(TT):
                sp.dma_start(x_res[:, t, :], io["x"][0, t * P:(t + 1) * P, :]).then_inc(x_loaded[t], 16)
            sp.dma_start(w_small[:, :, 0:FOX_H], W["w_in"][:, :, o_ff:o_ff + FOX_H]).then_inc(small_loaded, 16)
            sp.dma_start(w_small[:, :, FOX_H:N_SMALL], W["w_in"][:, :, o_gt:o_gt + 3 * NSA_H]).then_inc(
                small_loaded, 16)

            def slot_free(R, r, stride):
                R -= RAW_SLOTS
                if R < 0:
                    return
                if R_CMP <= R < R_CMP + N_CMPU:
                    sp.wait_ge(cmp_used, R - R_CMP + 1)
                else:
                    sp.wait_ge(lo_done, at((R if R < R_CMP else R - N_CMPU) + 1, r, stride))

            def ada_load(c, r, i):
                a = c["ada"]
                unit = a["A"] + i
                if unit >= 2:
                    sp.wait_ge(ada_used, at(2 * (unit - 1), r, 16))
                k = a["half"] * 8 + 2 * i
                n0 = at(a["col"], r, a["step"])
                sp.dma_start(ada_raw[:, unit % 2], W["ada_w_2"][:, k:k + KPU, bass.ds(n0, CW)]).then_inc(
                    ada_loaded[unit % 2], 16)
                if a["half"] == 0 and i == 0:
                    if a["blk"] >= 1:
                        sp.wait_ge(ada_summed, at(a["blk"], r, 1))
                    sp.dma_start(ada_bias[:, :], io["ada_b_2"][0:1, bass.ds(n0, CW)]).then_inc(ada_bias_loaded, 16)

            def load(c, r):
                for u in range(c["nu"]):
                    R = c["R"] + u
                    slot_free(R, r, 2 * c["nu"])
                    k = c["k0"] + KPU * u
                    n0 = at(c["n0"], r, c["n_step"])
                    sp.dma_start(raw[:, R % RAW_SLOTS], W[c["w"]][:, k:k + KPU, bass.ds(n0, CW)]).then_inc(
                        raw_loaded[R % RAW_SLOTS], 16)
                    if c["ada"] and u in (1, 2, 5, 6)[:4]:
                        ada_load(c, r, (1, 2, 5, 6).index(u))
                if c["ada"] and c["nu"] < 7:
                    ada_load(c, r, 3)

            run(S_IN1, sp, load)
            for j in range(N_CMPU):
                R = R_CMP + j
                slot_free(R, None, 0)
                src = io["cmp_w_k" if j < 4 else "cmp_w_v"][0].rearrange("l d e -> d l e")
                l0 = 8 * (j % 4)
                sp.dma_start(raw[:, R % RAW_SLOTS].rearrange("p a n -> p (a n)").rearrange("p (l e) -> p l e", e=HD),
                             src[:, l0:l0 + 8, :]).then_inc(raw_loaded[R % RAW_SLOTS], 16)
            c0 = S_OUT1[0]
            for u in range(RAW_SLOTS):
                slot_free(c0["R"] + u, None, 0)
                sp.dma_start(raw[:, (c0["R"] + u) % RAW_SLOTS],
                             W["w_out"][:, KPU * u:KPU * u + KPU, 0:CW]).then_inc(
                    raw_loaded[(c0["R"] + u) % RAW_SLOTS], 16)
            sp.wait_ge(o_lo, N_OUT_1)
            sp.dma_start(gate_row1[:, :], io["mix_post_g_2"][0].partition_broadcast(P)).then_inc(gate_loaded, 16)

            def load_out1(c, r):
                if c is c0:
                    for u in range(c["nu"]):
                        R = c["R"] + u
                        if u >= RAW_SLOTS:
                            slot_free(R, r, 0)
                            sp.dma_start(raw[:, R % RAW_SLOTS],
                                         W["w_out"][:, KPU * u:KPU * u + KPU, 0:CW]).then_inc(
                                raw_loaded[R % RAW_SLOTS], 16)
                        if u in (1, 2, 5, 6):
                            ada_load(c, r, (1, 2, 5, 6).index(u))
                else:
                    load(c, r)

            run(S_OUT1, sp, load_out1)
            run(S_FFN1, sp, load)
            run(S_IN2, sp, load)
            run(S_OUT2, sp, load)
            sp.wait_ge(o_lo, N_OUT_1 + 8)
            sp.wait_ge(ln_lo, 1)
            sp.dma_start(gate_row2[:, :], io["ffn_post_g_2"][0].partition_broadcast(P)).then_inc(gate_loaded, 16)
            run(S_FFN2, sp, load)
            for t in range(TT):
                for h in range(2):
                    sp.wait_ge(x_updated, 4 * (TT + t) + 2 * h + 2)
                    sp.dma_start(out[0, t * P:(t + 1) * P, h * D // 2:(h + 1) * D // 2],
                                 x_res[:, t, h * D // 2:(h + 1) * D // 2]).then_inc(out_stored, 16)
            sp.wait_ge(out_stored, 16 * 2 * TT)

        @block.gpsimd
        def _(pool):
            n = [0]

            def link(ins):
                n[0] += 1
                ins.then_inc(chain_p, 1)
                pool.wait_ge(chain_p, n[0])

            for i, val in enumerate((1e-6, 1e-5, 1.0, 0.0)):
                link(pool.memset(consts[:, i:i + 1], val))
            link(pool.memset(ident[:, :], 0.0))
            link(pool.affine_select(out=ident[:, :], in_=ident[:, :], pattern=[[-1, P]],
                                    compare_op=ALU.not_equal, fill=1.0, base=0, channel_multiplier=1))
            link(pool.memset(ones[:, :], 1.0))
            pool.memset(norm_shift[:, 0:2, :], 0.0).then_inc(tables_made, 1)
            link(pool.memset(upper[:, :], 1.0))
            link(pool.affine_select(out=upper[:, :], in_=upper[:, :], pattern=[[1, T]], compare_op=ALU.is_ge,
                                    fill=0.0, base=0, channel_multiplier=-1))
            link(pool.memset(mask[:, :], 0.0))
            link(pool.affine_select(out=mask[:, :], in_=mask[:, :], pattern=[[-1, T]], compare_op=ALU.is_ge,
                                    fill=BIG, base=P, channel_multiplier=1))
            link(pool.iota(dist[:, :], pattern=[[-1, T]], base=P, channel_multiplier=1,
                           allow_small_or_imprecise_dtypes=True))
            for h in range(NSA_H):
                slope = 2.0 ** (-8.0 * (h + 1) / NSA_H)
                link(pool.tensor_scalar(alibi[:, h, :], dist[:, :], slope, None, ALU.mult))
                link(pool.tensor_tensor(alibi[:, h, :], alibi[:, h, :], mask[:, :], ALU.add))
            pat = [[P, TT], [0, NSA_H], [-CMP_STRIDE, 32]]
            base = -(CMP_BLOCK - 1)
            link(pool.iota(cmp_tab[:, :, :, :], pattern=pat, base=base, channel_multiplier=1,
                           allow_small_or_imprecise_dtypes=True))
            for h in range(NSA_H):
                slope = 2.0 ** (-8.0 * (h + 1) / NSA_H)
                link(pool.tensor_scalar(cmp_tab[:, :, h, :], cmp_tab[:, :, h, :], slope, None, ALU.mult))
            link(pool.affine_select(out=cmp_tab[:, :, :, :], in_=cmp_tab[:, :, :, :], pattern=pat,
                                    compare_op=ALU.is_ge, fill=BIG, base=base, channel_multiplier=1))
            link(pool.memset(cmp_ok[:, :, :], 1.0))
            link(pool.affine_select(out=cmp_ok[:, :, :], in_=cmp_ok[:, :, :], pattern=[pat[0], pat[2]],
                                    compare_op=ALU.is_ge, fill=0.0, base=base, channel_multiplier=1))
            pool.memset(vcmp[:, :, :], 0.0).then_inc(tables_made, 1)
            pool.wait_ge(parts_used, U_CMP)
            pool.memset(lf_cols[:, :, :, :], 0.0).then_inc(blk_zero, 1)
            pool.memset(blk_k[:, :, :], 0.0).then_inc(blk_zero, 1)
            pool.memset(blk_v[:, :, :], 0.0).then_inc(blk_zero, 1)
            pool.wait_ge(cmp_used, N_CMPU)
            link(pool.memset(dec_l[:, :, :], 0.0))
            link(pool.memset(dec_r[:, :, :], 0.0))
            link(pool.memset(dec_l[32:33, :, :], 1.0))
            pool.memset(dec_r[0:1, :, :], 1.0).then_inc(dec_zero, 1)
            pool.wait_ge(o_lo, N_OUT_1)
            link(pool.memset(mask2[:, :], 0.0))
            link(pool.affine_select(out=mask2[:, :], in_=mask2[:, :], pattern=[[-1, T]], compare_op=ALU.is_ge,
                                    fill=BIG, base=P, channel_multiplier=1))
            pool.memset(uT[:, :, 0:CONV_K - 1], 0.0).then_inc(uT_zero, 1)
            pool.wait_ge(uT_zero, 1)
            pool.wait_ge(turn_out_a, TURNS.index(("glu", 0)) + 1)
            pool.wait_ge(turn_out_d, TURNS.index(("glu", 0)) + 1)
            for k in range(CONV_K):
                for g in CONV_POOL:
                    src = uT[:, g, k:k + T]
                    wk = conv_w_cols[:, g, k:k + 1]
                    if k == 0:
                        ins = pool.tensor_scalar(convT[:, g, :], src, wk, cols[:, 86 + g:87 + g], ALU.mult, ALU.add)
                        link(ins)
                    else:
                        link(pool.tensor_scalar(conv_tmp[:, 0, :], src, wk, None, ALU.mult))
                        ins = pool.tensor_tensor(convT[:, g, :], convT[:, g, :], conv_tmp[:, 0, :], ALU.add)
                        if (k, g) == (CONV_K - 1, CONV_POOL[-1]):
                            ins.then_inc(conv_pool, 1)
                        else:
                            link(ins)

        @block.tensor
        def _(pe):
            pe.wait_ge(tables_made, 1)
            pe.wait_ge(params_loaded, 16 * N_PARAM)
            pe.transpose(MISC[0][:, 0:110], rows0[0:110, :], ident[0:110, 0:110])
            pe.transpose(MISC[0][:, 128:192], rows1[:, :], ident[0:64, 0:64])
            for g in range(CONV_G):
                ins = pe.transpose(MISC[1][:, 32 * g:32 * g + CONV_K], conv_rows[:, g * P:(g + 1) * P],
                                   ident[0:CONV_K, 0:CONV_K])
            ins.then_inc(cols_turned, 1)

            def turn_rows(i):
                pe.wait_ge(xn_ready_a, i + 1)
                pe.wait_ge(xn_ready_d, i + 1)
                if i >= 2:
                    pe.wait_ge(full_ready, i - 1)
                for c in range(KPU):
                    for t in range(TT):
                        ins = pe.transpose(TURN[i % 2][:, (c * TT + t) * P:(c * TT + t + 1) * P],
                                           ysb[:, i % 2, (t * KPU + c) * P:(t * KPU + c + 1) * P], ident[:, :])
                ins.then_inc(xn_turned, 1)

            def first_gemm(c, n):
                turn_rows(n * NU)
                turn_rows(n * NU + 1)

                def after(u):
                    if n == 0:
                        small_gemm(u)
                    if u + 2 < NU:
                        turn_rows(n * NU + u + 2)

                gemm(c, None, lambda u: pe.wait_ge(act_lo_done, n * NU + u + 1), after)

            def small_gemm(u):
                if u == 0:
                    pe.wait_ge(ws_split, 1)
                    pe.wait_ge(cols_ready, 2)
                for kk in range(KPU):
                    k = KPU * u + kk
                    st = ws[:, k, :, :].rearrange("p s n -> p (s n)")
                    pe.matmul(MISC[0][0:2 * N_SMALL, 0:T], st, act_hi[:, k, :], start=(k == 0), stop=False)
                    ins = pe.matmul(MISC[0][0:2 * N_SMALL, 0:T], st, act_lo[:, k, :], start=False,
                                    stop=(k == KD - 1))
                if u == NU - 1:
                    ins.then_inc(small_mm, 1)

            def small_fold():
                pe.wait_ge(small_folded, 1)
                for t in range(TT):
                    for part in range(2):
                        ins = pe.matmul(MISC[0][:, t * N_SMALL:(t + 1) * N_SMALL],
                                        ysb[0:2 * N_SMALL, 0, t * P:(t + 1) * P],
                                        ident[0:2 * N_SMALL, part * N_SMALL:(part + 1) * N_SMALL],
                                        start=(part == 0), stop=(part == 1))
                ins.then_inc(small_mm, 1)

            def consume(prev, C, r):
                if prev is None or prev[0] in ("value", "keep_a", "add", "gate"):
                    return
                if prev[0] == "up":
                    q = prev[1]
                    pe.wait_ge(h_ready, at(2 * q + 2, r, 2))
                    if q >= 1:
                        pe.wait_ge(mid_lo_done, at(2 * q, r, 2))
                    for t in range(TT):
                        for c in range(HPC):
                            ins = pe.transpose(TURN[t][:, c * P:(c + 1) * P], zsb[:, t, c * P:(c + 1) * P], ident[:, :])
                        ins.then_inc(h_turned, 1)
                    return
                i = TURNS.index(prev)
                if prev[0] == "glu":
                    pe.wait_ge(glu_ready, 2 * prev[1] + 2)
                else:
                    wait_read(pe, C - 1)
                if i >= 1:
                    pe.wait_ge(turn_out_a, i)
                    pe.wait_ge(turn_out_d, i)
                k = NSA_G if prev[0] == "kv" else HPC
                for t in range(TT):
                    for c in range(k):
                        ins = pe.transpose(TURN[t][:, c * P:(c + 1) * P], ysb[:, t, c * P:(c + 1) * P], ident[:, :])
                ins.then_inc(turned, 1)

            def gemm(c, r, before=lambda u: None, after=lambda u: None):
                hi, lo = (act_hi, act_lo) if c["st"] == "act" else (mid_hi, mid_lo)
                C, nu = c["C"], c["nu"]
                A_ = acc(C)
                for u in range(nu):
                    if u == 0:
                        if C >= 2:
                            wait_read(pe, C - 2, r)
                        if c.get("first") == "mix1":
                            pe.wait_ge(o_lo, N_OUT_1)
                        if c.get("first") == "mix2":
                            pe.wait_ge(o_lo, N_OUT_1 + 8)
                            pe.wait_ge(ln_lo, 1)
                    if c.get("first") == "ffn":
                        pe.wait_ge(mid_lo_done, 2 * (c["pairs"] - (0 if u >= nu - 2 else 1)))
                    before(u)
                    U = c["U"] + u
                    pe.wait_ge(lo_done, at(U + 1, r, 2 * nu))
                    s = U % SPLIT_SLOTS
                    for kk in range(KPU):
                        k = KPU * u + kk
                        for t in range(TT):
                            h_, l_ = hi[:, k, t * P:(t + 1) * P], lo[:, k, t * P:(t + 1) * P]
                            pe.matmul(A_[t][:, :], h_, w_hi[:, s, kk, :], start=(k == 0), stop=False)
                            pe.matmul(A_[t][:, :], h_, w_lo[:, s, kk, :], start=False, stop=False)
                            ins = pe.matmul(A_[t][:, :], l_, w_hi[:, s, kk, :], start=False,
                                            stop=(k == KPU * nu - 1))
                    ins.then_inc(parts_used, 1)
                    after(u)
                    if u == min(4, nu - 3):
                        consume(c["prev"], C, r)
                    if c is S_IN1[SMALL_OUT] and u == 6:
                        small_fold()
                    a = c["ada"]
                    if a and a["half"] == 1 and u == 5:
                        pe.wait_ge(ada_used, at(2 * (a["A"] + 4), r, 16))
                        pe.wait_ge(ada_bias_loaded, at(16 * (a["blk"] + 1), r, 16))
                        if a["blk"] >= 1:
                            pe.wait_ge(ada_out, at(a["blk"], r, 1))
                        if a["kind"] == "col":
                            for j in range(4):
                                pe.matmul(MISC[0][:, j:j + 1], ada_acc[:, j * P:(j + 1) * P], ones[:, 0:1],
                                          start=True, stop=False)
                                ins = pe.matmul(MISC[0][:, j:j + 1], ada_bias[0:1, j * P:(j + 1) * P],
                                                ones[0:1, 0:1], start=False, stop=True)
                        else:
                            pe.matmul(MISC[0][:, :], ones[:, :], ada_acc[:, :], start=True, stop=False)
                            ins = pe.matmul(MISC[0][:, :], ones[0:1, :], ada_bias[0:1, :], start=False, stop=True)
                        ins.then_inc(ada_summed, 1)

            def attend(j0, j1, cost, prob, probT, hook=lambda i: None):
                def scores(j):
                    b, s = JOBS[j], bank[j % 2]
                    if j - j0 >= 2:
                        pe.wait_ge(reduced, 2 * (j - 1))
                    q, k = heads[b["q"]], heads[b["k"]]
                    for t, c0, n in ((0, 0, P), (1, P, T)):
                        ins = pe.matmul(s[:, c0:c0 + n], q[:, b["h"], t * P:(t + 1) * P], k[:, b["kv"], 0:n],
                                        start=True, stop=not b["decay"])
                        if b["decay"]:
                            ins = pe.matmul(s[:, c0:c0 + n], dec_l[:, b["h"], t * P:(t + 1) * P],
                                            dec_r[:, b["h"], 0:n], start=False, stop=True)
                    ins.then_inc(scored, 1)

                def turn(j):
                    pe.wait_ge(scaled, 2 * j + 2)
                    if j - j0 >= 2:
                        pe.wait_ge(p_out, j - 1)
                    for c in range(3):
                        ins = pe.transpose(bank[2 + j % 2][:, c * P:(c + 1) * P], prob[:, j % 2, c * P:(c + 1) * P],
                                           ident[:, :])
                    ins.then_inc(p_turned, 1)

                def values(j):
                    b = JOBS[j]
                    o = bank[4 + b["o"] % 2]
                    pe.wait_ge(p_out, j + 1)
                    if b["first"] and j > j0 and b["o"] - JOBS[j0]["o"] >= 2:
                        pe.wait_ge(o_lo, b["o"] - 1)
                    v = vals[b["v"]]
                    pT = probT[:, j % 2, :]
                    pe.matmul(o[:, 0:T], v[:, 0, b["kv"], :], pT[:, 0:T], start=b["first"], stop=False)
                    ins = pe.matmul(o[:, P:T], v[:, 1, b["kv"], :], pT[:, T:TAB], start=False, stop=b["last"] and not b["cmp"])
                    if b["cmp"]:
                        r0 = 32 * (b["h"] % 4)
                        ins = pe.matmul(o[:, 0:T], vcmp[r0:r0 + 32, b["kv"], :],
                                        cmp_probT[r0:r0 + 32, b["h"] // 4, :], start=False, stop=True)
                    ins.then_inc(pv_done, 1)

                for i in range(j0, j1 + 3):
                    if i < j1:
                        scores(i)
                    if j0 + 2 <= i < j1 + 2:
                        turn(i - 2)
                    if i >= j0 + 3:
                        values(i - 3)
                    hook(i)

            first_gemm(S_IN1[0], 0)
            run(S_IN1[1:], pe, gemm)
            consume(LAST1, C_IN1, None)
            wait_read(pe, C_IN1 - 2)
            wait_read(pe, C_IN1 - 1)
            pe.wait_ge(lf_d, 2)
            pe.wait_ge(tables_made, 2)
            for h in range(FOX_H):
                o, c0 = bank[h // 2], (h % 2) * T
                pe.matmul(o[0:64, c0:c0 + T], lf_cols[:, 0, h, :], upper[:, :], start=True, stop=False)
                ins = pe.matmul(o[0:64, c0 + P:c0 + T], lf_cols[:, 1, h, :], upper[:, 0:P], start=False, stop=True)
            ins.then_inc(lf_cum, 1)
            pe.wait_ge(small_out, 1)
            for kind, blk in ((0, blk_k), (1, blk_v)):
                pe.wait_ge(blk_ready, kind + 1)
                for j in range(4):
                    R = R_CMP + 4 * kind + j
                    pe.wait_ge(raw_loaded[R % RAW_SLOTS], 16 * (R // RAW_SLOTS + 1))
                    w = raw[:, R % RAW_SLOTS].rearrange("p a n -> p (a n)")
                    for l in range(8):
                        ins = pe.matmul(MISC[kind][0:64, 0:HD], blk[:, 8 * j + l, :], w[:, l * HD:(l + 1) * HD],
                                        start=(j + l == 0), stop=(j == 3 and l == 7))
                    ins.then_inc(cmp_used, 1)
            pe.wait_ge(kc_n, 1)
            pe.wait_ge(turn_out_a, len(IN1) - 2)
            pe.wait_ge(turn_out_d, len(IN1) - 2)
            pe.transpose(TURN[0][:, 0:64], kcn[:, :], ident[0:64, 0:64]).then_inc(kc_turned, 1)
            pe.wait_ge(kc_ready, 1)
            pe.wait_ge(vc_ready, 1)
            for h in range(NSA_H):
                for t in range(TT):
                    g = h // HPG
                    c0 = (t * NSA_H + h) * 32
                    ins = pe.matmul(MISC[1][:, c0:c0 + 32], heads["nq"][:, h, t * P:(t + 1) * P],
                                    kcmpT[:, 32 * g:32 * g + 32], start=True, stop=True)
            ins.then_inc(cmp_scored, 1)
            pe.wait_ge(cmp_p, 1)
            for hh in range(2):
                for t in range(TT):
                    src = cmp_prob[:, t * NSA_H + hh * 4:t * NSA_H + hh * 4 + 4, :].rearrange("p h n -> p (h n)")
                    ins = pe.transpose(MISC[0][:, (hh * TT + t) * P:(hh * TT + t + 1) * P], src, ident[:, :])
            ins.then_inc(cmp_pT, 1)
            pe.wait_ge(cmp_pT_out, 1)
            pe.wait_ge(dec_a, 1)
            pe.wait_ge(dec_d, 1)
            attend(0, N_JOB1, cost1, prob1, probT1)

            def flush_acc(C):
                wait_read(pe, C - 2)
                wait_read(pe, C - 1)

            run(S_OUT1, pe, gemm)
            first_gemm(S_FFN1[0], 1)
            run(S_FFN1[1:], pe, gemm)
            first_gemm(S_IN2[0], 2)
            run(S_IN2[1:], pe, gemm)
            consume(LAST2, LAST_C["in2"], None)
            flush_acc(LAST_C["in2"])
            pe.wait_ge(turn_out_a, len(TURNS))
            pe.wait_ge(turn_out_d, len(TURNS))
            attend(N_JOB1, len(JOBS), cost2, prob2, probT2)
            pe.wait_ge(conv_pool, 1)
            pe.wait_ge(conv_dve, len(early) + len(late))
            for g in range(CONV_G):
                ins = pe.matmul(MISC[0][:, 0:T], ones[:, :], convT[:, g, :], start=(g == 0), stop=(g == CONV_G - 1))
            ins.then_inc(ln_sum, 1)
            pe.wait_ge(ln_sq, 1)
            for g in range(CONV_G):
                ins = pe.matmul(MISC[1][:, 0:T], ones[:, :], conv_sq[:, g, :], start=(g == 0), stop=(g == CONV_G - 1))
            ins.then_inc(ln_var, 1)
            run(S_OUT2, pe, gemm)
            first_gemm(S_FFN2[0], 3)
            run(S_FFN2[1:], pe, gemm)

        @block.scalar
        def _(act):
            chain = [0]

            def link(ins):
                chain[0] += 1
                ins.then_inc(chain_a, 1)
                act.wait_ge(chain_a, chain[0])

            for src, r0, k in ROWS0:
                act.dma_start(rows0[r0:r0 + k, :], src).then_inc(params_loaded, 16)
            act.dma_start(rows1[0:CMP_BLOCK, :], io["cmp_pos_k"][0]).then_inc(params_loaded, 16)
            act.dma_start(rows1[CMP_BLOCK:, :], io["cmp_pos_v"][0]).then_inc(params_loaded, 16)
            act.dma_start(conv_rows[:, :], io["conv_w_2"][0]).then_inc(params_loaded, 16)
            act.dma_start(forget_bias[:, :], io["fox_forget_bias"][0].partition_broadcast(P)).then_inc(
                params_loaded, 16)

            n_sq = [0]

            def square(i, t, q, src):
                act.activation(ysb[:, 0, :], src, ACT.Square, accum_out=sq_sum[:, i, t, q:q + 1]).then_inc(ss_act, 1)
                n_sq[0] += 1
                act.wait_ge(ss_act, n_sq[0])

            def root(i):
                act.wait_ge(ms_ready, i + 1)
                act.activation(std[:, i, :], mean_sq[:, i, :], ACT.Sqrt, bias=consts[:, 0:1],
                               scale=1.0 / D).then_inc(std_ready, 1)

            def rows(i, i_stat):
                j = i % NU
                act.wait_ge(rstd_ready, i_stat + 1)
                if i >= 2:
                    act.wait_ge(xn_turned, i - 1)
                act.activation(ysb[:, i % 2, 0:KPU * P], x_res[:, 0, j * KPU * P:(j + 1) * KPU * P], ACT.Copy,
                               scale=rstd[:, i_stat, 0:1]).then_inc(xn_ready_a, 1)

            def first_split(c, n, i_stat):
                def norm_hi(j):
                    i = n * NU + j
                    act.wait_ge(full_ready, i + 1)
                    act.activation(act_hi[:, KPU * j:KPU * j + KPU, :].rearrange("p k t -> p (k t)"),
                                   zsb[:, i % 2, :], ACT.Copy).then_inc(act_hi_done, 1)

                def before(u):
                    if u + 1 < NU:
                        rows(n * NU + u + 1, i_stat)
                    if u >= 1:
                        norm_hi(u - 1)

                rows(n * NU, i_stat)
                split(c, None, before)
                norm_hi(NU - 1)

            def pre(prev, C, r):
                if prev is None:
                    return
                A_, free = acc(C - 1), acc_free[(C - 1) % 2]
                kind = prev[0]
                if kind == "gate":
                    q = prev[1]
                    if q >= 1:
                        act.wait_ge(h_ready, at(2 * q, r, 2))
                    for t in range(TT):
                        ins = act.activation(ysb[:, t, :], A_[t][:, :], ACT.Silu).then_inc(sig_ready, 1)
                elif kind == "add" and prev[4] is not None:
                    _, dst, n, how, i = prev
                    for t in range(TT):
                        if how == "gated_copy":
                            square(i, t, n, A_[t][:, :])
                        else:
                            wait_read(act, C - 1)
                            d = x_res if dst == "x" else y_acc
                            square(i, t, n, d[:, t, n * CW:(n + 1) * CW])
                elif kind == "value":
                    for t in range(TT):
                        ins = act.activation(vals[prev[1]][:, t, prev[2]:prev[2] + HPC, :].rearrange("p h d -> p (h d)"),
                                             A_[t][:, :], ACT.Copy)
                        if t == TT - 1:
                            ins.then_inc(free, 1)
                elif kind == "keep_a":
                    if prev[1] >= 1:
                        act.wait_ge(glu_ready, 2 * prev[1])
                    for t in range(TT):
                        ins = act.activation(a_keep[:, t, :], A_[t][:, :], ACT.Copy)
                        if t == TT - 1:
                            ins.then_inc(free, 1)
                elif kind == "glu":
                    for t in range(TT):
                        act.activation(zsb[:, t, :], A_[t][:, :], ACT.Sigmoid).then_inc(glu_sig, 1)
                elif kind == "plain":
                    i = TURNS.index(prev)
                    if i >= 1:
                        act.wait_ge(turned, i)
                    for t in range(TT):
                        ins = act.activation(ysb[:, t, :], A_[t][:, :], ACT.Copy)
                        if t == TT - 1:
                            ins.then_inc(free, 1)
                elif kind in ("normed", "kv"):
                    k = HPC if kind == "normed" else NSA_G
                    m = NORMED.index(prev)
                    for t in range(TT):
                        if kind == "kv":
                            act.activation(vals["vs" if prev[1] == "ks" else "vw"][:, t, :, :].rearrange(
                                "p h d -> p (h d)"), A_[t][:, NSA_G * HD:], ACT.Copy)
                        for h in range(k):
                            link(act.activation(zsb[:, t, h * HD:(h + 1) * HD], A_[t][:, h * HD:(h + 1) * HD],
                                                ACT.Square, accum_out=head_ss[:, t * HPC + h:t * HPC + h + 1]))
                    if m >= 1:
                        act.wait_ge(head_sq, m)
                    act.activation(head_std[:, :], head_ss[:, :], ACT.Sqrt, bias=consts[:, 0:1],
                                   scale=1.0 / HD).then_inc(head_std_ready, 1)

            def post(prev, C, r):
                if prev is None or prev[0] in ("value", "keep_a", "add", "gate"):
                    return
                if prev[0] == "up":
                    q = prev[1]
                    k0 = at(prev[2], r, 4)
                    for t in range(TT):
                        act.wait_ge(h_turned, at(2 * q + t + 1, r, 2))
                        act.activation(mid_hi[:, bass.ds(k0, 4), t * P:(t + 1) * P],
                                       TURN[t][:, :].rearrange("p (k t) -> p k t", t=P), ACT.Copy).then_inc(
                            mid_hi_done, 1)
                    return
                i = TURNS.index(prev)
                act.wait_ge(turned, i + 1)
                keep(act, prev, 0, lambda o, s, g: act.activation(o, s, ACT.Copy, scale=g), turn_out_a)

            def split(c, r, before=lambda u: None):
                for u in range(c["nu"]):
                    before(u)
                    R, U = c["R"] + u, c["U"] + u
                    act.wait_ge(raw_loaded[R % RAW_SLOTS], at(16 * (R // RAW_SLOTS + 1), r, 16 * 2 * c["nu"] // 4))
                    if U >= SPLIT_SLOTS:
                        act.wait_ge(parts_used, at(U - SPLIT_SLOTS + 1, r, 2 * c["nu"]))
                    act.activation(w_hi[:, U % SPLIT_SLOTS].rearrange("p k n -> p (k n)"),
                                   raw[:, R % RAW_SLOTS].rearrange("p k n -> p (k n)"), ACT.Copy).then_inc(hi_done, 1)
                    if u == 3:
                        pre(c["prev"], c["C"], r)
                post(c["prev"], c["C"], r)

            def attend(j0, j1, cost, prob, probT, row_min, row_sum, hook=lambda i: None):
                for i in range(j0, j1 + 3):
                    if i < j1:
                        for t, c0, n in ((0, 0, P), (1, P, T)):
                            act.wait_ge(reduced, 2 * i + t + 1)
                            if i - j0 >= 2:
                                act.wait_ge(p_turned, i - 1)
                            act.activation(prob[:, i % 2, c0:c0 + n], cost[:, i % 2, c0:c0 + n], ACT.Exp,
                                           bias=row_min[:, i % 2, t:t + 1], scale=-1.0,
                                           accum_out=row_sum[:, i % 2, t:t + 1]).then_inc(exped, 1)
                    if j0 + 2 <= i < j1 + 2:
                        j = i - 2
                        act.wait_ge(p_turned, j + 1)
                        if j - j0 >= 2:
                            act.wait_ge(pv_done, j - 1)
                        act.activation(probT[:, j % 2, :], bank[2 + j % 2][:, 0:TAB], ACT.Copy).then_inc(p_out, 1)
                    if i >= j0 + 3 and JOBS[i - 3]["last"]:
                        b = JOBS[i - 3]
                        act.wait_ge(pv_done, i - 2)
                        act.activation(mid_hi[:, b["chunk"], :], bank[4 + b["o"] % 2][:, 0:T], ACT.Copy).then_inc(
                            o_hi, 1)
                    hook(i)

            act.wait_ge(tables_made, 1)
            for t in range(TT):
                act.wait_ge(x_loaded[t], 16)
                for q in range(D // CW):
                    square(0, t, q, x_res[:, t, q * CW:(q + 1) * CW])
            root(0)
            act.wait_ge(small_loaded, 32)
            act.activation(ws[:, :, 0, :], w_small[:, :, :], ACT.Copy).then_inc(ws_split_hi, 1)
            act.wait_ge(cols_ready, 2)
            act.activation(c_act[:, :], cols[:, 64:64 + KD], ACT.Silu).then_inc(c_ready, 1)
            first_split(S_IN1[0], 0, 0)
            run(S_IN1[1:], act, split)
            act.wait_ge(parts_used, LAST_U["in1"])
            pre(LAST1, C_IN1, None)
            post(LAST1, C_IN1, None)
            act.wait_ge(lf_d, 1)
            link(act.activation(lf[:, 2], lf[:, 1], ACT.Exp, scale=-1.0))
            act.activation(lf[:, 3], lf[:, 2], ACT.Ln, bias=consts[:, 2:3]).then_inc(lf_a, 1)
            act.activation(gate_e[:, :, :], small[:, :, FOX_H:], ACT.Exp, scale=-1.0).then_inc(gate_exp, 1)
            act.wait_ge(dec_zero, 1)
            act.wait_ge(lf_cum, 1)
            for q in range(FOX_H // 2):
                ins = act.activation(dec_l[0:1, 2 * q:2 * q + 2, :].rearrange("p h t -> p (h t)"), bank[q][0:1, :],
                                     ACT.Copy)
            ins.then_inc(dec_a, 1)
            act.wait_ge(cmp_used, 4)
            link(act.activation(kcn[:, :], MISC[0][0:64, 0:HD], ACT.Square, accum_out=kc_ss[:, 0:1]))
            act.activation(kc_ss[:, 1:2], kc_ss[:, 0:1], ACT.Sqrt, bias=consts[0:64, 0:1],
                           scale=1.0 / HD).then_inc(kc_std, 1)
            act.wait_ge(cmp_shift, 1)
            act.activation(cmp_prob[:, :, :], cmp_cost[:, :, :], ACT.Exp, scale=-1.0).then_inc(cmp_exp, 1)
            act.wait_ge(cmp_pT, 1)
            act.activation(cmp_probT[:, :, :].rearrange("p h t -> p (h t)"), MISC[0][:, :], ACT.Copy).then_inc(
                cmp_pT_out, 1)
            attend(0, N_JOB1, cost1, prob1, probT1, row_min1, row_sum1)
            run(S_OUT1, act, split)
            pre(LAST_OUT1, LAST_C["out1"], None)
            root(1)
            first_split(S_FFN1[0], 1, 1)
            run(S_FFN1[1:], act, split)
            pre(LAST_FFN1, LAST_C["ffn1"], None)
            root(2)
            first_split(S_IN2[0], 2, 2)
            run(S_IN2[1:], act, split)
            act.wait_ge(parts_used, LAST_U["in2"])
            pre(LAST2, LAST_C["in2"], None)
            post(LAST2, LAST_C["in2"], None)
            attend(N_JOB1, len(JOBS), cost2, prob2, probT2, row_min2, row_sum2)
            act.wait_ge(ln_d, 1)
            act.activation(conv_sq[:, :, :], convT[:, :, :], ACT.Square).then_inc(ln_sq, 1)
            act.wait_ge(ln_var, 1)
            act.activation(conv_rs[:, :], MISC[1][:, 0:T], ACT.Sqrt, bias=consts[:, 1:2],
                           scale=1.0 / CONV_CH).then_inc(ln_std, 1)
            act.wait_ge(ln_y, 1)
            for g in range(CONV_G):
                link(act.activation(convT[:, g, :], convT[:, g, :], ACT.Silu, bias=cols[:, 102 + g:103 + g],
                                    scale=cols[:, 94 + g:95 + g]))
            act.activation(mid_hi[:, CONV_G:, :], convT[:, :, :], ACT.Copy).then_inc(ln_hi, 1)
            run(S_OUT2, act, split)
            act.wait_ge(parts_used, LAST_U["out2"])
            pre(LAST_OUT2, LAST_C["out2"], None)
            root(3)
            for t in range(TT):
                for q in range(D // CW):
                    act.wait_ge(x_updated, 4 * t + q + 1)
                    square(4, t, q, x_res[:, t, q * CW:(q + 1) * CW])
            root(4)
            first_split(S_FFN2[0], 3, 4)
            run(S_FFN2[1:], act, split)
            pre(LAST_FFN2, LAST_C["ffn2"], None)
            root(5)

        @block.vector
        def _(dve):
            chain = [0]

            def link(ins):
                chain[0] += 1
                ins.then_inc(chain_d, 1)
                dve.wait_ge(chain_d, chain[0])

            def mean_root(i):
                dve.wait_ge(ss_act, squares(i + 1))
                dve.tensor_reduce(mean_sq[:, i, :], sq_sum[:, i, :, :], AX.X, ALU.add).then_inc(ms_ready, 1)
                dve.wait_ge(std_ready, i + 1)
                dve.reciprocal(rstd[:, i, :], std[:, i, :]).then_inc(rstd_ready, 1)
                dve.wait_ge(rstd_ready, i + 1)

            def rows(i, i_stat):
                j = i % NU
                if i >= 2:
                    dve.wait_ge(xn_turned, i - 1)
                dve.tensor_scalar(ysb[:, i % 2, KPU * P:2 * KPU * P], x_res[:, 1, j * KPU * P:(j + 1) * KPU * P],
                                  rstd[:, i_stat, 1:2], None, ALU.mult).then_inc(xn_ready_d, 1)

            def first_split(c, n, i_stat):
                def before(u):
                    i = n * NU + u
                    if u + 1 < NU:
                        rows(i + 1, i_stat)
                    dve.wait_ge(xn_turned, i + 1)
                    if i >= 2:
                        dve.wait_ge(act_hi_done, i - 1)
                        dve.wait_ge(act_lo_done, i - 1)
                    for cc in range(KPU):
                        k = KPU * u + cc
                        o, s = zsb[:, i % 2, cc * T:(cc + 1) * T], TURN[i % 2][:, cc * T:(cc + 1) * T]
                        if n < 2:
                            ins = dve.tensor_scalar(o, s, norm_scale[:, n, k:k + 1], None, ALU.mult)
                        else:
                            ins = dve.tensor_scalar(o, s, norm_scale[:, n, k:k + 1], norm_shift[:, n, k:k + 1],
                                                    ALU.mult, ALU.add)
                    ins.then_inc(full_ready, 1)

                rows(n * NU, i_stat)
                split(c, None, before, lambda u: low(n * NU + u, u))

            def low(i, j):
                dve.wait_ge(full_ready, i + 1)
                dve.wait_ge(act_hi_done, i + 1)
                dve.tensor_tensor(act_lo[:, KPU * j:KPU * j + KPU, :].rearrange("p k t -> p (k t)"), zsb[:, i % 2, :],
                                  act_hi[:, KPU * j:KPU * j + KPU, :].bitcast(F32).rearrange("p k t -> p (k t)"),
                                  ALU.subtract).then_inc(act_lo_done, 1)

            def pre(prev, C, r):
                if prev is None:
                    return
                A_, free = acc(C - 1), acc_free[(C - 1) % 2]
                kind = prev[0]
                if kind == "up":
                    q = prev[1]
                    dve.wait_ge(sig_ready, at(2 * q + 2, r, 2))
                    if q >= 1:
                        dve.wait_ge(h_turned, at(2 * q, r, 2))
                    for t in range(TT):
                        dve.tensor_tensor(zsb[:, t, :], A_[t][:, :], ysb[:, t, :], ALU.mult).then_inc(h_ready, 1)
                    return
                if kind == "add":
                    _, dst, n, how, i = prev
                    d = x_res if dst == "x" else y_acc
                    cols_n = slice(n * CW, (n + 1) * CW)
                    for t in range(TT):
                        o = d[:, t, cols_n]
                        if how == "gated_copy":
                            dve.wait_ge(ss_act, squares(i) + TT * n + t + 1)
                            ins = dve.tensor_tensor(o, A_[t][:, :], gate_row1[:, cols_n], ALU.mult)
                        elif how == "copy":
                            ins = dve.tensor_copy(o, A_[t][:, :])
                        else:
                            ins = dve.tensor_tensor(o, A_[t][:, :], o, ALU.add)
                        if t == TT - 1:
                            ins.then_inc(free, 1)
                    if how == "gated_sum":
                        for t in range(TT):
                            dve.wait_ge(ss_act, squares(i) + TT * n + t + 1)
                            o = d[:, t, cols_n]
                            dve.tensor_tensor(o, o, gate_row2[:, cols_n], ALU.mult).then_inc(y_gated, 1)
                    return
                if kind in ("normed", "kv"):
                    k = HPC if kind == "normed" else NSA_G
                    m, i = NORMED.index(prev), TURNS.index(prev)
                    dve.wait_ge(head_std_ready, m + 1)
                    dve.reciprocal(head_rstd[:, :], head_std[:, :]).then_inc(head_sq, 1)
                    dve.wait_ge(head_sq, m + 1)
                    if i >= 1:
                        dve.wait_ge(turned, i)
                    for t in range(TT):
                        ins = dve.tensor_tensor(
                            ysb[:, t, 0:k * HD].rearrange("p (h d) -> p h d", d=HD),
                            A_[t][:, 0:k * HD].rearrange("p (h d) -> p h d", d=HD),
                            head_rstd[:, t * HPC:t * HPC + k].unsqueeze(2).to_broadcast([P, k, HD]), ALU.mult)
                        if t == TT - 1:
                            ins.then_inc(free, 1)
                elif kind == "glu":
                    i = TURNS.index(prev)
                    dve.wait_ge(turned, i)
                    for t in range(TT):
                        dve.wait_ge(glu_sig, 2 * prev[1] + t + 1)
                        dve.tensor_tensor(ysb[:, t, :], zsb[:, t, :], a_keep[:, t, :], ALU.mult).then_inc(glu_ready, 1)

            def post(prev, C, r):
                if prev is None or prev[0] in ("value", "keep_a", "add", "gate"):
                    return
                if prev[0] == "up":
                    q = prev[1]
                    k0 = at(prev[2], r, 4)
                    for t in range(TT):
                        dve.wait_ge(mid_hi_done, at(2 * q + t + 1, r, 2))
                        dve.tensor_tensor(mid_lo[:, bass.ds(k0, 4), t * P:(t + 1) * P],
                                          TURN[t][:, :].rearrange("p (k t) -> p k t", t=P),
                                          mid_hi[:, bass.ds(k0, 4), t * P:(t + 1) * P].bitcast(F32),
                                          ALU.subtract).then_inc(mid_lo_done, 1)
                    return
                dve.wait_ge(turned, TURNS.index(prev) + 1)
                keep(dve, prev, 1, lambda o, s, g: dve.tensor_scalar(o, s, g, None, ALU.mult), turn_out_d)

            conv_n, conv_at = [0], {}

            def conv_step(k, g):
                if k == 0:
                    dve.wait_ge(turn_out_a, TURNS.index(("glu", g // 4)) + 1)
                    dve.wait_ge(turn_out_d, TURNS.index(("glu", g // 4)) + 1)
                else:
                    dve.wait_ge(conv_dve, conv_at[g])
                conv_at[g] = conv_n[0] + 1
                src, wk = uT[:, g, k:k + T], conv_w_cols[:, g, k:k + 1]
                if k == 0:
                    ins = dve.tensor_scalar(convT[:, g, :], src, wk, cols[:, 86 + g:87 + g], ALU.mult, ALU.add)
                else:
                    ins = dve.scalar_tensor_tensor(convT[:, g, :], src, wk, convT[:, g, :], ALU.mult, ALU.add)
                ins.then_inc(conv_dve, 1)
                conv_n[0] += 1

            def ada_step(c, r, i):
                a = c["ada"]
                unit = a["A"] + i
                dve.wait_ge(ada_loaded[unit % 2], at(16 * (unit // 2 + 1), r, 64))
                for kk in range(KPU):
                    k = a["half"] * 8 + 2 * i + kk
                    w = ada_raw[:, unit % 2, kk, :]
                    cc = c_act[:, k:k + 1]
                    if k == 0:
                        if a["blk"] >= 1:
                            dve.wait_ge(ada_summed, at(a["blk"], r, 1))
                        ins = dve.tensor_scalar(ada_acc[:, :], w, cc, None, ALU.mult)
                    else:
                        dve.wait_ge(ada_used, at(2 * unit + kk, r, 16))
                        ins = dve.scalar_tensor_tensor(ada_acc[:, :], w, cc, ada_acc[:, :], ALU.mult, ALU.add)
                    ins.then_inc(ada_used, 1)

            def ada_keep(a, r):
                dve.wait_ge(ada_summed, at(a["blk"] + 1, r, 1))
                if a["kind"] == "col":
                    j0 = a["dst"]
                    dve.tensor_copy(mod_cols[:, bass.ds(at(j0, r, 4), 4)], MISC[0][:, 0:4]).then_inc(ada_out, 1)
                else:
                    row = gate_row1 if a["kind"] == "row" else gate_row2
                    o = row[:, bass.ds(at(a["dst"], r, CW), CW)]
                    dve.tensor_tensor(o, MISC[0][:, :], o, ALU.mult).then_inc(ada_out, 1)

            def split(c, r, before=lambda u: None, after=lambda u: None):
                nu = c["nu"]
                conv = list(c.get("conv", []))
                for u in range(nu):
                    before(u)
                    R, U = c["R"] + u, c["U"] + u
                    dve.wait_ge(hi_done, at(U + 1, r, 2 * nu))
                    if U >= SPLIT_SLOTS:
                        dve.wait_ge(parts_used, at(U - SPLIT_SLOTS + 1, r, 2 * nu))
                    dve.tensor_tensor(w_lo[:, U % SPLIT_SLOTS].rearrange("p k n -> p (k n)"),
                                      raw[:, R % RAW_SLOTS].rearrange("p k n -> p (k n)"),
                                      w_hi[:, U % SPLIT_SLOTS].bitcast(F32).rearrange("p k n -> p (k n)"),
                                      ALU.subtract).then_inc(lo_done, 1)
                    after(u)
                    for _ in range(-(-len(conv) // (nu - u))):
                        conv_step(*conv.pop(0))
                    if c["ada"] and u in (1, 2, 5, 6):
                        ada_step(c, r, (1, 2, 5, 6).index(u))
                    if u == 2 and c["keep"]:
                        ada_keep(c["keep"], r)
                    if u == 3:
                        pre(c["prev"], c["C"], r)
                    if c is S_IN1[SMALL_OUT] and u == 3:
                        dve.wait_ge(small_mm, 1)
                        dve.tensor_copy(ysb[0:2 * N_SMALL, 0, 0:T], MISC[0][0:2 * N_SMALL, 0:T]).then_inc(
                            small_folded, 1)
                    if c is S_IN1[SMALL_OUT + 1] and u == 3:
                        dve.wait_ge(small_mm, 2)
                        dve.tensor_copy(small[:, :, :].rearrange("p t n -> p (t n)"),
                                        MISC[0][:, 0:TT * N_SMALL]).then_inc(small_out, 1)
                if c["ada"] and nu < 7:
                    ada_step(c, r, 3)
                post(c["prev"], c["C"], r)

            def attend(j0, j1, cost, prob, row_min, row_sum, row_inv, hook=lambda i: None):
                for i in range(j0, j1 + 3):
                    if i < j1:
                        b = JOBS[i]
                        tab = {"mask": lambda: mask[:, :], "mask2": lambda: mask2[:, :],
                               "alibi": lambda: alibi[:, b["h"], :]}[b["table"]]()
                        dve.wait_ge(scored, i + 1)
                        if i - j0 >= 2:
                            dve.wait_ge(exped, 2 * (i - 1))
                        for t, c0, n in ((0, 0, P), (1, P, T)):
                            dve.tensor_tensor_reduce(cost[:, i % 2, c0:c0 + n], bank[i % 2][:, c0:c0 + n],
                                                     tab[:, T - n:T], 1.0, 3.0e38, ALU.add, ALU.min,
                                                     row_min[:, i % 2, t:t + 1]).then_inc(reduced, 1)
                    if j0 < i <= j1:
                        j = i - 1
                        b = JOBS[j]
                        dve.wait_ge(exped, 2 * j + 2)
                        link(dve.reciprocal(row_inv[:, j % 2, :], row_sum[:, j % 2, :]))
                        if b["gate"] is not None:
                            link(dve.tensor_tensor(row_inv[:, j % 2, :], row_inv[:, j % 2, :],
                                                   gates[:, :, b["gate"]], ALU.mult))
                        for t, c0, n in ((0, 0, P), (1, P, T)):
                            dve.tensor_scalar(prob[:, j % 2, c0:c0 + n], prob[:, j % 2, c0:c0 + n],
                                              row_inv[:, j % 2, t:t + 1], None, ALU.mult).then_inc(scaled, 1)
                    if i >= j0 + 3 and JOBS[i - 3]["last"]:
                        b = JOBS[i - 3]
                        dve.wait_ge(o_hi, b["o"] + 1)
                        dve.tensor_tensor(mid_lo[:, b["chunk"], :], bank[4 + b["o"] % 2][:, 0:T],
                                          mid_hi[:, b["chunk"], :].bitcast(F32), ALU.subtract).then_inc(o_lo, 1)
                    hook(i)

            def gated_add(i_stat, base):
                for t in range(TT):
                    for q in range(D // CW):
                        cols_q = slice(q * CW, (q + 1) * CW)
                        dve.scalar_tensor_tensor(x_res[:, t, cols_q], y_acc[:, t, cols_q], rstd[:, i_stat, t:t + 1],
                                                 x_res[:, t, cols_q], ALU.mult, ALU.add).then_inc(x_updated, 1)
                dve.wait_ge(x_updated, base + TT * (D // CW))

            dve.wait_ge(cols_turned, 1)
            dve.tensor_copy(cols[:, 0:110], MISC[0][:, 0:110]).then_inc(cols_ready, 1)
            dve.tensor_copy(pos_cols[:, :], MISC[0][:, 128:192])
            dve.tensor_copy(conv_w_cols[:, :, 0:CONV_K],
                            MISC[1][:, 0:32 * CONV_G].rearrange("p (g k) -> p g k", k=32)[:, :, 0:CONV_K]).then_inc(
                cols_ready, 1)
            dve.wait_ge(cols_ready, 2)
            dve.tensor_scalar(q_gain[:, 0:1], cols[:, 80:81], -SCALE, None, ALU.mult)
            dve.tensor_scalar(q_gain[:, 1:2], cols[:, 82:83], -SCALE, None, ALU.mult)
            link(dve.tensor_copy(norm_scale[:, 0:2, :].rearrange("p n k -> p (n k)"), cols[:, 0:2 * KD]))
            dve.wait_ge(tables_made, 1)
            mean_root(0)
            dve.wait_ge(ws_split_hi, 1)
            dve.tensor_tensor(ws[:, :, 1, :], w_small[:, :, :], ws[:, :, 0, :].bitcast(F32), ALU.subtract).then_inc(
                ws_split, 1)
            first_split(S_IN1[0], 0, 0)
            run(S_IN1[1:], dve, split)
            pre(LAST1, C_IN1, None)
            post(LAST1, C_IN1, None)
            link(dve.tensor_tensor(lf[:, 0], small[:, :, 0:FOX_H],
                                   forget_bias[:, :].unsqueeze(1).to_broadcast([P, TT, FOX_H]), ALU.add))
            dve.scalar_tensor_tensor(lf[:, 1], lf[:, 0], -1.0, lf[:, 0], ALU.mult, ALU.max).then_inc(lf_d, 1)
            link(dve.tensor_scalar(lf[:, 4], lf[:, 0], 0.0, None, ALU.min))
            dve.wait_ge(lf_a, 1)
            link(dve.tensor_tensor(lf[:, 5], lf[:, 4], lf[:, 3], ALU.subtract))
            dve.wait_ge(tables_made, 2)
            dve.wait_ge(blk_zero, 1)
            dve.tensor_scalar(lf_cols[:, :, :, 0], lf[:, 5], -1.0, None, ALU.mult)
            dve.tensor_copy(lf_cols[:, :, :, 32], lf[:, 5]).then_inc(lf_d, 1)
            for kind, (blk, src) in enumerate(((blk_k, "kc"), (blk_v, "vc"))):
                dve.wait_ge(blk_zero, kind + 2)
                for g in range(NSA_G):
                    for j in range(2):
                        tok = heads[src][:, g, CMP_STRIDE * j:CMP_STRIDE * (j + N_CMP)].rearrange(
                            "p (n l) -> p l n", l=CMP_STRIDE)
                        pc = pos_cols[:, kind * CMP_BLOCK + 16 * j:kind * CMP_BLOCK + 16 * j + 16]
                        ins = dve.tensor_tensor(blk[:, 16 * j:16 * j + 16, 32 * g:32 * g + N_CMP], tok,
                                                pc.unsqueeze(2).to_broadcast([P, 16, N_CMP]), ALU.add)
                ins.then_inc(blk_ready, 1)
            dve.wait_ge(gate_exp, 1)
            link(dve.tensor_scalar(gate_e[:, :, :], gate_e[:, :, :], 1.0, None, ALU.add))
            dve.reciprocal(gates[:, :, :], gate_e[:, :, :]).then_inc(gates_ready, 1)
            dve.wait_ge(dec_zero, 1)
            dve.wait_ge(lf_cum, 1)
            for q in range(FOX_H // 2):
                ins = dve.tensor_copy(dec_r[32:33, 2 * q:2 * q + 2, :].rearrange("p h t -> p (h t)"),
                                      bank[q][32:33, :])
            ins.then_inc(dec_d, 1)
            dve.wait_ge(kc_std, 1)
            link(dve.reciprocal(kc_ss[:, 2:3], kc_ss[:, 1:2]))
            dve.tensor_scalar(kcn[:, :], MISC[0][0:64, 0:HD], kc_ss[:, 2:3], None, ALU.mult).then_inc(kc_n, 1)
            dve.wait_ge(cmp_used, 8)
            for q in range(4):
                for g in range(NSA_G):
                    ins = dve.tensor_copy(vcmp[32 * q:32 * q + 16, g, :], MISC[1][32 * g:32 * g + 16, 0:HD])
            ins.then_inc(vc_ready, 1)
            dve.wait_ge(kc_turned, 1)
            dve.tensor_scalar(kcmpT[:, :], TURN[0][:, 0:64], cols[:, 83:84], None, ALU.mult).then_inc(kc_ready, 1)
            dve.wait_ge(cmp_scored, 1)
            link(dve.tensor_tensor(cmp_cost[:, :, :].rearrange("p h n -> p (h n)"), MISC[1][:, :],
                                   cmp_tab[:, :, :, :].rearrange("p t h n -> p (t h n)"), ALU.add))
            link(dve.tensor_reduce(cmp_min[:, :], cmp_cost[:, :, :], AX.X, ALU.min))
            dve.tensor_tensor(cmp_cost[:, :, :], cmp_cost[:, :, :],
                              cmp_min[:, :].unsqueeze(2).to_broadcast([P, TT * NSA_H, 32]),
                              ALU.subtract).then_inc(cmp_shift, 1)
            dve.wait_ge(cmp_exp, 1)
            probs4 = cmp_prob[:, :, :].rearrange("p (t h) n -> p t h n", t=TT)
            link(dve.tensor_tensor(probs4, probs4, cmp_ok[:, :, :].unsqueeze(2).to_broadcast([P, TT, NSA_H, 32]),
                                   ALU.mult))
            link(dve.tensor_reduce(cmp_sum[:, :], cmp_prob[:, :, :], AX.X, ALU.add))
            link(dve.tensor_scalar(cmp_sum[:, :], cmp_sum[:, :], 1e-30, None, ALU.max))
            link(dve.reciprocal(cmp_min[:, :], cmp_sum[:, :]))
            dve.wait_ge(gates_ready, 1)
            link(dve.tensor_tensor(cmp_min[:, :].rearrange("p (t h) -> p t h", t=TT),
                                   cmp_min[:, :].rearrange("p (t h) -> p t h", t=TT),
                                   gates[:, :, :].rearrange("p t (h b) -> p t h b", b=3)[:, :, :, 0], ALU.mult))
            dve.tensor_tensor(cmp_prob[:, :, :], cmp_prob[:, :, :],
                              cmp_min[:, :].unsqueeze(2).to_broadcast([P, TT * NSA_H, 32]),
                              ALU.mult).then_inc(cmp_p, 1)
            attend(0, N_JOB1, cost1, prob1, row_min1, row_sum1, row_inv1)
            dve.wait_ge(gate_loaded, 16)
            dve.wait_ge(c_ready, 1)
            run(S_OUT1, dve, split)

            def last_add(prev, C, U, kept=None):
                dve.wait_ge(parts_used, U)
                pre(prev, C, None)
                if kept:
                    ada_keep(kept, None)
                wait_read(dve, C - 1)

            last_add(LAST_OUT1, LAST_C["out1"], S_OUT1[-1]["U"] + NU, KEEP_OUT1)
            mean_root(1)
            first_split(S_FFN1[0], 1, 1)
            run(S_FFN1[1:], dve, split)
            last_add(LAST_FFN1, LAST_C["ffn1"], S_FFN1[-1]["U"] + S_FFN1[-1]["nu"], KEEP_FFN1)
            mean_root(2)
            dve.wait_ge(ada_out, 16)
            for i in range(2):
                sh, sc = 2 * i * KD, (2 * i + 1) * KD
                dve.tensor_copy(norm_shift[:, 2 + i, :], mod_cols[:, sh:sh + KD])
                link(dve.scalar_tensor_tensor(norm_scale[:, 2 + i, :], mod_cols[:, sc:sc + KD], 1.0,
                                              cols[:, (2 + i) * KD:(3 + i) * KD], ALU.add, ALU.mult))
            dve.wait_ge(uT_zero, 1)
            first_split(S_IN2[0], 2, 2)
            run(S_IN2[1:], dve, split)
            dve.wait_ge(parts_used, LAST_U["in2"])
            pre(LAST2, LAST_C["in2"], None)
            post(LAST2, LAST_C["in2"], None)
            attend(N_JOB1, len(JOBS), cost2, prob2, row_min2, row_sum2, row_inv2)
            dve.wait_ge(ln_sum, 1)
            link(dve.tensor_scalar(conv_mu[:, :], MISC[0][:, 0:T], 1.0 / CONV_CH, None, ALU.mult))
            dve.tensor_tensor(convT[:, :, :], convT[:, :, :],
                              conv_mu[:, :].unsqueeze(1).to_broadcast([P, CONV_G, T]), ALU.subtract).then_inc(ln_d, 1)
            dve.wait_ge(ln_std, 1)
            link(dve.reciprocal(conv_rs[:, :], conv_rs[:, :]))
            dve.tensor_tensor(convT[:, :, :], convT[:, :, :],
                              conv_rs[:, :].unsqueeze(1).to_broadcast([P, CONV_G, T]), ALU.mult).then_inc(ln_y, 1)
            dve.wait_ge(ln_hi, 1)
            dve.tensor_tensor(mid_lo[:, CONV_G:, :], convT[:, :, :], mid_hi[:, CONV_G:, :].bitcast(F32),
                              ALU.subtract).then_inc(ln_lo, 1)
            dve.wait_ge(ln_lo, 1)
            run(S_OUT2, dve, split)
            last_add(LAST_OUT2, LAST_C["out2"], LAST_U["out2"])
            mean_root(3)
            gated_add(3, 0)
            mean_root(4)
            dve.wait_ge(gate_loaded, 32)
            first_split(S_FFN2[0], 3, 4)
            run(S_FFN2[1:], dve, split)
            last_add(LAST_FFN2, LAST_C["ffn2"], S_FFN2[-1]["U"] + S_FFN2[-1]["nu"])
            mean_root(5)
            dve.wait_ge(y_gated, TT * (D // CW))
            gated_add(5, TT * (D // CW))


INPUTS = ["x", "attn_norm", "w_in", "fox_forget_bias", "fox_q_norm", "fox_k_norm", "nsa_q_norm", "cmp_k_norm",
          "slc_k_norm", "win_k_norm", "cmp_pos_k", "cmp_pos_v", "cmp_w_k", "cmp_w_v", "w_out", "ffn_norm",
          "w_gate", "w_up", "w_down", "c_2", "ada_w_2", "ada_b_2", "mix_pre_g_2", "mix_post_g_2", "w_in_2",
          "conv_w_2", "conv_b_2", "conv_ln_g_2", "conv_ln_b_2", "w_out_2", "ffn_pre_g_2", "ffn_post_g_2",
          "w_gate_2", "w_up_2", "w_down_2"]


def kernel(**inputs):
    import numpy as np
    import concourse.bacc as bacc
    from concourse import mybir
    from concourse.bass_utils import run_bass_kernel_spmd

    nc = bacc.Bacc("TRN2", target_bir_lowering=False, num_devices=1)
    arrays, io = {}, {}
    for name in INPUTS:
        a = np.ascontiguousarray(inputs[name])
        arrays[f"in_{name}"] = a
        io[name] = nc.dram_tensor(f"in_{name}", a.shape, mybir.dt.from_np(a.dtype), kind="ExternalInput").ap()
    shape = inputs["x"].shape
    out = nc.dram_tensor("out_x", shape, mybir.dt.float32, kind="ExternalOutput").ap()
    build_two_blocks(nc, io, out)
    r = run_bass_kernel_spmd(nc, [arrays], core_ids=[0])
    return r.results[0]["out_x"]
```

```python
def build_two_blocks(nc, io, out):
    import concourse.bass as bass
    from concourse import mybir
    from contextlib import ExitStack

    F32, F32R = mybir.dt.float32, mybir.dt.float32r
    ACT = mybir.ActivationFunctionType
    ALU = mybir.AluOpType
    AX = mybir.AxisListType
    P = 128

    T, D = io["x"].shape[1], io["x"].shape[2]
    TT = T // P
    KD = D // P
    FF = io["w_gate"].shape[2]
    HD = io["fox_q_norm"].shape[1]
    FOX_H = io["fox_forget_bias"].shape[1]
    NSA_H, NSA_G = 8, 2
    HPG = NSA_H // NSA_G
    CW = 512
    HPC = CW // HD
    KPU = 2
    NU = KD // KPU
    RAW_SLOTS, SPLIT_SLOTS = 4, 4
    SCALE = HD ** -0.5
    CMP_STRIDE, CMP_BLOCK = 16, io["cmp_pos_k"].shape[1]
    N_CMP = T // CMP_STRIDE - 1
    CONV_K, CONV_CH = io["conv_w_2"].shape[1], io["conv_w_2"].shape[2]
    CONV_G = CONV_CH // P
    BIG = 1e30
    TAB = T + P

    def wview(name):
        return io[name][0].rearrange("(k p) n -> p k n", p=P)

    W = {n: wview(n) for n in ("w_in", "w_out", "w_gate", "w_up", "w_down",
                               "w_in_2", "w_out_2", "w_gate_2", "w_up_2", "w_down_2", "ada_w_2")}

    def at(base, r, stride):
        return base if r is None else r * stride + base

    pos = {"C": 0, "U": 0, "R": 0, "A": 0}

    pending = []

    def chunk(w, n0, st, prev=None, k0=0, nu=NU, n_step=0, ada=None, **more):
        c = dict(w=w, n0=n0, n_step=n_step, st=st, prev=prev, k0=k0, nu=nu, C=pos["C"], U=pos["U"],
                 R=pos["R"], ada=None, keep=pending.pop() if pending else None, **more)
        if ada is not None and ada["half"] == 1:
            pending.append(dict(kind=ada["kind"], dst=ada["dst"], blk=ada["blk"]))
        if ada is not None:
            c["ada"] = dict(ada, A=pos["A"])
            pos["A"] += 4
        pos["C"] += 1
        pos["U"] += nu
        pos["R"] += nu
        return c

    o_ff = 3 * FOX_H * HD
    o_qn = o_ff + FOX_H
    o_kv = o_qn + NSA_H * HD
    o_gt = o_kv + 6 * NSA_G * HD
    N_SMALL = FOX_H + 3 * NSA_H
    IN1 = [(0, ("normed", "fq", 0)), (CW, ("normed", "fq", 4)), (2 * CW, ("normed", "fk", 0)),
           (3 * CW, ("normed", "fk", 4)), (4 * CW, ("value", "fv", 0)),
           (o_qn, ("normed", "nq", 0)), (o_qn + CW, ("normed", "nq", 4)), (o_kv, ("plain", "kcvc", 0)),
           (o_kv + CW, ("kv", "ks", 0)), (o_kv + 2 * CW, ("kv", "kw", 0)),
           (5 * CW, ("value", "fv", 4))]
    S_IN1 = []
    prev = None
    for n0, cons in IN1:
        S_IN1.append(chunk("w_in", n0, "act", prev))
        prev = cons
    LAST1 = prev
    SMALL_OUT = 5
    assert IN1[SMALL_OUT - 1][1][0] == "value"
    R_CMP = pos["R"]
    N_CMPU = 2 * 4
    ADA_AT = (1, 2, 5, 6)
    ADA_LATE = (4, 5, 6, 7)
    EARLY = 3
    pos["R"] += N_CMPU
    U_CMP = pos["U"]

    ada_blk = [0]

    def ada_pair(kind, col, dst, step=0, n=1):
        b = ada_blk[0]
        ada_blk[0] += n
        return [dict(kind=kind, col=col, dst=dst, blk=b, half=h, step=step) for h in range(2)]

    def out_pairs(w, dst, prev, ada, first):
        got = []
        for p in range(2):
            a = ada[p] or [None, None]
            for h in range(2):
                n = 2 * p + h
                got.append(chunk(w, n * CW, "mid", prev, ada=a[h], first=first if n == 0 else None))
                prev = ("add", dst, n, *(("sum", 1) if dst == "x" else ("gated_copy", 3)))
        return got, prev

    S_OUT1, prev = out_pairs("w_out", "x", None,
                             [ada_pair("row", 4 * CW * 2, 0), ada_pair("row", 4 * CW * 2 + CW, CW)], "mix1")
    LAST_OUT1 = prev
    KEEP_OUT1 = pending.pop()

    def ffn(tag, dst, ada_list, f):
        steps, prev, pair0 = [], None, f * (FF // CW)
        groups = [4, 4, 3]
        assert sum(groups) * CW == FF
        done = 0
        al = list(ada_list)
        for g, n in enumerate(groups):
            def pair(j, trips, prev):
                a = [None, None]
                if al and al[0] is None:
                    al.pop(0)
                elif al:
                    blocks = [al.pop(0) for _ in range(min(trips, len(al)))]
                    assert len(blocks) == trips
                    st = blocks[1][1] - blocks[0][1] if trips > 1 else 0
                    assert all(blocks[q + 1][1] - blocks[q][1] == st and blocks[q + 1][0] == blocks[q][0]
                               for q in range(trips - 1))
                    a = ada_pair(blocks[0][0], blocks[0][1], blocks[0][2], st, trips)
                col = (done + j) * CW
                q = pair0 + done + j
                a1 = chunk("w_gate" + tag, col, "act", prev, n_step=CW, ada=a[0])
                a2 = chunk("w_up" + tag, col, "act", ("gate", q), n_step=CW, ada=a[1])
                if trips > 1:
                    for k, m in (("C", 2), ("U", 2 * NU), ("R", 2 * NU)):
                        pos[k] += m * (trips - 1)
                    if a[0]:
                        pos["A"] += 8 * (trips - 1)
                        pending[0]["blk"] += trips - 1
                        pending[0]["dst"] += (trips - 1) * (4 if a[0]["kind"] == "col" else CW)
                    else:
                        assert a1["keep"] is None
                return [a1, a2], ("up", q, 4 * j)
            body, nxt = pair(0, 1, prev)
            steps += body
            j = 1
            while j < n:
                trips = 1
                while j + trips < n and (not al or pending and (len(al) > trips and al[trips][0] == al[0][0]
                                         and al[trips][1] - al[trips - 1][1] == CW)):
                    trips += 1
                if trips > 1:
                    body, _ = pair(j, trips, nxt)
                    steps.append(dict(loop=trips, body=body))
                else:
                    body, _ = pair(j, 1, nxt)
                    steps += body
                j += trips
                nxt = ("up", pair0 + done + j - 1, 4 * (j - 1))
            prev = nxt
            kc = 4 * n
            for p in range(2):
                a = [None, None]
                if al:
                    k_, c_, d_ = al.pop(0)
                    a = ada_pair(k_, c_, d_)
                for h in range(2):
                    m = 2 * p + h
                    steps.append(chunk("w_down" + tag, m * CW, "mid", prev, k0=4 * done, nu=kc // KPU, ada=a[h],
                                       pairs=pair0 + done + n, first="ffn" if m == 0 else None))
                    how = ("copy" if dst == "y" and g == 0 else "part", None)
                    if g == len(groups) - 1:
                        how = ("sum", 2) if dst == "x" else ("gated_sum", 5)
                    prev = ("add", dst, m, *how)
            done += n
        return steps, prev

    col_blocks = [("col", part * D + q * CW, (i * 4 + q) * 4) for i, part in enumerate((0, 1, 3, 4))
                  for q in range(4)]
    S_FFN1, LAST_FFN1 = ffn("", "x", [None] + col_blocks, 0)

    KEEP_FFN1 = pending.pop()
    IN2 = [(3 * 1024, ("keep_a", 0)), (4 * 1024, ("glu", 0)), (3 * 1024 + CW, ("keep_a", 1)),
           (4 * 1024 + CW, ("glu", 1)),
           (0, ("plain", "mq", 0)), (CW, ("plain", "mq", 4)), (2 * CW, ("plain", "mk", 0)),
           (3 * CW, ("plain", "mk", 4)), (4 * CW, ("value", "mv", 0)), (5 * CW, ("value", "mv", 4))]
    S_IN2 = []
    prev = None
    CONV_POOL = [1, 2, 3]
    CONV_DVE = [g for g in range(CONV_G) if g not in CONV_POOL]
    CONV_A, CONV_B = 3, 5
    CONV_CUT = 128
    early = [(k, g) for k in range(CONV_K) for g in CONV_DVE + CONV_POOL[-1:] if g < 4]
    late = [(k, g) for k in range(CONV_K) for g in CONV_DVE if g >= 4]
    for i, (n0, cons) in enumerate(IN2):
        cv = []
        if CONV_A <= i < CONV_B:
            per = -(-len(early) // (CONV_B - CONV_A))
            cv = early[(i - CONV_A) * per:(i - CONV_A + 1) * per]
        if i >= CONV_B:
            per = -(-len(late) // (len(IN2) - CONV_B))
            cv = late[(i - CONV_B) * per:(i - CONV_B + 1) * per]
        S_IN2.append(chunk("w_in_2", n0, "act", prev, conv=cv))
        prev = cons
    LAST2 = prev
    S_OUT2, LAST_OUT2 = out_pairs("w_out_2", "y", None, [ada_pair("row", 2 * D + q * CW, q * CW) for q in (2, 3)], "mix2")
    KEEP_OUT2 = pending.pop()
    S_FFN2, LAST_FFN2 = ffn("_2", "y", [None] + [("row2", 5 * D + q * CW, q * CW) for q in range(4)], 1)
    C_IN1 = len(S_IN1)
    LAST_C = {"in1": C_IN1, "out1": S_OUT1[-1]["C"] + 1, "ffn1": S_FFN1[-1]["C"] + 1,
              "in2": S_IN2[-1]["C"] + 1, "out2": S_OUT2[-1]["C"] + 1, "ffn2": S_FFN2[-1]["C"] + 1}
    LAST_U = {"in1": U_CMP, "out2": S_OUT2[-1]["U"] + NU, "in2": S_IN2[-1]["U"] + NU}
    TURNS = [c for _, c in IN1 if c[0] != "value"] + [c for _, c in IN2 if c[0] not in ("value", "keep_a")]
    NORMED = [c for _, c in IN1 if c[0] in ("normed", "kv")]

    consumer_of = {}

    def note(steps, last):
        for s in steps:
            for trip in range(s.get("loop", 1)):
                for c in s.get("body", [s]):
                    p = c["prev"]
                    C = c["C"] + 2 * trip
                    if p:
                        consumer_of[C - 1] = (p[0], p[1] + trip) if p[0] in ("gate", "up") else p
        consumer_of[C] = last

    note(S_IN1, LAST1)
    note(S_OUT1, LAST_OUT1)
    note(S_FFN1, LAST_FFN1)
    note(S_IN2, LAST2)
    note(S_OUT2, LAST_OUT2)
    note(S_FFN2, LAST_FFN2)
    READ, n_free = {}, [0, 0]
    for C in range(len(consumer_of)):
        p = consumer_of[C]
        if p[0] in ("gate", "up", "glu"):
            READ[C] = (p[0], 2 * p[1] + 2)
        else:
            n_free[C % 2] += 1
            READ[C] = (("free", C % 2), n_free[C % 2])

    JOBS = []
    for h in range(FOX_H):
        JOBS.append(dict(q="fq", k="fk", v="fv", h=h, kv=h, o=h, chunk=h, first=True, last=True, gate=None,
                         table="mask", decay=True, cmp=False))
    for h in range(NSA_H):
        for b, (k, vv) in enumerate((("ks", "vs"), ("kw", "vw"))):
            JOBS.append(dict(q="nq", k=k, v=vv, h=h, kv=h // HPG, o=FOX_H + h, chunk=FOX_H + h, first=b == 0,
                             last=b == 1, gate=3 * h + 1 + b, table="alibi", decay=False, cmp=b == 1))
    N_JOB1, N_OUT_1 = len(JOBS), FOX_H + NSA_H
    for h in range(8):
        JOBS.append(dict(q="mq", k="mk", v="mv", h=h, kv=h, o=N_OUT_1 + h, chunk=h, first=True, last=True,
                         gate=None, table="mask2", decay=False, cmp=False))

    top = ExitStack()
    with top:
        def sb(name, shape, dt=F32, scope=None, side=None):
            kw = {"side": side} if side else {}
            return (scope or top).enter_context(nc.sbuf_tensor(name, shape, dt, **kw))

        def sem(name):
            return top.enter_context(nc.semaphore(name))

        x_res = sb("x_res", [P, TT, D])
        mid_hi = sb("mid_hi", [P, KD, T], F32R)
        mid_lo = sb("mid_lo", [P, KD, T], F32R)
        raw = sb("raw", [P, RAW_SLOTS, KPU, CW])
        w_hi = sb("w_hi", [P, SPLIT_SLOTS, KPU, CW], F32R)
        w_lo = sb("w_lo", [P, SPLIT_SLOTS, KPU, CW], F32R)
        ysb = sb("ysb", [P, TT, CW])
        zsb = sb("zsb", [P, TT, CW])
        ident = sb("ident", [P, P])
        ones = sb("ones", [P, P])
        consts = sb("consts", [P, 4])
        cols = sb("cols", [P, P])
        pos_cols = sb("pos_cols", [P, 2 * CMP_BLOCK])
        conv_w_cols = sb("conv_w_cols", [P, CONV_G, CONV_K + 1])
        q_gain = sb("q_gain", [P, 2])
        norm_scale = sb("norm_scale", [P, 4, KD])
        norm_shift = sb("norm_shift", [P, 4, KD])
        mod_cols = sb("mod_cols", [P, 4 * KD])
        c_act = sb("c_act", [P, KD])
        sq_sum = sb("sq_sum", [P, 6, TT, D // CW])
        mean_sq = sb("mean_sq", [P, 6, TT])
        std = sb("std", [P, 6, TT])
        rstd = sb("rstd", [P, 6, TT])
        head_ss = sb("head_ss", [P, TT * HPC])
        head_std = sb("head_std", [P, TT * HPC])
        head_rstd = sb("head_rstd", [P, TT * HPC])
        ada_bias = sb("ada_bias", [P, CW])

        right = ExitStack()
        act_hi = sb("act_hi", [P, KD, T], F32R, right, "right")
        act_lo = sb("act_lo", [P, KD, T], F32R, right, "right")
        right.close()
        right = ExitStack()
        rows0 = sb("rows0", [P, P], F32, right, "right")
        rows1 = sb("rows1", [2 * CMP_BLOCK, P], F32, right, "right")
        conv_rows = sb("conv_rows", [CONV_K, CONV_CH], F32, right, "right")
        w_small = sb("w_small", [P, KD, N_SMALL], F32, right, "right")
        right.close()
        right = ExitStack()
        blk_k = sb("blk_k", [P, CMP_BLOCK, 64], F32, right, "right")
        blk_v = sb("blk_v", [P, CMP_BLOCK, 64], F32, right, "right")
        cost1 = sb("cost1", [P, 2, TAB], F32, right, "right")
        prob1 = sb("prob1", [P, 2, TAB], F32, right, "right")
        probT1 = sb("probT1", [P, 2, TAB], F32, right, "right")
        cmp_cost = sb("cmp_cost", [P, TT * NSA_H, 32], F32, right, "right")
        cmp_prob = sb("cmp_prob", [P, TT * NSA_H, 32], F32, right, "right")
        cmp_probT = sb("cmp_probT", [P, 2, T], F32, right, "right")
        right.close()
        right = ExitStack()
        cost2 = sb("cost2", [P, 2, TAB], F32, right, "right")
        prob2 = sb("prob2", [P, 2, TAB], F32, right, "right")
        probT2 = sb("probT2", [P, 2, TAB], F32, right, "right")
        conv_sq = sb("conv_sq", [P, CONV_G, T], F32, right, "right")
        conv_mu = sb("conv_mu", [P, T], F32, right, "right")
        conv_rs = sb("conv_rs", [P, T], F32, right, "right")
        right.close()
        right = ExitStack()
        for n_ in ("act_hold_a", "act_hold_b"):
            sb(n_, [P, KD, T], F32, right, "right")

        A = ExitStack()
        heads = {n: sb(n, [P, k, T], F32, A) for n, k in
                 (("fq", FOX_H), ("fk", FOX_H), ("nq", NSA_H), ("kc", NSA_G), ("vc", NSA_G), ("ks", NSA_G),
                  ("kw", NSA_G))}
        vals = {n: sb(n, [P, TT, k, HD], F32, A) for n, k in (("fv", FOX_H), ("vs", NSA_G), ("vw", NSA_G))}
        ws = sb("ws", [P, KD, 2, N_SMALL], F32R, A)
        small = sb("small", [P, TT, N_SMALL], F32, A)
        forget_bias = sb("forget_bias", [P, FOX_H], F32, A)
        upper = sb("upper", [P, T], F32, A)
        mask = sb("mask", [P, T], F32, A)
        dist = sb("dist", [P, T], F32, A)
        alibi = sb("alibi", [P, NSA_H, T], F32, A)
        cmp_tab = sb("cmp_tab", [P, TT, NSA_H, 32], F32, A)
        cmp_ok = sb("cmp_ok", [P, TT, 32], F32, A)
        lf = sb("lf", [P, 6, TT, FOX_H], F32, A)
        decay = sb("decay", [FOX_H, T], F32, A)
        minus_eye = sb("minus_eye", [FOX_H, FOX_H], F32, A)
        gates = sb("gates", [P, TT, 3 * NSA_H], F32, A)
        gate_e = sb("gate_e", [P, TT, 3 * NSA_H], F32, A)
        kcn = sb("kcn", [64, HD], F32, A)
        kc_ss = sb("kc_ss", [64, 3], F32, A)
        kcmpT = sb("kcmpT", [P, 64], F32, A)
        vcmp = sb("vcmp", [P, NSA_G, HD], F32, A)
        cmp_min = sb("cmp_min", [P, TT * NSA_H], F32, A)
        cmp_sum = sb("cmp_sum", [P, TT * NSA_H], F32, A)
        row_min1 = sb("row_min1", [P, 2, TT], F32, A)
        row_sum1 = sb("row_sum1", [P, 2, TT], F32, A)
        row_inv1 = sb("row_inv1", [P, 2, TT], F32, A)
        A.close()

        B = ExitStack()
        gate_row1 = sb("gate_row1", [P, D], F32, B)
        ada_raw = sb("ada_raw", [P, 2, KPU, CW], F32, B)
        ada_acc = sb("ada_acc", [P, CW], F32, B)
        mask2 = sb("mask2", [P, T], F32, B)
        Cs = ExitStack()
        for n in ("mq", "mk"):
            heads[n] = sb(n, [P, 8, T], F32, Cs)
        vals["mv"] = sb("mv", [P, TT, 8, HD], F32, Cs)
        a_keep = sb("a_keep", [P, TT, CW], F32, Cs)
        uT = sb("uT", [P, CONV_G, CONV_K - 1 + T], F32, Cs)
        convT = sb("convT", [P, CONV_G, T], F32, Cs)
        conv_tmp = sb("conv_tmp", [P, 1, T], F32, Cs)
        row_min2 = sb("row_min2", [P, 2, TT], F32, Cs)
        row_sum2 = sb("row_sum2", [P, 2, TT], F32, Cs)
        row_inv2 = sb("row_inv2", [P, 2, TT], F32, Cs)
        Cs.close()
        Ds = ExitStack()
        y_acc = sb("y_acc", [P, TT, D], F32, Ds)
        gate_row2 = sb("gate_row2", [P, D], F32, Ds)
        Ds.close()
        B.close()
        right.close()

        bank = [top.enter_context(nc.psum_tensor(f"bank{i}", [P, CW], F32)) for i in range(8)]

        def acc(C):
            return [bank[2 * (C % 2)], bank[2 * (C % 2) + 1]]

        TURN = [bank[4], bank[5]]
        MISC = [bank[6], bank[7]]

        raw_loaded = [sem(f"raw_loaded{i}") for i in range(RAW_SLOTS)]
        hi_done, lo_done, parts_used = sem("hi_done"), sem("lo_done"), sem("parts_used")
        acc_free = [sem("acc_free0"), sem("acc_free1")]
        params_loaded, small_loaded = sem("params_loaded"), sem("small_loaded")
        x_loaded = [sem(f"x_loaded{t}") for t in range(TT)]
        tables_made = sem("tables_made")
        cols_turned, cols_ready = sem("cols_turned"), sem("cols_ready")
        c_ready = sem("c_ready")
        ss_act, ms_ready, std_ready, rstd_ready = (sem("ss_act"), sem("ms_ready"), sem("std_ready"),
                                                   sem("rstd_ready"))
        xn_ready_a, xn_ready_d, xn_turned, full_ready = (sem("xn_ready_a"), sem("xn_ready_d"), sem("xn_turned"),
                                                         sem("full_ready"))
        y_gated, small_folded = sem("y_gated"), sem("small_folded")
        act_hi_done, act_lo_done = sem("act_hi_done"), sem("act_lo_done")
        ws_split_hi, ws_split, small_mm, small_out = (sem("ws_split_hi"), sem("ws_split"), sem("small_mm"),
                                                      sem("small_out"))
        head_sq, head_std_ready = sem("head_sq"), sem("head_std_ready")
        turned, turn_out_a, turn_out_d = sem("turned"), sem("turn_out_a"), sem("turn_out_d")
        glu_sig, glu_ready = sem("glu_sig"), sem("glu_ready")
        sig_ready, h_ready, h_turned = sem("sig_ready"), sem("h_ready"), sem("h_turned")
        mid_hi_done, mid_lo_done = sem("mid_hi_done"), sem("mid_lo_done")
        ada_loaded = [sem("ada_loaded0"), sem("ada_loaded1")]
        ada_bias_loaded, ada_used, ada_summed, ada_out = (sem("ada_bias_loaded"), sem("ada_used"),
                                                          sem("ada_summed"), sem("ada_out"))
        gate_loaded = sem("gate_loaded")
        blk_zero, blk_ready, cmp_used = sem("blk_zero"), sem("blk_ready"), sem("cmp_used")
        kc_std, kc_n, kc_turned, kc_ready, vc_ready = (sem("kc_std"), sem("kc_n"), sem("kc_turned"),
                                                       sem("kc_ready"), sem("vc_ready"))
        lf_a, lf_d, lf_cum, decay_ready = sem("lf_a"), sem("lf_d"), sem("lf_cum"), sem("decay_ready")
        gate_exp, gates_ready = sem("gate_exp"), sem("gates_ready")
        cmp_scored, cmp_shift, cmp_exp, cmp_p, cmp_pT, cmp_pT_out = (
            sem("cmp_scored"), sem("cmp_shift"), sem("cmp_exp"), sem("cmp_p"), sem("cmp_pT"), sem("cmp_pT_out"))
        scored, reduced, exped, scaled, p_turned, p_out, pv_done = (
            sem("scored"), sem("reduced"), sem("exped"), sem("scaled"), sem("p_turned"), sem("p_out"),
            sem("pv_done"))
        o_hi, o_lo = sem("o_hi"), sem("o_lo")
        uT_zero, conv_pool, conv_dve = sem("uT_zero"), sem("conv_pool"), sem("conv_dve")
        ln_sum, ln_d, ln_sq, ln_var, ln_std, ln_y, ln_silu, ln_hi, ln_lo = (
            sem("ln_sum"), sem("ln_d"), sem("ln_sq"), sem("ln_var"), sem("ln_std"), sem("ln_y"), sem("ln_silu"),
            sem("ln_hi"), sem("ln_lo"))
        x_updated, out_stored = sem("x_updated"), sem("out_stored")
        chain_d, chain_a, chain_p = sem("chain_d"), sem("chain_a"), sem("chain_p")

        READ_SEM = {"gate": sig_ready, "up": h_ready, "glu": glu_sig, ("free", 0): acc_free[0],
                    ("free", 1): acc_free[1]}

        def wait_read(eng, C, r=None):
            key, value = READ[C]
            eng.wait_ge(READ_SEM[key], at(value, r, 2))

        ROWS0 = [(io["attn_norm"][0].rearrange("(k p) -> k p", p=P), 0, KD),
                 (io["ffn_norm"][0].rearrange("(k p) -> k p", p=P), 16, KD),
                 (io["mix_pre_g_2"][0].rearrange("(k p) -> k p", p=P), 32, KD),
                 (io["ffn_pre_g_2"][0].rearrange("(k p) -> k p", p=P), 48, KD),
                 (io["c_2"][0].rearrange("(k p) -> k p", p=P), 64, KD),
                 (io["fox_q_norm"], 80, 1), (io["fox_k_norm"], 81, 1), (io["nsa_q_norm"], 82, 1),
                 (io["cmp_k_norm"], 83, 1), (io["slc_k_norm"], 84, 1), (io["win_k_norm"], 85, 1),
                 (io["conv_b_2"][0].rearrange("(k p) -> k p", p=P), 86, CONV_G),
                 (io["conv_ln_g_2"][0].rearrange("(k p) -> k p", p=P), 94, CONV_G),
                 (io["conv_ln_b_2"][0].rearrange("(k p) -> k p", p=P), 102, CONV_G)]
        N_PARAM = len(ROWS0) + 4

        block = top.enter_context(nc.Block())

        def keep(eng, prev, t, put, done):
            kind = prev[0]
            src = TURN[t]
            cols_t = slice(t * P, (t + 1) * P)

            def v(k0, k1):
                return src[:, k0 * P:k1 * P].rearrange("p (k t) -> p k t", t=P)

            if kind == "glu":
                o = uT[:, 4 * prev[1]:4 * prev[1] + 4, CONV_K - 1 + t * P:CONV_K - 1 + (t + 1) * P]
                put(o, v(0, 4), 1.0).then_inc(done, 1)
            elif kind == "plain" and prev[1] == "kcvc":
                put(heads["kc"][:, :, cols_t], v(0, 2), 1.0)
                put(heads["vc"][:, :, cols_t], v(2, 4), 1.0).then_inc(done, 1)
            elif kind == "plain":
                g = -SCALE if prev[1] == "mq" else 1.0
                put(heads[prev[1]][:, prev[2]:prev[2] + HPC, cols_t], v(0, 4), g).then_inc(done, 1)
            else:
                k = HPC if kind == "normed" else NSA_G
                gain = {"fq": q_gain[:, 0:1], "fk": cols[:, 81:82], "nq": q_gain[:, 1:2],
                        "ks": cols[:, 84:85], "kw": cols[:, 85:86]}[prev[1]]
                put(heads[prev[1]][:, prev[2]:prev[2] + k, cols_t], v(0, k), gain).then_inc(done, 1)

        def squares(i):
            return i * TT * (D // CW) - (D // CW if i else 0)

        def run(steps, eng, do):
            for s in steps:
                if "loop" in s:
                    with eng.Fori(0, s["loop"]) as r:
                        for c in s["body"]:
                            do(c, r)
                else:
                    do(s, None)

        @block.sync
        def _(sp):
            for t in range(TT):
                sp.dma_start(x_res[:, t, :], io["x"][0, t * P:(t + 1) * P, :]).then_inc(x_loaded[t], 16)
            sp.dma_start(raw[:, 0], W["w_in"][:, 0:KPU, 0:CW]).then_inc(raw_loaded[0], 16)
            for src, r0, k in ROWS0:
                sp.dma_start(rows0[r0:r0 + k, :], src).then_inc(params_loaded, 16)
            sp.dma_start(rows1[0:CMP_BLOCK, :], io["cmp_pos_k"][0]).then_inc(params_loaded, 16)
            sp.dma_start(rows1[CMP_BLOCK:, :], io["cmp_pos_v"][0]).then_inc(params_loaded, 16)
            sp.dma_start(conv_rows[:, :], io["conv_w_2"][0]).then_inc(params_loaded, 16)
            sp.dma_start(forget_bias[:, :], io["fox_forget_bias"][0].partition_broadcast(P)).then_inc(
                params_loaded, 16)
            def slot_free(R, r, stride):
                R -= RAW_SLOTS
                if R < 0:
                    return
                if R_CMP <= R < R_CMP + N_CMPU:
                    sp.wait_ge(cmp_used, R - R_CMP + 1)
                else:
                    sp.wait_ge(lo_done, at((R if R < R_CMP else R - N_CMPU) + 1, r, stride))

            def ada_load(c, r, i):
                a = c["ada"]
                unit = a["A"] + i
                if unit >= 2:
                    sp.wait_ge(ada_used, at(2 * (unit - 1), r, 16))
                k = a["half"] * 8 + 2 * i
                n0 = at(a["col"], r, a["step"])
                sp.dma_start(ada_raw[:, unit % 2], W["ada_w_2"][:, k:k + KPU, bass.ds(n0, CW)]).then_inc(
                    ada_loaded[unit % 2], 16)
                if a["half"] == 0 and i == 0:
                    if unit < 2:
                        sp.wait_ge(tables_made, 2)
                    sp.dma_start(ada_bias[0:1, :], io["ada_b_2"][0:1, bass.ds(n0, CW)]).then_inc(ada_bias_loaded, 16)

            def load(c, r):
                for u in range(c["nu"]):
                    R = c["R"] + u
                    slot_free(R, r, 2 * c["nu"])
                    k = c["k0"] + KPU * u
                    n0 = at(c["n0"], r, c["n_step"])
                    if R == 0:
                        sp.dma_start(w_small[:, :, 0:FOX_H], W["w_in"][:, :, o_ff:o_ff + FOX_H]).then_inc(small_loaded, 16)
                        sp.dma_start(w_small[:, :, FOX_H:N_SMALL], W["w_in"][:, :, o_gt:o_gt + 3 * NSA_H]).then_inc(
                            small_loaded, 16)
                        continue
                    sp.dma_start(raw[:, R % RAW_SLOTS], W[c["w"]][:, k:k + KPU, bass.ds(n0, CW)]).then_inc(
                        raw_loaded[R % RAW_SLOTS], 16)
                    ada_at = ADA_LATE if c is S_OUT2[0] else ADA_AT
                    if c["ada"] and u in ada_at:
                        ada_load(c, r, ada_at.index(u))
                if c["ada"] and c["nu"] < 7:
                    ada_load(c, r, 3)

            run(S_IN1, sp, load)
            for j in range(N_CMPU):
                R = R_CMP + j
                slot_free(R, None, 0)
                src = io["cmp_w_k" if j < 4 else "cmp_w_v"][0].rearrange("l d e -> d l e")
                l0 = 8 * (j % 4)
                sp.dma_start(raw[:, R % RAW_SLOTS].rearrange("p a n -> p (a n)").rearrange("p (l e) -> p l e", e=HD),
                             src[:, l0:l0 + 8, :]).then_inc(raw_loaded[R % RAW_SLOTS], 16)
            c0 = S_OUT1[0]
            for u in range(RAW_SLOTS):
                slot_free(c0["R"] + u, None, 0)
                sp.dma_start(raw[:, (c0["R"] + u) % RAW_SLOTS],
                             W["w_out"][:, KPU * u:KPU * u + KPU, 0:CW]).then_inc(
                    raw_loaded[(c0["R"] + u) % RAW_SLOTS], 16)
            def load_out1(c, r):
                if c is c0:
                    for u in range(c["nu"]):
                        R = c["R"] + u
                        if u >= RAW_SLOTS:
                            slot_free(R, r, 0)
                            sp.dma_start(raw[:, R % RAW_SLOTS],
                                         W["w_out"][:, KPU * u:KPU * u + KPU, 0:CW]).then_inc(
                                raw_loaded[R % RAW_SLOTS], 16)
                        if u == ADA_LATE[0]:
                            sp.wait_ge(o_lo, N_OUT_1)
                        if u in ADA_LATE:
                            ada_load(c, r, ADA_LATE.index(u))
                    sp.dma_start(gate_row1[:, :], io["mix_post_g_2"][0].partition_broadcast(P)).then_inc(
                        gate_loaded, 16)
                else:
                    load(c, r)

            run(S_OUT1, sp, load_out1)
            run(S_FFN1, sp, load)
            run(S_IN2, sp, load)
            run(S_OUT2, sp, load)
            sp.wait_ge(o_lo, N_OUT_1 + 8)
            sp.wait_ge(ln_lo, 2)
            sp.dma_start(gate_row2[:, :], io["ffn_post_g_2"][0].partition_broadcast(P)).then_inc(gate_loaded, 16)
            run(S_FFN2, sp, load)
            for t in range(TT):
                for h in range(2):
                    sp.wait_ge(x_updated, 4 * (TT + t) + 2 * h + 2)
                    sp.dma_start(out[0, t * P:(t + 1) * P, h * D // 2:(h + 1) * D // 2],
                                 x_res[:, t, h * D // 2:(h + 1) * D // 2]).then_inc(out_stored, 16)
            sp.wait_ge(out_stored, 16 * 2 * TT)

        @block.gpsimd
        def _(pool):
            n = [0]

            def link(ins):
                n[0] += 1
                ins.then_inc(chain_p, 1)
                pool.wait_ge(chain_p, n[0])

            for i, val in enumerate((1e-6, 1e-5, 1.0, 0.0)):
                link(pool.memset(consts[:, i:i + 1], val))
            link(pool.memset(ident[:, :], 0.0))
            link(pool.affine_select(out=ident[:, :], in_=ident[:, :], pattern=[[-1, P]],
                                    compare_op=ALU.not_equal, fill=1.0, base=0, channel_multiplier=1))
            link(pool.memset(ones[:, :], 1.0))
            pool.memset(norm_shift[:, 0:2, :], 0.0).then_inc(tables_made, 1)
            link(pool.memset(upper[:, :], 1.0))
            link(pool.affine_select(out=upper[:, :], in_=upper[:, :], pattern=[[1, T]], compare_op=ALU.is_ge,
                                    fill=0.0, base=0, channel_multiplier=-1))
            link(pool.memset(mask[:, :], 0.0))
            link(pool.affine_select(out=mask[:, :], in_=mask[:, :], pattern=[[-1, T]], compare_op=ALU.is_ge,
                                    fill=BIG, base=P, channel_multiplier=1))
            link(pool.iota(dist[:, :], pattern=[[-1, T]], base=P, channel_multiplier=1,
                           allow_small_or_imprecise_dtypes=True))
            for h in range(NSA_H):
                slope = 2.0 ** (-8.0 * (h + 1) / NSA_H)
                link(pool.tensor_scalar(alibi[:, h, :], dist[:, :], slope, None, ALU.mult))
                link(pool.tensor_tensor(alibi[:, h, :], alibi[:, h, :], mask[:, :], ALU.add))
            pat = [[P, TT], [0, NSA_H], [-CMP_STRIDE, 32]]
            base = -(CMP_BLOCK - 1)
            link(pool.iota(cmp_tab[:, :, :, :], pattern=pat, base=base, channel_multiplier=1,
                           allow_small_or_imprecise_dtypes=True))
            for h in range(NSA_H):
                slope = 2.0 ** (-8.0 * (h + 1) / NSA_H)
                link(pool.tensor_scalar(cmp_tab[:, :, h, :], cmp_tab[:, :, h, :], slope, None, ALU.mult))
            link(pool.affine_select(out=cmp_tab[:, :, :, :], in_=cmp_tab[:, :, :, :], pattern=pat,
                                    compare_op=ALU.is_ge, fill=BIG, base=base, channel_multiplier=1))
            pool.memset(ada_bias[:, :], 0.0)
            link(pool.memset(cmp_ok[:, :, :], 1.0))
            link(pool.affine_select(out=cmp_ok[:, :, :], in_=cmp_ok[:, :, :], pattern=[pat[0], pat[2]],
                                    compare_op=ALU.is_ge, fill=0.0, base=base, channel_multiplier=1))
            pool.memset(vcmp[:, :, :], 0.0).then_inc(tables_made, 1)
            pool.wait_ge(parts_used, U_CMP)
            for blk in (blk_k, blk_v):
                pads = blk[:, :, :].rearrange("p l (g n) -> p l g n", g=NSA_G)[:, :, :, N_CMP:]
                pool.memset(pads, 0.0).then_inc(blk_zero, 1)
            pool.wait_ge(o_lo, N_OUT_1)
            link(pool.memset(mask2[:, :], 0.0))
            link(pool.affine_select(out=mask2[:, :], in_=mask2[:, :], pattern=[[-1, T]], compare_op=ALU.is_ge,
                                    fill=BIG, base=P, channel_multiplier=1))
            pool.memset(uT[:, :, 0:CONV_K - 1], 0.0).then_inc(uT_zero, 1)
            pool.wait_ge(uT_zero, 1)
            pool.wait_ge(turn_out_a, TURNS.index(("glu", 0)) + 1)
            pool.wait_ge(turn_out_d, TURNS.index(("glu", 0)) + 1)
            for k in range(CONV_K):
                for g in CONV_POOL:
                    t0 = CONV_CUT if g == CONV_POOL[-1] else 0
                    src = uT[:, g, k + t0:k + T]
                    wk = conv_w_cols[:, g, k:k + 1]
                    if k == 0:
                        ins = pool.tensor_scalar(convT[:, g, t0:], src, wk, cols[:, 86 + g:87 + g], ALU.mult, ALU.add)
                        link(ins)
                    else:
                        link(pool.tensor_scalar(conv_tmp[:, 0, t0:], src, wk, None, ALU.mult))
                        ins = pool.tensor_tensor(convT[:, g, t0:], convT[:, g, t0:], conv_tmp[:, 0, t0:], ALU.add)
                        if (k, g) == (CONV_K - 1, CONV_POOL[-1]):
                            ins.then_inc(conv_pool, 1)
                        else:
                            link(ins)

        @block.tensor
        def _(pe):
            pe.wait_ge(tables_made, 1)
            pe.wait_ge(params_loaded, 16 * N_PARAM)
            pe.transpose(MISC[0][:, 0:110], rows0[0:110, :], ident[0:110, 0:110])
            pe.transpose(MISC[0][:, 128:192], rows1[:, :], ident[0:64, 0:64])
            for g in range(CONV_G):
                ins = pe.transpose(MISC[1][:, 32 * g:32 * g + CONV_K], conv_rows[:, g * P:(g + 1) * P],
                                   ident[0:CONV_K, 0:CONV_K])
            ins.then_inc(cols_turned, 1)

            def turn_rows(i):
                pe.wait_ge(xn_ready_a, i + 1)
                pe.wait_ge(xn_ready_d, i + 1)
                if i >= 2:
                    pe.wait_ge(full_ready, i - 1)
                for c in range(KPU):
                    for t in range(TT):
                        ins = pe.transpose(TURN[i % 2][:, (c * TT + t) * P:(c * TT + t + 1) * P],
                                           ysb[:, i % 2, (t * KPU + c) * P:(t * KPU + c + 1) * P], ident[:, :])
                ins.then_inc(xn_turned, 1)

            def first_gemm(c, n):
                turn_rows(n * NU)
                turn_rows(n * NU + 1)

                def after(u):
                    if n == 0:
                        for v in ([] if u == 0 else [u - 1] if u < NU - 1 else [u - 1, u]):
                            small_gemm(v)
                    if u + 2 < NU:
                        turn_rows(n * NU + u + 2)

                gemm(c, None, lambda u: pe.wait_ge(act_lo_done, n * NU + u + 1), after)

            def small_gemm(u):
                if u == 0:
                    pe.wait_ge(ws_split, 1)
                    pe.wait_ge(cols_ready, 2)
                for kk in range(KPU):
                    k = KPU * u + kk
                    st = ws[:, k, :, :].rearrange("p s n -> p (s n)")
                    pe.matmul(MISC[0][0:2 * N_SMALL, 0:T], st, act_hi[:, k, :], start=(k == 0), stop=False)
                    ins = pe.matmul(MISC[0][0:2 * N_SMALL, 0:T], st, act_lo[:, k, :], start=False,
                                    stop=(k == KD - 1))
                if u == NU - 1:
                    ins.then_inc(small_mm, 1)

            def small_fold():
                pe.wait_ge(small_folded, 1)
                for t in range(TT):
                    for part in range(2):
                        ins = pe.matmul(MISC[0][:, t * N_SMALL:(t + 1) * N_SMALL],
                                        ysb[0:2 * N_SMALL, 0, t * P:(t + 1) * P],
                                        ident[0:2 * N_SMALL, part * N_SMALL:(part + 1) * N_SMALL],
                                        start=(part == 0), stop=(part == 1))
                ins.then_inc(small_mm, 1)

            def consume(prev, C, r):
                if prev is None or prev[0] in ("value", "keep_a", "add", "gate"):
                    return
                if prev[0] == "up":
                    q = prev[1]
                    pe.wait_ge(h_ready, at(2 * q + 2, r, 2))
                    if q >= 1:
                        pe.wait_ge(mid_lo_done, at(2 * q, r, 2))
                    for t in range(TT):
                        for c in range(HPC):
                            ins = pe.transpose(TURN[t][:, c * P:(c + 1) * P], zsb[:, t, c * P:(c + 1) * P], ident[:, :])
                        ins.then_inc(h_turned, 1)
                    return
                i = TURNS.index(prev)
                if prev[0] == "glu":
                    pe.wait_ge(glu_ready, 2 * prev[1] + 2)
                else:
                    wait_read(pe, C - 1)
                if i >= 1:
                    pe.wait_ge(turn_out_a, i)
                    pe.wait_ge(turn_out_d, i)
                k = NSA_G if prev[0] == "kv" else HPC
                for t in range(TT):
                    for c in range(k):
                        ins = pe.transpose(TURN[t][:, c * P:(c + 1) * P], ysb[:, t, c * P:(c + 1) * P], ident[:, :])
                ins.then_inc(turned, 1)

            def gemm(c, r, before=lambda u: None, after=lambda u: None):
                hi, lo = (act_hi, act_lo) if c["st"] == "act" else (mid_hi, mid_lo)
                C, nu = c["C"], c["nu"]
                A_ = acc(C)
                for u in range(nu):
                    if u == 0:
                        if C >= 2:
                            wait_read(pe, C - 2, r)
                    if c.get("first") == "mix1":
                        pe.wait_ge(o_lo, KPU * (u + 1))
                    if c.get("first") == "mix2" and u < NU - CONV_G // KPU:
                        pe.wait_ge(o_lo, N_OUT_1 + KPU * (u + 1))
                    if c.get("first") == "mix2" and u >= NU - CONV_G // KPU:
                        pe.wait_ge(ln_lo, 1 if u < NU - CONV_G // KPU // 2 else 2)
                    if c.get("first") == "ffn":
                        pe.wait_ge(mid_lo_done, 2 * (c["pairs"] - (0 if u >= nu - 2 else 1)))
                    before(u)
                    U = c["U"] + u
                    pe.wait_ge(lo_done, at(U + 1, r, 2 * nu))
                    s = U % SPLIT_SLOTS
                    for kk in range(KPU):
                        k = KPU * u + kk
                        for t in range(TT):
                            h_, l_ = hi[:, k, t * P:(t + 1) * P], lo[:, k, t * P:(t + 1) * P]
                            pe.matmul(A_[t][:, :], h_, w_hi[:, s, kk, :], start=(k == 0), stop=False)
                            pe.matmul(A_[t][:, :], h_, w_lo[:, s, kk, :], start=False, stop=False)
                            ins = pe.matmul(A_[t][:, :], l_, w_hi[:, s, kk, :], start=False,
                                            stop=(k == KPU * nu - 1))
                    ins.then_inc(parts_used, 1)
                    after(u)
                    if u == min(4, nu - 3):
                        consume(c["prev"], C, r)
                    if c is S_IN1[SMALL_OUT] and u == 6:
                        small_fold()
                    if c is S_IN1[SMALL_OUT + 2] and u == 3:
                        pe.wait_ge(lf_d, 2)
                        pe.wait_ge(tables_made, 2)
                        o = MISC[0][0:FOX_H, 0:T]
                        pe.matmul(o, lf[:, 5, 0, :], upper[:, :], start=True, stop=False)
                        pe.matmul(MISC[0][0:FOX_H, P:T], lf[:, 5, 1, :], upper[:, 0:P], start=False,
                                  stop=True).then_inc(lf_cum, 1)
                    a = c["ada"]
                    if a and a["half"] == 1 and u == 5:
                        pe.wait_ge(ada_used, at(2 * (a["A"] + 4), r, 16))
                        if a["blk"] >= 1:
                            pe.wait_ge(ada_out, at(a["blk"], r, 1))
                        if a["kind"] == "col":
                            for j in range(4):
                                ins = pe.matmul(MISC[0][:, j:j + 1], ada_acc[:, j * P:(j + 1) * P], ones[:, 0:1],
                                                start=True, stop=True)
                        else:
                            ins = pe.matmul(MISC[0][:, :], ones[:, :], ada_acc[:, :], start=True, stop=True)
                        ins.then_inc(ada_summed, 1)

            def attend(j0, j1, cost, prob, probT, hook=lambda i: None):
                def scores(j):
                    b, s = JOBS[j], bank[j % 2]
                    if j - j0 >= 2:
                        pe.wait_ge(reduced, 2 * (j - 1))
                    q, k = heads[b["q"]], heads[b["k"]]
                    for t, c0, n in ((0, 0, P), (1, P, T)):
                        ins = pe.matmul(s[:, c0:c0 + n], q[:, b["h"], t * P:(t + 1) * P], k[:, b["kv"], 0:n],
                                        start=True, stop=not b["decay"])
                        if b["decay"]:
                            h = b["h"]
                            pe.matmul(s[:, c0:c0 + n], decay[:, t * P:(t + 1) * P],
                                      minus_eye[:, h:h + 1].to_broadcast([FOX_H, n]), start=False, stop=False)
                            ins = pe.matmul(s[:, c0:c0 + n], ident[0:FOX_H, h:h + 1].to_broadcast([FOX_H, P]),
                                            decay[:, 0:n], start=False, stop=True)
                    ins.then_inc(scored, 1)

                def turn(j):
                    pe.wait_ge(scaled, 2 * j + 2)
                    if j - j0 >= 2:
                        pe.wait_ge(p_out, j - 1)
                    for c in range(3):
                        ins = pe.transpose(bank[2 + j % 2][:, c * P:(c + 1) * P], prob[:, j % 2, c * P:(c + 1) * P],
                                           ident[:, :])
                    ins.then_inc(p_turned, 1)

                def values(j):
                    b = JOBS[j]
                    o = bank[4 + b["o"] % 2]
                    pe.wait_ge(p_out, j + 1)
                    if b["first"] and j > j0 and b["o"] - JOBS[j0]["o"] >= 2:
                        pe.wait_ge(o_lo, b["o"] - 1)
                    v = vals[b["v"]]
                    pT = probT[:, j % 2, :]
                    pe.matmul(o[:, 0:T], v[:, 0, b["kv"], :], pT[:, 0:T], start=b["first"], stop=False)
                    ins = pe.matmul(o[:, P:T], v[:, 1, b["kv"], :], pT[:, T:TAB], start=False, stop=b["last"] and not b["cmp"])
                    if b["cmp"]:
                        pe.wait_ge(cmp_pT_out, 1)
                        r0 = 32 * (b["h"] % 4)
                        ins = pe.matmul(o[:, 0:T], vcmp[r0:r0 + 32, b["kv"], :],
                                        cmp_probT[r0:r0 + 32, b["h"] // 4, :], start=False, stop=True)
                    ins.then_inc(pv_done, 1)

                for i in range(j0, j1 + 3):
                    if i < j1:
                        scores(i)
                    if j0 + 2 <= i < j1 + 2:
                        turn(i - 2)
                    if i >= j0 + 3:
                        values(i - 3)
                    hook(i)

            first_gemm(S_IN1[0], 0)
            run(S_IN1[1:], pe, gemm)
            consume(LAST1, C_IN1, None)
            wait_read(pe, C_IN1 - 2)
            wait_read(pe, C_IN1 - 1)
            pe.wait_ge(decay_ready, 1)
            pe.wait_ge(turn_out_a, len(IN1) - 2)
            pe.wait_ge(turn_out_d, len(IN1) - 2)

            def compressed(i):
                if i in (-1, 0):
                    kind, blk = i + 1, (blk_k, blk_v)[i + 1]
                    pe.wait_ge(blk_zero, kind + 1)
                    pe.wait_ge(blk_ready, kind + 1)
                    for j in range(4):
                        R = R_CMP + 4 * kind + j
                        pe.wait_ge(raw_loaded[R % RAW_SLOTS], 16 * (R // RAW_SLOTS + 1))
                        w = raw[:, R % RAW_SLOTS].rearrange("p a n -> p (a n)")
                        for l in range(8):
                            ins = pe.matmul(MISC[kind][0:64, 0:HD], blk[:, 8 * j + l, :], w[:, l * HD:(l + 1) * HD],
                                            start=(j + l == 0), stop=(j == 3 and l == 7))
                        ins.then_inc(cmp_used, 1)
                if i == 1:
                    pe.wait_ge(kc_n, 1)
                    pe.transpose(MISC[0][:, T:T + 64], kcn[:, :], ident[0:64, 0:64]).then_inc(kc_turned, 1)
                if i == 3:
                    pe.wait_ge(kc_ready, 1)
                    pe.wait_ge(vc_ready, 1)
                    for h in range(NSA_H):
                        for t in range(TT):
                            g = h // HPG
                            c0 = (t * NSA_H + h) * 32
                            ins = pe.matmul(MISC[1][:, c0:c0 + 32], heads["nq"][:, h, t * P:(t + 1) * P],
                                            kcmpT[:, 32 * g:32 * g + 32], start=True, stop=True)
                    ins.then_inc(cmp_scored, 1)
                if i == 8:
                    pe.wait_ge(cmp_p, 1)
                    for hh in range(2):
                        for t in range(TT):
                            src = cmp_prob[:, t * NSA_H + hh * 4:t * NSA_H + hh * 4 + 4, :].rearrange(
                                "p h n -> p (h n)")
                            ins = pe.transpose(MISC[0][:, (hh * TT + t) * P:(hh * TT + t + 1) * P], src, ident[:, :])
                    ins.then_inc(cmp_pT, 1)

            compressed(-1)
            attend(0, N_JOB1, cost1, prob1, probT1, compressed)

            run(S_OUT1, pe, gemm)
            first_gemm(S_FFN1[0], 1)
            run(S_FFN1[1:], pe, gemm)
            first_gemm(S_IN2[0], 2)
            run(S_IN2[1:], pe, gemm)
            consume(LAST2, LAST_C["in2"], None)
            wait_read(pe, LAST_C["in2"] - 2)
            wait_read(pe, LAST_C["in2"] - 1)
            pe.wait_ge(turn_out_a, len(TURNS))
            pe.wait_ge(turn_out_d, len(TURNS))

            def layer_norm(i):
                if i == N_JOB1 + 2:
                    pe.wait_ge(conv_pool, 1)
                    pe.wait_ge(conv_dve, len(early) + len(late))
                    for g in range(CONV_G):
                        ins = pe.matmul(MISC[0][:, 0:T], ones[:, :], convT[:, g, :], start=(g == 0),
                                        stop=(g == CONV_G - 1))
                    ins.then_inc(ln_sum, 1)
                if i == N_JOB1 + 5:
                    pe.wait_ge(ln_sq, 1)
                    for g in range(CONV_G):
                        ins = pe.matmul(MISC[1][:, 0:T], ones[:, :], conv_sq[:, g, :], start=(g == 0),
                                        stop=(g == CONV_G - 1))
                    ins.then_inc(ln_var, 1)

            attend(N_JOB1, len(JOBS), cost2, prob2, probT2, layer_norm)
            run(S_OUT2, pe, gemm)
            first_gemm(S_FFN2[0], 3)
            run(S_FFN2[1:], pe, gemm)

        @block.scalar
        def _(act):
            chain = [0]

            def link(ins):
                chain[0] += 1
                ins.then_inc(chain_a, 1)
                act.wait_ge(chain_a, chain[0])

            n_sq = [0]

            def square(i, t, q, src):
                act.activation(ysb[:, 0, :], src, ACT.Square, accum_out=sq_sum[:, i, t, q:q + 1]).then_inc(ss_act, 1)
                n_sq[0] += 1
                act.wait_ge(ss_act, n_sq[0])

            def root_table():
                link(act.activation(head_std[:, 0:1], consts[:, 2:3], ACT.Sqrt))

            def root(i):
                act.wait_ge(ms_ready, i + 1)
                act.activation(std[:, i, :], mean_sq[:, i, :], ACT.Sqrt, bias=consts[:, 0:1],
                               scale=1.0 / D).then_inc(std_ready, 1)

            def rows(i, i_stat):
                j = i % NU
                act.wait_ge(rstd_ready, i_stat + 1)
                if i >= 2:
                    act.wait_ge(xn_turned, i - 1)
                act.activation(ysb[:, i % 2, 0:KPU * P], x_res[:, 0, j * KPU * P:(j + 1) * KPU * P], ACT.Copy,
                               scale=rstd[:, i_stat, 0:1]).then_inc(xn_ready_a, 1)

            def first_split(c, n, i_stat):
                def norm_hi(j):
                    i = n * NU + j
                    act.wait_ge(full_ready, i + 1)
                    act.activation(act_hi[:, KPU * j:KPU * j + KPU, :].rearrange("p k t -> p (k t)"),
                                   zsb[:, i % 2, :], ACT.Copy).then_inc(act_hi_done, 1)

                def before(u):
                    if u + 1 < NU:
                        rows(n * NU + u + 1, i_stat)
                    if u >= 1:
                        norm_hi(u - 1)
                    if n == 0 and u == 1:
                        act.wait_ge(small_loaded, 32)
                        act.activation(ws[:, :, 0, :], w_small[:, :, :], ACT.Copy).then_inc(ws_split_hi, 1)

                rows(n * NU, i_stat)
                split(c, None, before)
                norm_hi(NU - 1)

            def pre(prev, C, r):
                if prev is None:
                    return
                A_, free = acc(C - 1), acc_free[(C - 1) % 2]
                kind = prev[0]
                if kind == "gate":
                    q = prev[1]
                    if q >= 1:
                        act.wait_ge(h_ready, at(2 * q, r, 2))
                    for t in range(TT):
                        ins = act.activation(ysb[:, t, :], A_[t][:, :], ACT.Silu).then_inc(sig_ready, 1)
                elif kind == "add" and prev[4] is not None:
                    _, dst, n, how, i = prev
                    for t in range(TT):
                        if how == "gated_copy":
                            square(i, t, n, A_[t][:, :])
                        else:
                            wait_read(act, C - 1)
                            d = x_res if dst == "x" else y_acc
                            square(i, t, n, d[:, t, n * CW:(n + 1) * CW])
                elif kind == "value":
                    for t in range(TT):
                        ins = act.activation(vals[prev[1]][:, t, prev[2]:prev[2] + HPC, :].rearrange("p h d -> p (h d)"),
                                             A_[t][:, :], ACT.Copy)
                        if t == TT - 1:
                            ins.then_inc(free, 1)
                elif kind == "keep_a":
                    if prev[1] >= 1:
                        act.wait_ge(glu_ready, 2 * prev[1])
                    for t in range(TT):
                        ins = act.activation(a_keep[:, t, :], A_[t][:, :], ACT.Copy)
                        if t == TT - 1:
                            ins.then_inc(free, 1)
                elif kind == "glu":
                    for t in range(TT):
                        act.activation(zsb[:, t, :], A_[t][:, :], ACT.Sigmoid).then_inc(glu_sig, 1)
                elif kind == "plain":
                    i = TURNS.index(prev)
                    if i >= 1:
                        act.wait_ge(turned, i)
                    for t in range(TT):
                        ins = act.activation(ysb[:, t, :], A_[t][:, :], ACT.Copy)
                        if t == TT - 1:
                            ins.then_inc(free, 1)
                elif kind in ("normed", "kv"):
                    k = HPC if kind == "normed" else NSA_G
                    m = NORMED.index(prev)
                    for t in range(TT):
                        if kind == "kv":
                            act.activation(vals["vs" if prev[1] == "ks" else "vw"][:, t, :, :].rearrange(
                                "p h d -> p (h d)"), A_[t][:, NSA_G * HD:], ACT.Copy)
                        for h in range(k):
                            link(act.activation(zsb[:, t, h * HD:(h + 1) * HD], A_[t][:, h * HD:(h + 1) * HD],
                                                ACT.Square, accum_out=head_ss[:, t * HPC + h:t * HPC + h + 1]))
                    if m >= 1:
                        act.wait_ge(head_sq, m)
                    act.activation(head_std[:, :], head_ss[:, :], ACT.Sqrt, bias=consts[:, 0:1],
                                   scale=1.0 / HD).then_inc(head_std_ready, 1)

            def post(prev, C, r):
                if prev is None or prev[0] in ("value", "keep_a", "add", "gate"):
                    return
                if prev[0] == "up":
                    q = prev[1]
                    k0 = at(prev[2], r, 4)
                    for t in range(TT):
                        act.wait_ge(h_turned, at(2 * q + t + 1, r, 2))
                        act.activation(mid_hi[:, bass.ds(k0, 4), t * P:(t + 1) * P],
                                       TURN[t][:, :].rearrange("p (k t) -> p k t", t=P), ACT.Copy).then_inc(
                            mid_hi_done, 1)
                    return
                i = TURNS.index(prev)
                act.wait_ge(turned, i + 1)
                keep(act, prev, 0, lambda o, s, g: act.activation(o, s, ACT.Copy, scale=g), turn_out_a)

            def split(c, r, before=lambda u: None, units=None):
                for u in units or range(c["nu"]):
                    before(u)
                    R, U = c["R"] + u, c["U"] + u
                    act.wait_ge(raw_loaded[R % RAW_SLOTS], at(16 * (R // RAW_SLOTS + 1), r, 16 * 2 * c["nu"] // 4))
                    if U >= SPLIT_SLOTS:
                        act.wait_ge(parts_used, at(U - SPLIT_SLOTS + 1, r, 2 * c["nu"]))
                    act.activation(w_hi[:, U % SPLIT_SLOTS].rearrange("p k n -> p (k n)"),
                                   raw[:, R % RAW_SLOTS].rearrange("p k n -> p (k n)"), ACT.Copy).then_inc(hi_done, 1)
                    if u == 3:
                        pre(c["prev"], c["C"], r)
                    if c is S_IN1[SMALL_OUT] and u == 6:
                        act.wait_ge(cols_ready, 2)
                        act.activation(c_act[:, :], cols[:, 64:64 + KD], ACT.Silu).then_inc(c_ready, 1)
                    if c is S_IN1[SMALL_OUT + 1] and u == 6:
                        act.wait_ge(lf_d, 1)
                        link(act.activation(lf[:, 2], lf[:, 1], ACT.Exp, scale=-1.0))
                        act.activation(lf[:, 3], lf[:, 2], ACT.Ln, bias=consts[:, 2:3]).then_inc(lf_a, 1)
                        act.activation(gate_e[:, :, :], small[:, :, FOX_H:], ACT.Exp, scale=-1.0).then_inc(gate_exp, 1)
                if u == c["nu"] - 1:
                    post(c["prev"], c["C"], r)

            def early_split(c, i, j1):
                if j1 - 3 <= i < j1 - 3 + EARLY:
                    split(c, None, units=[i - (j1 - 3)])

            def attend(j0, j1, cost, prob, probT, row_min, row_sum, hook=lambda i: None):
                for i in range(j0, j1 + 3):
                    if i < j1:
                        for t, c0, n in ((0, 0, P), (1, P, T)):
                            act.wait_ge(reduced, 2 * i + t + 1)
                            if i - j0 >= 2:
                                act.wait_ge(p_turned, i - 1)
                            act.activation(prob[:, i % 2, c0:c0 + n], cost[:, i % 2, c0:c0 + n], ACT.Exp,
                                           bias=row_min[:, i % 2, t:t + 1], scale=-1.0,
                                           accum_out=row_sum[:, i % 2, t:t + 1]).then_inc(exped, 1)
                    if j0 + 2 <= i < j1 + 2:
                        j = i - 2
                        act.wait_ge(p_turned, j + 1)
                        if j - j0 >= 2:
                            act.wait_ge(pv_done, j - 1)
                        act.activation(probT[:, j % 2, :], bank[2 + j % 2][:, 0:TAB], ACT.Copy).then_inc(p_out, 1)
                    if i >= j0 + 3 and JOBS[i - 3]["last"]:
                        b = JOBS[i - 3]
                        act.wait_ge(pv_done, i - 2)
                        act.activation(mid_hi[:, b["chunk"], :], bank[4 + b["o"] % 2][:, 0:T], ACT.Copy).then_inc(
                            o_hi, 1)
                    hook(i)

            act.wait_ge(tables_made, 1)
            root_table()
            act.wait_ge(x_loaded[0], 16)
            for q in range(D // CW):
                square(0, 0, q, x_res[:, 0, q * CW:(q + 1) * CW])
            root(0)
            first_split(S_IN1[0], 0, 0)
            run(S_IN1[1:], act, split)
            act.wait_ge(parts_used, LAST_U["in1"])
            pre(LAST1, C_IN1, None)
            post(LAST1, C_IN1, None)

            def compressed(i):
                if i == -1:
                    act.wait_ge(cmp_used, 4)
                    link(act.activation(kcn[:, :], MISC[0][0:64, 0:HD], ACT.Square, accum_out=kc_ss[:, 0:1]))
                    act.activation(kc_ss[:, 1:2], kc_ss[:, 0:1], ACT.Sqrt, bias=consts[0:64, 0:1],
                                   scale=1.0 / HD).then_inc(kc_std, 1)
                if i == 5:
                    act.wait_ge(cmp_shift, 1)
                    act.activation(cmp_prob[:, :, :], cmp_cost[:, :, :], ACT.Exp, scale=-1.0).then_inc(cmp_exp, 1)
                if i == 9:
                    act.wait_ge(cmp_pT, 1)
                    act.activation(cmp_probT[:, :, :].rearrange("p h t -> p (h t)"), MISC[0][:, :],
                                   ACT.Copy).then_inc(cmp_pT_out, 1)
                early_split(S_OUT1[0], i, N_JOB1)

            compressed(-1)
            attend(0, N_JOB1, cost1, prob1, probT1, row_min1, row_sum1, compressed)
            split(S_OUT1[0], None, units=range(EARLY, NU))
            run(S_OUT1[1:], act, split)
            root_table()
            pre(LAST_OUT1, LAST_C["out1"], None)
            root(1)
            first_split(S_FFN1[0], 1, 1)
            run(S_FFN1[1:], act, split)
            root_table()
            pre(LAST_FFN1, LAST_C["ffn1"], None)
            root(2)
            first_split(S_IN2[0], 2, 2)
            run(S_IN2[1:], act, split)
            act.wait_ge(parts_used, LAST_U["in2"])
            pre(LAST2, LAST_C["in2"], None)
            post(LAST2, LAST_C["in2"], None)

            def layer_norm(i):
                if i == N_JOB1 + 4:
                    act.wait_ge(ln_d, 1)
                    act.activation(conv_sq[:, :, :], convT[:, :, :], ACT.Square).then_inc(ln_sq, 1)
                if i == len(JOBS):
                    act.wait_ge(ln_var, 1)
                    act.activation(conv_rs[:, :], MISC[1][:, 0:T], ACT.Sqrt, bias=consts[:, 1:2],
                                   scale=1.0 / CONV_CH).then_inc(ln_std, 1)
                early_split(S_OUT2[0], i, len(JOBS))

            def conv_hi(u):
                if u in (EARLY, EARLY + 2):
                    half = (u - EARLY) // 2
                    g0, g1 = half * CONV_G // 2, (half + 1) * CONV_G // 2
                    act.wait_ge(ln_y, half + 1)
                    for g in range(g0, g1):
                        act.activation(convT[:, g, :], convT[:, g, :], ACT.Silu, bias=cols[:, 102 + g:103 + g],
                                       scale=cols[:, 94 + g:95 + g]).then_inc(ln_silu, 1)
                    act.wait_ge(ln_silu, g1)
                    act.activation(mid_hi[:, CONV_G + g0:CONV_G + g1, :], convT[:, g0:g1, :], ACT.Copy).then_inc(
                        ln_hi, 1)

            attend(N_JOB1, len(JOBS), cost2, prob2, probT2, row_min2, row_sum2, layer_norm)
            split(S_OUT2[0], None, before=conv_hi, units=range(EARLY, NU))
            run(S_OUT2[1:], act, split)
            root_table()
            act.wait_ge(parts_used, LAST_U["out2"])
            pre(LAST_OUT2, LAST_C["out2"], None)
            root(3)
            for t in range(TT):
                for q in range(D // CW):
                    act.wait_ge(x_updated, 4 * t + q + 1)
                    square(4, t, q, x_res[:, t, q * CW:(q + 1) * CW])
            root(4)
            first_split(S_FFN2[0], 3, 4)
            run(S_FFN2[1:], act, split)
            root_table()
            pre(LAST_FFN2, LAST_C["ffn2"], None)
            root(5)

        @block.vector
        def _(dve):
            chain = [0]

            def link(ins):
                chain[0] += 1
                ins.then_inc(chain_d, 1)
                dve.wait_ge(chain_d, chain[0])

            def mean_root(i):
                dve.wait_ge(ss_act, squares(i + 1))
                dve.tensor_reduce(mean_sq[:, i, :], sq_sum[:, i, :, :], AX.X, ALU.add).then_inc(ms_ready, 1)
                dve.wait_ge(std_ready, i + 1)
                dve.reciprocal(rstd[:, i, :], std[:, i, :]).then_inc(rstd_ready, 1)
                dve.wait_ge(rstd_ready, i + 1)

            def rows(i, i_stat):
                j = i % NU
                if i >= 2:
                    dve.wait_ge(xn_turned, i - 1)
                dve.tensor_scalar(ysb[:, i % 2, KPU * P:2 * KPU * P], x_res[:, 1, j * KPU * P:(j + 1) * KPU * P],
                                  rstd[:, i_stat, 1:2], None, ALU.mult).then_inc(xn_ready_d, 1)

            def first_split(c, n, i_stat):
                def before(u):
                    i = n * NU + u
                    if u + 1 < NU:
                        rows(i + 1, i_stat)
                    dve.wait_ge(xn_turned, i + 1)
                    if i >= 2:
                        dve.wait_ge(act_hi_done, i - 1)
                        dve.wait_ge(act_lo_done, i - 1)
                    for cc in range(KPU):
                        k = KPU * u + cc
                        o, s = zsb[:, i % 2, cc * T:(cc + 1) * T], TURN[i % 2][:, cc * T:(cc + 1) * T]
                        if n < 2:
                            ins = dve.tensor_scalar(o, s, norm_scale[:, n, k:k + 1], None, ALU.mult)
                        else:
                            ins = dve.tensor_scalar(o, s, norm_scale[:, n, k:k + 1], norm_shift[:, n, k:k + 1],
                                                    ALU.mult, ALU.add)
                    ins.then_inc(full_ready, 1)

                def after(u):
                    low(n * NU + u, u)
                    if n == 0 and u == 1:
                        dve.wait_ge(ws_split_hi, 1)
                        dve.tensor_tensor(ws[:, :, 1, :], w_small[:, :, :], ws[:, :, 0, :].bitcast(F32),
                                          ALU.subtract).then_inc(ws_split, 1)

                if n > 0:
                    rows(n * NU, i_stat)
                split(c, None, before, after)

            def low(i, j):
                dve.wait_ge(full_ready, i + 1)
                dve.wait_ge(act_hi_done, i + 1)
                dve.tensor_tensor(act_lo[:, KPU * j:KPU * j + KPU, :].rearrange("p k t -> p (k t)"), zsb[:, i % 2, :],
                                  act_hi[:, KPU * j:KPU * j + KPU, :].bitcast(F32).rearrange("p k t -> p (k t)"),
                                  ALU.subtract).then_inc(act_lo_done, 1)

            def pre(prev, C, r):
                if prev is None:
                    return
                A_, free = acc(C - 1), acc_free[(C - 1) % 2]
                kind = prev[0]
                if kind == "up":
                    q = prev[1]
                    dve.wait_ge(sig_ready, at(2 * q + 2, r, 2))
                    if q >= 1:
                        dve.wait_ge(h_turned, at(2 * q, r, 2))
                    for t in range(TT):
                        dve.tensor_tensor(zsb[:, t, :], A_[t][:, :], ysb[:, t, :], ALU.mult).then_inc(h_ready, 1)
                    return
                if kind == "add":
                    _, dst, n, how, i = prev
                    d = x_res if dst == "x" else y_acc
                    cols_n = slice(n * CW, (n + 1) * CW)
                    for t in range(TT):
                        o = d[:, t, cols_n]
                        if how == "gated_copy":
                            dve.wait_ge(ss_act, squares(i) + TT * n + t + 1)
                            ins = dve.tensor_tensor(o, A_[t][:, :], gate_row1[:, cols_n], ALU.mult)
                        elif how == "copy":
                            ins = dve.tensor_copy(o, A_[t][:, :])
                        else:
                            ins = dve.tensor_tensor(o, A_[t][:, :], o, ALU.add)
                        if t == TT - 1:
                            ins.then_inc(free, 1)
                    if how == "gated_sum":
                        for t in range(TT):
                            dve.wait_ge(ss_act, squares(i) + TT * n + t + 1)
                            o = d[:, t, cols_n]
                            dve.tensor_tensor(o, o, gate_row2[:, cols_n], ALU.mult).then_inc(y_gated, 1)
                    return
                if kind in ("normed", "kv"):
                    k = HPC if kind == "normed" else NSA_G
                    m, i = NORMED.index(prev), TURNS.index(prev)
                    dve.wait_ge(head_std_ready, m + 1)
                    dve.reciprocal(head_rstd[:, :], head_std[:, :]).then_inc(head_sq, 1)
                    dve.wait_ge(head_sq, m + 1)
                    if i >= 1:
                        dve.wait_ge(turned, i)
                    for t in range(TT):
                        ins = dve.tensor_tensor(
                            ysb[:, t, 0:k * HD].rearrange("p (h d) -> p h d", d=HD),
                            A_[t][:, 0:k * HD].rearrange("p (h d) -> p h d", d=HD),
                            head_rstd[:, t * HPC:t * HPC + k].unsqueeze(2).to_broadcast([P, k, HD]), ALU.mult)
                        if t == TT - 1:
                            ins.then_inc(free, 1)
                elif kind == "glu":
                    i = TURNS.index(prev)
                    dve.wait_ge(turned, i)
                    for t in range(TT):
                        dve.wait_ge(glu_sig, 2 * prev[1] + t + 1)
                        dve.tensor_tensor(ysb[:, t, :], zsb[:, t, :], a_keep[:, t, :], ALU.mult).then_inc(glu_ready, 1)

            def post(prev, C, r):
                if prev is None or prev[0] in ("value", "keep_a", "add", "gate"):
                    return
                if prev[0] == "up":
                    q = prev[1]
                    k0 = at(prev[2], r, 4)
                    for t in range(TT):
                        dve.wait_ge(mid_hi_done, at(2 * q + t + 1, r, 2))
                        dve.tensor_tensor(mid_lo[:, bass.ds(k0, 4), t * P:(t + 1) * P],
                                          TURN[t][:, :].rearrange("p (k t) -> p k t", t=P),
                                          mid_hi[:, bass.ds(k0, 4), t * P:(t + 1) * P].bitcast(F32),
                                          ALU.subtract).then_inc(mid_lo_done, 1)
                    return
                dve.wait_ge(turned, TURNS.index(prev) + 1)
                keep(dve, prev, 1, lambda o, s, g: dve.tensor_scalar(o, s, g, None, ALU.mult), turn_out_d)

            conv_n, conv_at = [0], {}

            def conv_step(k, g):
                if k == 0:
                    dve.wait_ge(turn_out_a, TURNS.index(("glu", g // 4)) + 1)
                    dve.wait_ge(turn_out_d, TURNS.index(("glu", g // 4)) + 1)
                else:
                    dve.wait_ge(conv_dve, conv_at[g])
                conv_at[g] = conv_n[0] + 1
                n = CONV_CUT if g == CONV_POOL[-1] else T
                src, wk, o = uT[:, g, k:k + n], conv_w_cols[:, g, k:k + 1], convT[:, g, 0:n]
                if k == 0:
                    ins = dve.tensor_scalar(o, src, wk, cols[:, 86 + g:87 + g], ALU.mult, ALU.add)
                else:
                    ins = dve.scalar_tensor_tensor(o, src, wk, o, ALU.mult, ALU.add)
                ins.then_inc(conv_dve, 1)
                conv_n[0] += 1

            def ada_step(c, r, i):
                a = c["ada"]
                unit = a["A"] + i
                dve.wait_ge(ada_loaded[unit % 2], at(16 * (unit // 2 + 1), r, 64))
                for kk in range(KPU):
                    k = a["half"] * 8 + 2 * i + kk
                    w = ada_raw[:, unit % 2, kk, :]
                    cc = c_act[:, k:k + 1]
                    if k == 0:
                        if a["blk"] >= 1:
                            dve.wait_ge(ada_summed, at(a["blk"], r, 1))
                        dve.wait_ge(ada_bias_loaded, at(16 * (a["blk"] + 1), r, 16))
                        ins = dve.scalar_tensor_tensor(ada_acc[:, :], w, cc, ada_bias[:, :], ALU.mult, ALU.add)
                    else:
                        dve.wait_ge(ada_used, at(2 * unit + kk, r, 16))
                        ins = dve.scalar_tensor_tensor(ada_acc[:, :], w, cc, ada_acc[:, :], ALU.mult, ALU.add)
                    ins.then_inc(ada_used, 1)

            def ada_keep(a, r):
                dve.wait_ge(ada_summed, at(a["blk"] + 1, r, 1))
                if a["kind"] == "col":
                    j0 = a["dst"]
                    dve.tensor_copy(mod_cols[:, bass.ds(at(j0, r, 4), 4)], MISC[0][:, 0:4]).then_inc(ada_out, 1)
                else:
                    row = gate_row1 if a["kind"] == "row" else gate_row2
                    o = row[:, bass.ds(at(a["dst"], r, CW), CW)]
                    dve.tensor_tensor(o, MISC[0][:, :], o, ALU.mult).then_inc(ada_out, 1)

            def split(c, r, before=lambda u: None, after=lambda u: None, units=None):
                nu = c["nu"]
                conv = list(c.get("conv", []))
                for u in units or range(nu):
                    before(u)
                    R, U = c["R"] + u, c["U"] + u
                    dve.wait_ge(hi_done, at(U + 1, r, 2 * nu))
                    if U >= SPLIT_SLOTS:
                        dve.wait_ge(parts_used, at(U - SPLIT_SLOTS + 1, r, 2 * nu))
                    dve.tensor_tensor(w_lo[:, U % SPLIT_SLOTS].rearrange("p k n -> p (k n)"),
                                      raw[:, R % RAW_SLOTS].rearrange("p k n -> p (k n)"),
                                      w_hi[:, U % SPLIT_SLOTS].bitcast(F32).rearrange("p k n -> p (k n)"),
                                      ALU.subtract).then_inc(lo_done, 1)
                    after(u)
                    for _ in range(-(-len(conv) // (nu - u))):
                        conv_step(*conv.pop(0))
                    ada_at = ADA_LATE if c in (S_OUT1[0], S_OUT2[0]) else ADA_AT
                    if c["ada"] and u in ada_at:
                        ada_step(c, r, ada_at.index(u))
                    if u == 2 and c is S_OUT1[2]:
                        dve.wait_ge(gate_loaded, 16)
                    if u == 2 and c["keep"]:
                        ada_keep(c["keep"], r)
                    if c is S_IN1[SMALL_OUT + 1] and u == 3:
                        dve.wait_ge(small_mm, 2)
                        dve.tensor_copy(small[:, :, :].rearrange("p t n -> p (t n)"),
                                        MISC[0][:, 0:TT * N_SMALL]).then_inc(small_out, 1)
                    if u == 3:
                        pre(c["prev"], c["C"], r)
                    if c is S_IN1[SMALL_OUT] and u == 3:
                        dve.wait_ge(small_mm, 1)
                        dve.tensor_copy(ysb[0:2 * N_SMALL, 0, 0:T], MISC[0][0:2 * N_SMALL, 0:T]).then_inc(
                            small_folded, 1)
                    if c is S_IN1[SMALL_OUT + 1] and u == 3:
                        dve.wait_ge(small_out, 1)
                        link(dve.tensor_tensor(lf[:, 0], small[:, :, 0:FOX_H],
                                               forget_bias[:, :].unsqueeze(1).to_broadcast([P, TT, FOX_H]), ALU.add))
                        dve.scalar_tensor_tensor(lf[:, 1], lf[:, 0], -1.0, lf[:, 0], ALU.mult, ALU.max).then_inc(lf_d, 1)
                        link(dve.tensor_scalar(lf[:, 4], lf[:, 0], 0.0, None, ALU.min))
                    if c is S_IN1[SMALL_OUT + 2] and u == 1:
                        dve.wait_ge(lf_a, 1)
                        dve.tensor_tensor(lf[:, 5], lf[:, 4], lf[:, 3], ALU.subtract).then_inc(lf_d, 1)
                        dve.wait_ge(gate_exp, 1)
                        link(dve.tensor_scalar(gate_e[:, :, :], gate_e[:, :, :], 1.0, None, ALU.add))
                        dve.reciprocal(gates[:, :, :], gate_e[:, :, :]).then_inc(gates_ready, 1)
                        dve.tensor_scalar(minus_eye[:, :], ident[0:FOX_H, 0:FOX_H], -1.0, None, ALU.mult)
                    if c is S_IN1[SMALL_OUT + 2] and u == 6:
                        dve.wait_ge(lf_cum, 1)
                        dve.tensor_copy(decay[:, :], MISC[0][0:FOX_H, 0:T]).then_inc(decay_ready, 1)
                if u < nu - 1:
                    return
                if c["ada"] and nu < 7:
                    ada_step(c, r, 3)
                post(c["prev"], c["C"], r)

            def early_split(c, i, j1):
                if j1 - 2 <= i < j1 - 2 + EARLY:
                    split(c, None, units=[i - (j1 - 2)])

            def attend(j0, j1, cost, prob, row_min, row_sum, row_inv, hook=lambda i: None):
                for i in range(j0, j1 + 4):
                    if i < j1:
                        b = JOBS[i]
                        tab = {"mask": lambda: mask[:, :], "mask2": lambda: mask2[:, :],
                               "alibi": lambda: alibi[:, b["h"], :]}[b["table"]]()
                        dve.wait_ge(scored, i + 1)
                        if i - j0 >= 2:
                            dve.wait_ge(exped, 2 * (i - 1))
                        for t, c0, n in ((0, 0, P), (1, P, T)):
                            dve.tensor_tensor_reduce(cost[:, i % 2, c0:c0 + n], bank[i % 2][:, c0:c0 + n],
                                                     tab[:, T - n:T], 1.0, 3.0e38, ALU.add, ALU.min,
                                                     row_min[:, i % 2, t:t + 1]).then_inc(reduced, 1)
                    if j0 < i <= j1:
                        j = i - 1
                        b = JOBS[j]
                        dve.wait_ge(exped, 2 * j + 2)
                        link(dve.reciprocal(row_inv[:, j % 2, :], row_sum[:, j % 2, :]))
                        if b["gate"] is not None:
                            link(dve.tensor_tensor(row_inv[:, j % 2, :], row_inv[:, j % 2, :],
                                                   gates[:, :, b["gate"]], ALU.mult))
                        for t, c0, n in ((0, 0, P), (1, P, T)):
                            dve.tensor_scalar(prob[:, j % 2, c0:c0 + n], prob[:, j % 2, c0:c0 + n],
                                              row_inv[:, j % 2, t:t + 1], None, ALU.mult).then_inc(scaled, 1)
                    if i >= j0 + 4 and JOBS[i - 4]["last"]:
                        b = JOBS[i - 4]
                        dve.wait_ge(o_hi, b["o"] + 1)
                        dve.tensor_tensor(mid_lo[:, b["chunk"], :], bank[4 + b["o"] % 2][:, 0:T],
                                          mid_hi[:, b["chunk"], :].bitcast(F32), ALU.subtract).then_inc(o_lo, 1)
                    hook(i)

            def gated_add(i_stat, base):
                for t in range(TT):
                    for q in range(D // CW):
                        cols_q = slice(q * CW, (q + 1) * CW)
                        dve.scalar_tensor_tensor(x_res[:, t, cols_q], y_acc[:, t, cols_q], rstd[:, i_stat, t:t + 1],
                                                 x_res[:, t, cols_q], ALU.mult, ALU.add).then_inc(x_updated, 1)
                dve.wait_ge(x_updated, base + TT * (D // CW))

            dve.wait_ge(x_loaded[1], 16)
            for q in range(D // CW):
                x_q = x_res[:, 1, q * CW:(q + 1) * CW]
                link(dve.tensor_tensor_reduce(zsb[:, 1, :], x_q, x_q, 1.0, 0.0, ALU.mult, ALU.add,
                                              sq_sum[:, 0, 1, q:q + 1]))
            mean_root(0)
            rows(0, 0)
            dve.wait_ge(cols_turned, 1)
            dve.tensor_copy(cols[:, 0:110], MISC[0][:, 0:110]).then_inc(cols_ready, 1)
            dve.tensor_copy(pos_cols[:, :], MISC[0][:, 128:192])
            dve.tensor_copy(conv_w_cols[:, :, 0:CONV_K],
                            MISC[1][:, 0:32 * CONV_G].rearrange("p (g k) -> p g k", k=32)[:, :, 0:CONV_K]).then_inc(
                cols_ready, 1)
            dve.wait_ge(cols_ready, 2)
            dve.tensor_scalar(q_gain[:, 0:1], cols[:, 80:81], -SCALE, None, ALU.mult)
            dve.tensor_scalar(q_gain[:, 1:2], cols[:, 82:83], -SCALE, None, ALU.mult)
            link(dve.tensor_copy(norm_scale[:, 0:2, :].rearrange("p n k -> p (n k)"), cols[:, 0:2 * KD]))
            dve.wait_ge(tables_made, 1)
            first_split(S_IN1[0], 0, 0)
            run(S_IN1[1:], dve, split)
            dve.wait_ge(parts_used, U_CMP)
            dve.wait_ge(gates_ready, 1)

            def compressed(i):
                if i in (-2, -1):
                    kind, blk, src = ((0, blk_k, "kc"), (1, blk_v, "vc"))[i + 2]
                    for g in range(NSA_G):
                        for j in range(2):
                            tok = heads[src][:, g, CMP_STRIDE * j:CMP_STRIDE * (j + N_CMP)].rearrange(
                                "p (n l) -> p l n", l=CMP_STRIDE)
                            pc = pos_cols[:, kind * CMP_BLOCK + 16 * j:kind * CMP_BLOCK + 16 * j + 16]
                            ins = dve.tensor_tensor(blk[:, 16 * j:16 * j + 16, 32 * g:32 * g + N_CMP], tok,
                                                    pc.unsqueeze(2).to_broadcast([P, 16, N_CMP]), ALU.add)
                    ins.then_inc(blk_ready, 1)
                early_split(S_OUT1[0], i, N_JOB1)
                if i == 0:
                    dve.wait_ge(kc_std, 1)
                    link(dve.reciprocal(kc_ss[:, 2:3], kc_ss[:, 1:2]))
                    dve.tensor_scalar(kcn[:, :], MISC[0][0:64, 0:HD], kc_ss[:, 2:3], None, ALU.mult).then_inc(kc_n, 1)
                if i == 2:
                    dve.wait_ge(cmp_used, 8)
                    dve.wait_ge(tables_made, 2)
                    for q in range(4):
                        for g in range(NSA_G):
                            ins = dve.tensor_copy(vcmp[32 * q:32 * q + 16, g, :], MISC[1][32 * g:32 * g + 16, 0:HD])
                    ins.then_inc(vc_ready, 1)
                    dve.wait_ge(kc_turned, 1)
                    dve.tensor_scalar(kcmpT[:, :], MISC[0][:, T:T + 64], cols[:, 83:84], None, ALU.mult).then_inc(
                        kc_ready, 1)
                if i == 4:
                    dve.wait_ge(cmp_scored, 1)
                    link(dve.tensor_tensor(cmp_cost[:, :, :].rearrange("p h n -> p (h n)"), MISC[1][:, :],
                                           cmp_tab[:, :, :, :].rearrange("p t h n -> p (t h n)"), ALU.add))
                    link(dve.tensor_reduce(cmp_min[:, :], cmp_cost[:, :, :], AX.X, ALU.min))
                    dve.tensor_tensor(cmp_cost[:, :, :], cmp_cost[:, :, :],
                                      cmp_min[:, :].unsqueeze(2).to_broadcast([P, TT * NSA_H, 32]),
                                      ALU.subtract).then_inc(cmp_shift, 1)
                if i == 6:
                    dve.wait_ge(cmp_exp, 1)
                    probs4 = cmp_prob[:, :, :].rearrange("p (t h) n -> p t h n", t=TT)
                    link(dve.tensor_tensor(probs4, probs4,
                                           cmp_ok[:, :, :].unsqueeze(2).to_broadcast([P, TT, NSA_H, 32]), ALU.mult))
                    link(dve.tensor_reduce(cmp_sum[:, :], cmp_prob[:, :, :], AX.X, ALU.add))
                    link(dve.tensor_scalar(cmp_sum[:, :], cmp_sum[:, :], 1e-30, None, ALU.max))
                    link(dve.reciprocal(cmp_min[:, :], cmp_sum[:, :]))
                    link(dve.tensor_tensor(cmp_min[:, :].rearrange("p (t h) -> p t h", t=TT),
                                           cmp_min[:, :].rearrange("p (t h) -> p t h", t=TT),
                                           gates[:, :, :].rearrange("p t (h b) -> p t h b", b=3)[:, :, :, 0], ALU.mult))
                    dve.tensor_tensor(cmp_prob[:, :, :], cmp_prob[:, :, :],
                                      cmp_min[:, :].unsqueeze(2).to_broadcast([P, TT * NSA_H, 32]),
                                      ALU.mult).then_inc(cmp_p, 1)

            compressed(-2)
            compressed(-1)
            attend(0, N_JOB1, cost1, prob1, row_min1, row_sum1, row_inv1, compressed)
            dve.wait_ge(c_ready, 1)
            split(S_OUT1[0], None, units=range(EARLY, NU))
            run(S_OUT1[1:], dve, split)

            def last_add(prev, C, U, kept=None):
                dve.wait_ge(parts_used, U)
                if kept:
                    ada_keep(kept, None)
                    dve.wait_ge(ada_out, kept["blk"] + 1)
                pre(prev, C, None)
                wait_read(dve, C - 1)

            last_add(LAST_OUT1, LAST_C["out1"], S_OUT1[-1]["U"] + NU, KEEP_OUT1)
            mean_root(1)
            first_split(S_FFN1[0], 1, 1)
            run(S_FFN1[1:], dve, split)
            last_add(LAST_FFN1, LAST_C["ffn1"], S_FFN1[-1]["U"] + S_FFN1[-1]["nu"], KEEP_FFN1)
            mean_root(2)
            dve.wait_ge(ada_out, KEEP_FFN1["blk"] + 1)
            for i in range(2):
                sh, sc = 2 * i * KD, (2 * i + 1) * KD
                dve.tensor_copy(norm_shift[:, 2 + i, :], mod_cols[:, sh:sh + KD])
                link(dve.scalar_tensor_tensor(norm_scale[:, 2 + i, :], mod_cols[:, sc:sc + KD], 1.0,
                                              cols[:, (2 + i) * KD:(3 + i) * KD], ALU.add, ALU.mult))
            dve.wait_ge(uT_zero, 1)
            first_split(S_IN2[0], 2, 2)
            run(S_IN2[1:], dve, split)
            dve.wait_ge(parts_used, LAST_U["in2"])
            pre(LAST2, LAST_C["in2"], None)
            post(LAST2, LAST_C["in2"], None)

            def layer_norm(i):
                if i == N_JOB1 + 3:
                    dve.wait_ge(ln_sum, 1)
                    link(dve.tensor_scalar(conv_mu[:, :], MISC[0][:, 0:T], 1.0 / CONV_CH, None, ALU.mult))
                    dve.tensor_tensor(convT[:, :, :], convT[:, :, :],
                                      conv_mu[:, :].unsqueeze(1).to_broadcast([P, CONV_G, T]),
                                      ALU.subtract).then_inc(ln_d, 1)
                early_split(S_OUT2[0], i, len(JOBS))
                if i == len(JOBS) + 1:
                    dve.wait_ge(ln_std, 1)
                    dve.reciprocal(conv_rs[:, :], conv_rs[:, :]).then_inc(ln_d, 1)
                if i == len(JOBS) + 3:
                    dve.wait_ge(ln_d, 2)
                    for half in range(2):
                        part = convT[:, half * CONV_G // 2:(half + 1) * CONV_G // 2, :]
                        dve.tensor_tensor(part, part, conv_rs[:, :].unsqueeze(1).to_broadcast([P, CONV_G // 2, T]),
                                          ALU.mult).then_inc(ln_y, 1)

            def conv_lo(u):
                if u in (EARLY + 1, EARLY + 3):
                    half = (u - EARLY) // 2
                    k0, k1 = half * CONV_G // 2, (half + 1) * CONV_G // 2
                    dve.wait_ge(ln_hi, half + 1)
                    dve.tensor_tensor(mid_lo[:, CONV_G + k0:CONV_G + k1, :], convT[:, k0:k1, :],
                                      mid_hi[:, CONV_G + k0:CONV_G + k1, :].bitcast(F32), ALU.subtract).then_inc(
                        ln_lo, 1)

            attend(N_JOB1, len(JOBS), cost2, prob2, row_min2, row_sum2, row_inv2, layer_norm)
            split(S_OUT2[0], None, before=conv_lo, units=range(EARLY, NU))
            run(S_OUT2[1:], dve, split)
            last_add(LAST_OUT2, LAST_C["out2"], LAST_U["out2"], KEEP_OUT2)
            mean_root(3)
            gated_add(3, 0)
            mean_root(4)
            dve.wait_ge(gate_loaded, 32)
            first_split(S_FFN2[0], 3, 4)
            run(S_FFN2[1:], dve, split)
            last_add(LAST_FFN2, LAST_C["ffn2"], S_FFN2[-1]["U"] + S_FFN2[-1]["nu"])
            mean_root(5)
            dve.wait_ge(y_gated, TT * (D // CW))
            gated_add(5, TT * (D // CW))


INPUTS = ["x", "attn_norm", "w_in", "fox_forget_bias", "fox_q_norm", "fox_k_norm", "nsa_q_norm", "cmp_k_norm",
          "slc_k_norm", "win_k_norm", "cmp_pos_k", "cmp_pos_v", "cmp_w_k", "cmp_w_v", "w_out", "ffn_norm",
          "w_gate", "w_up", "w_down", "c_2", "ada_w_2", "ada_b_2", "mix_pre_g_2", "mix_post_g_2", "w_in_2",
          "conv_w_2", "conv_b_2", "conv_ln_g_2", "conv_ln_b_2", "w_out_2", "ffn_pre_g_2", "ffn_post_g_2",
          "w_gate_2", "w_up_2", "w_down_2"]


def kernel(**inputs):
    import numpy as np
    import concourse.bacc as bacc
    from concourse import mybir
    from concourse.bass_utils import run_bass_kernel_spmd

    nc = bacc.Bacc("TRN2", target_bir_lowering=False, num_devices=1)
    arrays, io = {}, {}
    for name in INPUTS:
        a = np.ascontiguousarray(inputs[name])
        arrays[f"in_{name}"] = a
        io[name] = nc.dram_tensor(f"in_{name}", a.shape, mybir.dt.from_np(a.dtype), kind="ExternalInput").ap()
    shape = inputs["x"].shape
    out = nc.dram_tensor("out_x", shape, mybir.dt.float32, kind="ExternalOutput").ap()
    build_two_blocks(nc, io, out)
    r = run_bass_kernel_spmd(nc, [arrays], core_ids=[0])
    return r.results[0]["out_x"]
```
